# Optimizing a Trainium2 kernel written in Bass

```python
import jax, jax.numpy as jnp
from jax import lax
import numpy as np
import math
import jax
import jax.numpy as jnp

D_MODEL = 1024
BATCH = 1
SEQ = 256
DEPTH = 2

A_HEADS = 4
A_KEY_DIM = 128
A_VAL_DIM = 128
A_KEY_WIDTH = A_HEADS * A_KEY_DIM
A_WIDTH = A_HEADS * A_VAL_DIM
HGRN_CHUNK = 64
B_WIDTH = D_MODEL - A_WIDTH
B_BLOCKS = 8
B_BLOCK_DIM = B_WIDTH // B_BLOCKS
B_CONV = 4
RG_C = 8.0
C_HEADS = 16
C_HEAD_DIM = D_MODEL // C_HEADS
Q_BLOCK = 128
D_FF = 2816
FFN_CONV = 3
EPS = 1e-6

N_EVEN = (DEPTH + 1) // 2
N_ODD = DEPTH // 2
EVEN_SIZES = (A_KEY_WIDTH, A_KEY_WIDTH, A_WIDTH, A_WIDTH, B_WIDTH, B_WIDTH)
EVEN_IN = sum(EVEN_SIZES)
ODD_SIZES = (D_MODEL, D_MODEL, D_MODEL, C_HEADS)
ODD_IN = sum(ODD_SIZES)


def rms_norm(x, gain):
    xf = x.astype(jnp.float32)
    y = xf * lax.rsqrt(jnp.mean(xf * xf, axis=-1, keepdims=True) + EPS)
    return (y * gain.astype(jnp.float32)).astype(x.dtype)

def split_cols(t, sizes):
    return jnp.split(t, list(np.cumsum(sizes)[:-1]), axis=-1)

def causal_dwconv(x, w, b):
    K, C = w.shape
    y = lax.conv_general_dilated(x, w[:, None, :].astype(x.dtype), window_strides=(1,),
                                 padding=[(K - 1, 0)], dimension_numbers=('NWC', 'WIO', 'NWC'),
                                 feature_group_count=C)
    return y + b.astype(x.dtype)

def hgrn2_mix(q, f_logit, v, g, lb, norm_gain):
    Bsz, T, _ = q.shape
    N = T // HGRN_CHUNK

    def heads(t, d):
        return t.reshape(Bsz, N, HGRN_CHUNK, A_HEADS, d).transpose(0, 3, 1, 2, 4)

    forget = lb + (1.0 - lb) * jax.nn.sigmoid(f_logit.astype(jnp.float32))
    qh = heads(jax.nn.silu(q.astype(jnp.float32)), A_KEY_DIM)
    kh = heads(1.0 - forget, A_KEY_DIM)
    bcum = jnp.cumsum(heads(jnp.log(forget), A_KEY_DIM), axis=3)
    vh = heads(v.astype(jnp.float32), A_VAL_DIM)
    b_last = bcum[:, :, :, -1:]
    q_dec = qh * jnp.exp(bcum)
    scores = jnp.einsum('bhnck,bhnsk->bhncs', q_dec, kh * jnp.exp(-bcum))
    causal = jnp.tril(jnp.ones((HGRN_CHUNK, HGRN_CHUNK), dtype=bool))
    scores = jnp.where(causal, scores, 0.0)
    o_intra = jnp.einsum('bhncs,bhnsv->bhncv', scores, vh)
    chunk_upd = jnp.einsum('bhnck,bhncv->bhnkv', kh * jnp.exp(b_last - bcum), vh)
    chunk_dec = jnp.exp(b_last[:, :, :, 0])

    def step(S, inp):
        dec, upd = inp
        return dec[..., None] * S + upd, S

    S0 = jnp.zeros((Bsz, A_HEADS, A_KEY_DIM, A_VAL_DIM), jnp.float32)
    _, S_prev = lax.scan(step, S0, (jnp.moveaxis(chunk_dec, 2, 0), jnp.moveaxis(chunk_upd, 2, 0)))
    S_prev = jnp.moveaxis(S_prev, 0, 2)
    o = o_intra + jnp.einsum('bhnck,bhnkv->bhncv', q_dec, S_prev)
    o = o.transpose(0, 2, 3, 1, 4).reshape(Bsz, T, A_HEADS, A_VAL_DIM)
    o = o * lax.rsqrt(jnp.mean(o * o, axis=-1, keepdims=True) + EPS)
    o = o * norm_gain.astype(jnp.float32).reshape(A_HEADS, A_VAL_DIM)
    return o.reshape(Bsz, T, A_WIDTH) * jax.nn.sigmoid(g.astype(jnp.float32))

def block_diag(x, w, b):
    xb = x.reshape(x.shape[0], x.shape[1], B_BLOCKS, B_BLOCK_DIM)
    return jnp.einsum('btni,nij->btnj', xb, w.astype(jnp.float32)).reshape(x.shape) + b.astype(jnp.float32)

def rglru_mix(x_br, y_br, conv_w, conv_b, wa, ba, wx, bx, lam):
    xf = causal_dwconv(x_br, conv_w, conv_b).astype(jnp.float32)
    r = jax.nn.sigmoid(block_diag(xf, wa, ba))
    i = jax.nn.sigmoid(block_diag(xf, wx, bx))
    log_a = -RG_C * r * jax.nn.softplus(-lam.astype(jnp.float32))
    a = jnp.exp(log_a)
    u = jnp.sqrt(-jnp.expm1(2.0 * log_a)) * (i * xf)

    def combine(left, right):
        a1, b1 = left
        a2, b2 = right
        return a1 * a2, a2 * b1 + b2

    _, h = lax.associative_scan(combine, (a, u), axis=1)
    return h * jax.nn.gelu(y_br.astype(jnp.float32))

def fox_attention(q, k, v, f_logit):
    Bsz, T, _ = q.shape

    def heads(t):
        return t.astype(jnp.float32).reshape(Bsz, T, C_HEADS, C_HEAD_DIM).transpose(0, 2, 1, 3)

    qh = heads(q) * (C_HEAD_DIM ** -0.5)
    kh, vh = heads(k), heads(v)
    c = jnp.cumsum(jax.nn.log_sigmoid(f_logit.astype(jnp.float32)), axis=1).transpose(0, 2, 1)
    outs = []
    for blk in range(T // Q_BLOCK):
        s0 = blk * Q_BLOCK
        end = s0 + Q_BLOCK
        logits = jnp.einsum('bhqd,bhkd->bhqk', qh[:, :, s0:end], kh[:, :, :end])
        logits = logits + c[:, :, s0:end, None] - c[:, :, None, :end]
        mask = (s0 + jnp.arange(Q_BLOCK))[:, None] >= jnp.arange(end)[None, :]
        p = jax.nn.softmax(jnp.where(mask, logits, -jnp.inf), axis=-1)
        outs.append(jnp.einsum('bhqk,bhkd->bhqd', p, vh[:, :, :end]))
    o = jnp.concatenate(outs, axis=2)
    return o.transpose(0, 2, 1, 3).reshape(Bsz, T, D_MODEL)

def conv_ffn(x, w_up, conv_w, conv_b, w_down):
    hid = causal_dwconv(x @ w_up, conv_w, conv_b)
    gate, val = jnp.split(hid, 2, axis=-1)
    return (jax.nn.gelu(gate) * val) @ w_down

def first_inputs(seed: int = 0) -> dict:
    key = jax.random.key(seed)
    ks = jax.random.split(key, 20)
    f32 = jnp.float32
    nrm = jax.random.normal
    a0 = jax.random.uniform(ks[11], (N_EVEN, B_WIDTH), f32, 0.9 ** (1.0 / RG_C), 0.999 ** (1.0 / RG_C))
    return {
        'x': nrm(ks[0], (BATCH, SEQ, D_MODEL), f32),
        'norm_gains': 1.0 + 0.1 * nrm(ks[1], (DEPTH, 4, D_MODEL), f32),
        'even_w_in': nrm(ks[2], (N_EVEN, D_MODEL, EVEN_IN), f32) * D_MODEL ** -0.5,
        'hgrn_lb_logits': 0.1 * nrm(ks[3], (DEPTH + 1, A_KEY_WIDTH), f32),
        'hgrn_norm': 1.0 + 0.1 * nrm(ks[4], (N_EVEN, A_WIDTH), f32),
        'rg_conv_w': nrm(ks[5], (N_EVEN, B_CONV, B_WIDTH), f32) * B_CONV ** -0.5,
        'rg_conv_b': 0.01 * nrm(ks[6], (N_EVEN, B_WIDTH), f32),
        'rg_wa': nrm(ks[7], (N_EVEN, B_BLOCKS, B_BLOCK_DIM, B_BLOCK_DIM), f32) * B_BLOCK_DIM ** -0.5,
        'rg_ba': 0.01 * nrm(ks[8], (N_EVEN, B_WIDTH), f32),
        'rg_wx': nrm(ks[9], (N_EVEN, B_BLOCKS, B_BLOCK_DIM, B_BLOCK_DIM), f32) * B_BLOCK_DIM ** -0.5,
        'rg_bx': 0.01 * nrm(ks[10], (N_EVEN, B_WIDTH), f32),
        'rg_lambda': jnp.log(a0) - jnp.log1p(-a0),
        'even_w_out': nrm(ks[12], (N_EVEN, A_WIDTH + B_WIDTH, D_MODEL), f32) * (A_WIDTH + B_WIDTH) ** -0.5,
        'odd_w_in': nrm(ks[13], (N_ODD, D_MODEL, ODD_IN), f32) * D_MODEL ** -0.5,
        'fox_f_bias': jax.random.uniform(ks[14], (N_ODD, C_HEADS), f32, 1.0, 5.0),
        'odd_w_out': nrm(ks[15], (N_ODD, D_MODEL, D_MODEL), f32) * D_MODEL ** -0.5,
        'ffn_w_up': nrm(ks[16], (DEPTH, D_MODEL, 2 * D_FF), f32) * D_MODEL ** -0.5,
        'ffn_conv_w': nrm(ks[17], (DEPTH, FFN_CONV, 2 * D_FF), f32) * FFN_CONV ** -0.5,
        'ffn_conv_b': 0.01 * nrm(ks[18], (DEPTH, 2 * D_FF), f32),
        'ffn_w_down': nrm(ks[19], (DEPTH, D_FF, D_MODEL), f32) * D_FF ** -0.5,
    }

def first_block(x, norm_gains, even_w_in, hgrn_lb_logits, hgrn_norm, rg_conv_w, rg_conv_b, rg_wa, rg_ba,
              rg_wx, rg_bx, rg_lambda, even_w_out, odd_w_in, fox_f_bias, odd_w_out,
              ffn_w_up, ffn_conv_w, ffn_conv_b, ffn_w_down):
    lb_all = jnp.cumsum(jax.nn.softmax(hgrn_lb_logits.astype(jnp.float32), axis=0), axis=0)
    for l in range(DEPTH):
        g = norm_gains[l]
        h = rms_norm(x, g[0])
        if l % 2 == 0:
            e = l // 2
            qa, fa, ia, ga, xb, yb = split_cols(h @ even_w_in[e], EVEN_SIZES)
            oa = hgrn2_mix(qa, fa, ia, ga, lb_all[l], hgrn_norm[e])
            ob = rglru_mix(xb, yb, rg_conv_w[e], rg_conv_b[e], rg_wa[e], rg_ba[e], rg_wx[e], rg_bx[e], rg_lambda[e])
            mix = jnp.concatenate([oa, ob], axis=-1).astype(h.dtype) @ even_w_out[e]
        else:
            o = l // 2
            qc, kc, vc, fc = split_cols(h @ odd_w_in[o], ODD_SIZES)
            mix = fox_attention(qc, kc, vc, fc + fox_f_bias[o]).astype(h.dtype) @ odd_w_out[o]
        x = x + rms_norm(mix, g[1])
        h = rms_norm(x, g[2])
        x = x + rms_norm(conv_ffn(h, ffn_w_up[l], ffn_conv_w[l], ffn_conv_b[l], ffn_w_down[l]), g[3])
    return x


CTX_LEN = 256
GRID_W = 64
NORM_EPS = 1e-6

HY_WIDTH = 1024
HY_SHORT = 3
HY_EMB = 33
HY_BANDS = (HY_EMB - 1) // 2
HY_HIDDEN = 64
HY_TARGET = 1e-2
HY_SHORT_DECAY_PCT = 0.3
HY_LONG_DECAY_PCT = 1.5

ATT_HEADS = 8
ATT_KV_HEADS = 2
HEAD_DIM = 128
ATT_WIDTH = ATT_HEADS * HEAD_DIM
ROPE_THETA = 10000.0

EVEN_MIX = HY_WIDTH + ATT_WIDTH
EVEN_SPLITS = (3 * HY_WIDTH, HY_WIDTH, ATT_WIDTH, ATT_KV_HEADS * HEAD_DIM, ATT_KV_HEADS * HEAD_DIM, ATT_WIDTH)
EVEN_IN_2 = sum(EVEN_SPLITS)

ML_HEADS = 8
ML_QK = 128
ML_V = 256
ML_WIDTH = ML_HEADS * ML_V
ML_CHUNK = 64
ML_SHORT = 3
ODD_SPLITS = (ML_HEADS * ML_QK, ML_HEADS * ML_QK, ML_WIDTH, ML_WIDTH, ML_WIDTH, 4 * ML_HEADS)
ODD_IN_2 = sum(ODD_SPLITS)

N_EVEN_2 = (DEPTH + 1) // 2
N_ODD_2 = DEPTH // 2


def _split(a, sizes):
    out, start = [], 0
    for s in sizes:
        out.append(a[..., start:start + s])
        start += s
    return out

def rms_norm_2(x, g):
    xf = x.astype(jnp.float32)
    y = xf * lax.rsqrt(jnp.mean(xf * xf, axis=-1, keepdims=True) + NORM_EPS)
    return (y * g.astype(jnp.float32)).astype(x.dtype)

def dw_conv(u, w, b):
    ch = u.shape[-1]
    k = w.shape[0]
    y = lax.conv_general_dilated(u, w[:, None, :].astype(u.dtype), window_strides=(1,),
                                 padding=[(k // 2, k // 2)], dimension_numbers=('NWC', 'WIO', 'NWC'),
                                 feature_group_count=ch)
    return y + b.astype(u.dtype)

def adaln(cond, w_mod, b_mod):
    m = jax.nn.silu(cond) @ w_mod + b_mod
    return _split(m, (D_MODEL, D_MODEL, D_MODEL))

def axial_rope(x, rows, cols):
    f32 = jnp.float32
    half = x.shape[-1] // 2
    nf = half // 2
    inv = ROPE_THETA ** (-jnp.arange(nf, dtype=f32) / nf)

    def rot(xa, pos):
        ang = pos.astype(f32)[:, None] * inv
        cos = jnp.cos(ang)[None, :, None, :]
        sin = jnp.sin(ang)[None, :, None, :]
        x1 = xa[..., :nf].astype(f32)
        x2 = xa[..., nf:].astype(f32)
        return jnp.concatenate([x1 * cos - x2 * sin, x1 * sin + x2 * cos], axis=-1)

    out = jnp.concatenate([rot(x[..., :half], rows), rot(x[..., half:], cols)], axis=-1)
    return out.astype(x.dtype)

def hyena_filter(n, w1, b1, freq, w2, b2, w3):
    f32 = jnp.float32
    t = jnp.linspace(0.0, 1.0, n, dtype=f32)[:, None]
    bands = jnp.linspace(1e-4, HY_BANDS - 1, HY_BANDS, dtype=f32)
    ang = (2.0 * math.pi / n) * jnp.arange(n, dtype=f32)[:, None] * bands
    z = jnp.concatenate([t, jnp.cos(ang), -jnp.sin(ang)], axis=-1)
    fr = freq.astype(f32)
    hdn = jnp.sin(fr * (z @ w1.astype(f32) + b1.astype(f32)))
    hdn = jnp.sin(fr * (hdn @ w2.astype(f32) + b2.astype(f32)))
    h = (hdn @ w3.astype(f32)).reshape(n, 2, HY_WIDTH)
    max_decay = math.log(HY_TARGET) / HY_SHORT_DECAY_PCT
    min_decay = math.log(HY_TARGET) / HY_LONG_DECAY_PCT
    deltas = jnp.linspace(min_decay, max_decay, HY_WIDTH, dtype=f32)
    h = h * jnp.exp(-t * jnp.abs(deltas))[:, None, :]
    two_sided = jnp.concatenate([h[:, 0], jnp.zeros((1, HY_WIDTH), f32), h[:0:-1, 1]], axis=0)
    return two_sided / jnp.sum(jnp.abs(two_sided), axis=0, keepdims=True)

def bidir_long_conv(u, filt):
    n = u.shape[1]
    uf = jnp.fft.rfft(u.astype(jnp.float32), n=2 * n, axis=1)
    ff = jnp.fft.rfft(filt, axis=0)
    return jnp.fft.irfft(uf * ff[None], n=2 * n, axis=1)[:, :n].astype(u.dtype)

def hyena_mixer(xv, conv_w, conv_b, f_w1, f_b1, f_freq, f_w2, f_b2, f_w3, hy_bias):
    n = xv.shape[1]
    x0, x1, v = _split(dw_conv(xv, conv_w, conv_b), (HY_WIDTH, HY_WIDTH, HY_WIDTH))
    filt = hyena_filter(n, f_w1, f_b1, f_freq, f_w2, f_b2, f_w3)
    g = v * x1
    return x0 * (bidir_long_conv(g, filt) + g * hy_bias.astype(g.dtype))

def block_attention(q, k, v):
    B, n, H, Dh = q.shape
    kvh = k.shape[2]
    grp = H // kvh
    nb = n // Q_BLOCK
    qb = jnp.moveaxis(q.reshape(B, nb, Q_BLOCK, kvh, grp, Dh), 1, 0)
    scale = Dh ** -0.5

    def attend(qblk):
        s = jnp.einsum('bqkgd,btkd->bkgqt', qblk, k, preferred_element_type=jnp.float32) * scale
        p = jax.nn.softmax(s, axis=-1).astype(v.dtype)
        return jnp.einsum('bkgqt,btkd->bqkgd', p, v)

    out = lax.map(attend, qb)
    return jnp.moveaxis(out, 0, 1).reshape(B, n, H * Dh)

def even_mixer(h_lat, h_ctx, rows, cols, need_ctx, w_in, conv_w, conv_b, f_w1, f_b1, f_freq,
               f_w2, f_b2, f_w3, hy_bias, q_norm, k_norm, w_out):
    def project(h):
        B, n = h.shape[:2]
        xv, g_hy, q, k, v, g_att = _split(h @ w_in, EVEN_SPLITS)
        q = rms_norm_2(q.reshape(B, n, ATT_HEADS, HEAD_DIM), q_norm)
        k = rms_norm_2(k.reshape(B, n, ATT_KV_HEADS, HEAD_DIM), k_norm)
        v = v.reshape(B, n, ATT_KV_HEADS, HEAD_DIM)
        return xv, g_hy, q, k, v, g_att

    def hyena(xv):
        return hyena_mixer(xv, conv_w, conv_b, f_w1, f_b1, f_freq, f_w2, f_b2, f_w3, hy_bias)

    def combine(hy, att, g_hy, g_att):
        return jnp.concatenate([hy * jax.nn.silu(g_hy), att * jax.nn.silu(g_att)], axis=-1) @ w_out

    xv_l, gh_l, q_l, k_l, v_l, ga_l = project(h_lat)
    xv_c, gh_c, q_c, k_c, v_c, ga_c = project(h_ctx)
    q_l = axial_rope(q_l, rows, cols)
    k_l = axial_rope(k_l, rows, cols)
    att_l = block_attention(q_l, jnp.concatenate([k_l, k_c], axis=1), jnp.concatenate([v_l, v_c], axis=1))
    y_lat = combine(hyena(xv_l), att_l, gh_l, ga_l)
    y_ctx = None
    if need_ctx:
        y_ctx = combine(hyena(xv_c), block_attention(q_c, k_c, v_c), gh_c, ga_c)
    return y_lat, y_ctx

def mlstm_chunkwise(q, k, v, i_pre, f_pre, state):
    f32 = jnp.float32
    B, H, n, _ = q.shape
    nc = n // ML_CHUNK

    def chunks(a):
        a = a.astype(f32)
        return jnp.moveaxis(a.reshape(B, H, nc, ML_CHUNK, *a.shape[3:]), 2, 0)

    lower = jnp.tril(jnp.ones((ML_CHUNK, ML_CHUNK), dtype=bool))

    def step(carry, inp):
        C, nvec, m = carry
        qc, kc, vc, ic, lfc = inp
        b = jnp.cumsum(lfc, axis=-1)
        d = jnp.where(lower, b[..., :, None] - b[..., None, :] + ic[..., None, :], -jnp.inf)
        inter = b + m[..., None]
        m_row = jnp.maximum(inter, jnp.max(d, axis=-1))
        s = jnp.einsum('bhtd,bhsd->bhts', qc, kc) * jnp.exp(d - m_row[..., None])
        w_prev = jnp.exp(inter - m_row)
        num = jnp.einsum('bhts,bhsv->bhtv', s, vc) + w_prev[..., None] * jnp.einsum('bhvd,bhtd->bhtv', C, qc)
        den = jnp.sum(s, axis=-1) + w_prev * jnp.einsum('bhd,bhtd->bht', nvec, qc)
        h = num / jnp.maximum(jnp.abs(den), jnp.exp(-m_row))[..., None]
        b_end = b[..., -1]
        g = b_end[..., None] - b + ic
        m_new = jnp.maximum(b_end + m, jnp.max(g, axis=-1))
        a = jnp.exp(g - m_new[..., None])
        a_prev = jnp.exp(b_end + m - m_new)
        C = a_prev[..., None, None] * C + jnp.einsum('bhsv,bhsd->bhvd', vc * a[..., None], kc)
        nvec = a_prev[..., None] * nvec + jnp.einsum('bhs,bhsd->bhd', a, kc)
        return (C, nvec, m_new), h

    xs = (chunks(q), chunks(k), chunks(v), chunks(i_pre), chunks(jax.nn.log_sigmoid(f_pre.astype(f32))))
    state, hs = lax.scan(step, state, xs)
    return state, jnp.moveaxis(hs, 0, 2).reshape(B, H, n, v.shape[-1])

def odd_mixer(h_lat, h_ctx, need_ctx, w_in, conv_w, conv_b, gate_b, head_norm, w_out):
    f32 = jnp.float32

    def project(h):
        B, n = h.shape[:2]
        q, k, v, o, z, gates = _split(h @ w_in, ODD_SPLITS)
        qk = jax.nn.silu(dw_conv(jnp.concatenate([q, k], axis=-1), conv_w, conv_b))
        q, k = _split(qk, (ML_HEADS * ML_QK, ML_HEADS * ML_QK))
        q = q.reshape(B, n, ML_HEADS, ML_QK).transpose(0, 2, 1, 3)
        k = k.reshape(B, n, ML_HEADS, ML_QK).transpose(0, 2, 1, 3) * (ML_QK ** -0.5)
        v = v.reshape(B, n, ML_HEADS, ML_V).transpose(0, 2, 1, 3)
        gates = (gates + gate_b).astype(f32).reshape(B, n, 4, ML_HEADS).transpose(2, 0, 3, 1)
        return q, k, v, o, z, gates

    def flip(a):
        return jnp.flip(a, axis=2)

    ql, kl, vl, ol, zl, gl = project(h_lat)
    qc, kc, vc, oc, zc, gc = project(h_ctx)
    B = h_lat.shape[0]
    zero = (jnp.zeros((B, ML_HEADS, ML_V, ML_QK), f32), jnp.zeros((B, ML_HEADS, ML_QK), f32),
            jnp.zeros((B, ML_HEADS), f32))
    st_f, hc_f = mlstm_chunkwise(qc, kc, vc, gc[0], gc[1], zero)
    _, hl_f = mlstm_chunkwise(ql, kl, vl, gl[0], gl[1], st_f)
    st_b, hc_b = mlstm_chunkwise(flip(qc), flip(kc), flip(vc), flip(gc[2]), flip(gc[3]), zero)
    _, hl_b = mlstm_chunkwise(flip(ql), flip(kl), flip(vl), flip(gl[2]), flip(gl[3]), st_b)

    def finish(h_f, h_b, o, z):
        Bn, _, n, _ = h_f.shape
        h = (h_f + h_b).transpose(0, 2, 1, 3).reshape(Bn, n, ML_WIDTH).astype(o.dtype) * jax.nn.sigmoid(o)
        h = rms_norm_2(h.reshape(Bn, n, ML_HEADS, ML_V), head_norm.reshape(ML_HEADS, ML_V)).reshape(Bn, n, ML_WIDTH)
        return (h * jax.nn.silu(z)) @ w_out

    y_lat = finish(hl_f, flip(hl_b), ol, zl)
    y_ctx = finish(hc_f, flip(hc_b), oc, zc) if need_ctx else None
    return y_lat, y_ctx

def second_inputs(seed: int = 0) -> dict:
    key = jax.random.key(seed)
    keys = jax.random.split(key, 32)
    f32 = jnp.float32

    def nrm(i, shape, scale):
        return jax.random.normal(keys[i], shape, f32) * scale

    D = D_MODEL
    forget_init = jnp.linspace(3.0, 6.0, ML_HEADS, dtype=f32)
    o_gate_b = jnp.concatenate([
        nrm(24, (N_ODD_2, ML_HEADS), 0.1),
        forget_init + nrm(25, (N_ODD_2, ML_HEADS), 0.1),
        nrm(26, (N_ODD_2, ML_HEADS), 0.1),
        forget_init + nrm(27, (N_ODD_2, ML_HEADS), 0.1)], axis=-1)
    return {
        'x': nrm(0, (BATCH, SEQ, D), 1.0),
        'c': nrm(1, (BATCH, D), 1.0),
        'ctx': nrm(2, (BATCH, CTX_LEN, D), 1.0),
        'c_ctx': nrm(3, (D,), 1.0),
        'w_mod': nrm(4, (DEPTH, D, 3 * D), D ** -0.5),
        'b_mod': nrm(5, (DEPTH, 3 * D), 0.02),
        'g_pre': 1.0 + nrm(6, (DEPTH, D), 0.02),
        'g_post': 1.0 + nrm(7, (DEPTH, D), 0.02),
        'e_w_in': nrm(8, (N_EVEN_2, D, EVEN_IN_2), D ** -0.5),
        'e_conv_w': nrm(9, (N_EVEN_2, HY_SHORT, 3 * HY_WIDTH), HY_SHORT ** -0.5),
        'e_conv_b': nrm(10, (N_EVEN_2, 3 * HY_WIDTH), 0.02),
        'e_filt_w1': nrm(11, (N_EVEN_2, HY_EMB, HY_HIDDEN), HY_EMB ** -0.5),
        'e_filt_b1': nrm(12, (N_EVEN_2, HY_HIDDEN), 0.1),
        'e_filt_freq': 1.0 + nrm(13, (N_EVEN_2, HY_HIDDEN), 0.02),
        'e_filt_w2': nrm(14, (N_EVEN_2, HY_HIDDEN, HY_HIDDEN), HY_HIDDEN ** -0.5),
        'e_filt_b2': nrm(15, (N_EVEN_2, HY_HIDDEN), 0.1),
        'e_filt_w3': nrm(16, (N_EVEN_2, HY_HIDDEN, 2 * HY_WIDTH), HY_HIDDEN ** -0.5),
        'e_hy_bias': nrm(17, (N_EVEN_2, HY_WIDTH), 0.1),
        'e_q_norm': 1.0 + nrm(18, (N_EVEN_2, HEAD_DIM), 0.02),
        'e_k_norm': 1.0 + nrm(19, (N_EVEN_2, HEAD_DIM), 0.02),
        'e_w_out': nrm(20, (N_EVEN_2, EVEN_MIX, D), EVEN_MIX ** -0.5),
        'o_w_in': nrm(21, (N_ODD_2, D, ODD_IN_2), D ** -0.5),
        'o_conv_w': nrm(22, (N_ODD_2, ML_SHORT, 2 * ML_HEADS * ML_QK), ML_SHORT ** -0.5),
        'o_conv_b': nrm(23, (N_ODD_2, 2 * ML_HEADS * ML_QK), 0.02),
        'o_gate_b': o_gate_b,
        'o_head_norm': 1.0 + nrm(28, (N_ODD_2, ML_WIDTH), 0.02),
        'o_w_out': nrm(29, (N_ODD_2, ML_WIDTH, D), ML_WIDTH ** -0.5),
    }

def second_block(x, c, ctx, c_ctx, w_mod, b_mod, g_pre, g_post, e_w_in, e_conv_w, e_conv_b, e_filt_w1,
              e_filt_b1, e_filt_freq, e_filt_w2, e_filt_b2, e_filt_w3, e_hy_bias, e_q_norm, e_k_norm,
              e_w_out, o_w_in, o_conv_w, o_conv_b, o_gate_b, o_head_norm, o_w_out):
    n_lat = x.shape[1]
    ROWS = n_lat // GRID_W
    rows = jnp.repeat(jnp.arange(ROWS, dtype=jnp.int32), GRID_W)
    cols = jnp.tile(jnp.arange(GRID_W, dtype=jnp.int32), ROWS)
    x_lat, x_ctx = x, ctx
    for layer in range(DEPTH):
        need_ctx = layer < DEPTH - 1
        sh_l, sc_l, ga_l = adaln(c, w_mod[layer], b_mod[layer])
        sh_c, sc_c, ga_c = adaln(c_ctx, w_mod[layer], b_mod[layer])
        h_lat = rms_norm_2(x_lat, g_pre[layer]) * (1 + sc_l[:, None]) + sh_l[:, None]
        h_ctx = rms_norm_2(x_ctx, g_pre[layer]) * (1 + sc_c) + sh_c
        j = layer // 2
        if layer % 2 == 0:
            y_lat, y_ctx = even_mixer(h_lat, h_ctx, rows, cols, need_ctx, e_w_in[j], e_conv_w[j], e_conv_b[j],
                                      e_filt_w1[j], e_filt_b1[j], e_filt_freq[j], e_filt_w2[j], e_filt_b2[j],
                                      e_filt_w3[j], e_hy_bias[j], e_q_norm[j], e_k_norm[j], e_w_out[j])
        else:
            y_lat, y_ctx = odd_mixer(h_lat, h_ctx, need_ctx, o_w_in[j], o_conv_w[j], o_conv_b[j], o_gate_b[j],
                                     o_head_norm[j], o_w_out[j])
        x_lat = x_lat + ga_l[:, None] * rms_norm_2(y_lat, g_post[layer])
        if need_ctx:
            x_ctx = x_ctx + ga_c * rms_norm_2(y_ctx, g_post[layer])
    return x_lat


def setup_inputs(seed=0):
    out = dict(first_inputs(seed))
    for name, value in second_inputs(seed + 1).items():
        if name != "x":
            out[name + "_2"] = value
    return out


def reference(
    x, norm_gains, even_w_in, hgrn_lb_logits, hgrn_norm, rg_conv_w, rg_conv_b, rg_wa, rg_ba,
    rg_wx, rg_bx, rg_lambda, even_w_out, odd_w_in, fox_f_bias, odd_w_out, ffn_w_up, ffn_conv_w,
    ffn_conv_b, ffn_w_down, c_2, ctx_2, c_ctx_2, w_mod_2, b_mod_2, g_pre_2, g_post_2, e_w_in_2,
    e_conv_w_2, e_conv_b_2, e_filt_w1_2, e_filt_b1_2, e_filt_freq_2, e_filt_w2_2, e_filt_b2_2,
    e_filt_w3_2, e_hy_bias_2, e_q_norm_2, e_k_norm_2, e_w_out_2, o_w_in_2, o_conv_w_2,
    o_conv_b_2, o_gate_b_2, o_head_norm_2, o_w_out_2,
):
    x = first_block(
        x, norm_gains, even_w_in, hgrn_lb_logits, hgrn_norm, rg_conv_w, rg_conv_b, rg_wa, rg_ba,
        rg_wx, rg_bx, rg_lambda, even_w_out, odd_w_in, fox_f_bias, odd_w_out, ffn_w_up,
        ffn_conv_w, ffn_conv_b, ffn_w_down,
    )
    return second_block(
        x, c_2, ctx_2, c_ctx_2, w_mod_2, b_mod_2, g_pre_2, g_post_2, e_w_in_2, e_conv_w_2,
        e_conv_b_2, e_filt_w1_2, e_filt_b1_2, e_filt_freq_2, e_filt_w2_2, e_filt_b2_2,
        e_filt_w3_2, e_hy_bias_2, e_q_norm_2, e_k_norm_2, e_w_out_2, o_w_in_2, o_conv_w_2,
        o_conv_b_2, o_gate_b_2, o_head_norm_2, o_w_out_2,
    )


_drawn_inputs = setup_inputs


def setup_inputs(seed=0):
    import zlib

    import numpy as np

    out = dict(_drawn_inputs(seed))
    spreads = {}
    factors = {'hgrn_lb_logits': 8.0,
     'rg_ba': 8.0,
     'rg_bx': 8.0,
     'ffn_conv_b': 4.518,
     'b_mod_2': 2.692,
     'g_pre_2': 5.813,
     'g_post_2': 7.382,
     'e_conv_b_2': 8.0,
     'e_filt_freq_2': 8.0,
     'e_q_norm_2': 8.0,
     'e_k_norm_2': 8.0,
     'o_conv_b_2': 200.0,
     'o_head_norm_2': 139.481}
    for name, (base, spread) in spreads.items():
        noise = np.random.default_rng([zlib.crc32(name.encode()), seed]).standard_normal(out[name].shape)
        drawn = base * np.exp(spread * noise) if base else spread * noise
        out[name] = jnp.asarray(drawn.astype(out[name].dtype))
    for name, factor in factors.items():
        out[name] = (out[name] * factor).astype(out[name].dtype)
    return out
```

```python
from contextlib import ExitStack
import math

import numpy as np
import concourse.bass as bass
from concourse import mybir

F32 = mybir.dt.float32
ALU = mybir.AluOpType
ACT = mybir.ActivationFunctionType
AXX = mybir.AxisListType.X

EPS = 1e-6
RING = 5
TPC = 16
NEG = -1e30


def param_layout():
    sizes = [("ng", 64), ("lbl", 12), ("hgn", 4), ("rcw", 16), ("rcb", 4), ("rba", 4), ("rbx", 4), ("lam", 4),
             ("fxb", 1), ("fcw", 264), ("fcb", 88), ("cc", 16), ("bmod", 96), ("gpre", 16), ("gpost", 16),
             ("ecw", 72), ("ecb", 24), ("fb1", 1), ("ffr", 1), ("fb2", 1), ("hyb", 8), ("qn", 1), ("kn", 1),
             ("ocw", 48), ("ocb", 16), ("gtb", 1), ("ohn", 16)]
    at, out = 0, {}
    for name, n in sizes:
        out[name] = at
        at += n
    return out, at


def const_layout():
    sizes = [("ident", 128), ("mean", 128), ("mean128", 128), ("mean256", 128), ("ones", 256), ("perm", 128),
             ("cos", 256), ("sin", 256), ("maskd", 128), ("maskf", 512), ("maskb", 512),
             ("sel8", 1024), ("cols", 8), ("dft", 1024), ("idft", 1024), ("zT", 256)]
    at, out = 0, {}
    for name, n in sizes:
        out[name] = (at, n)
        at += n
    return out, at


def weight_plan():
    out = []

    def cm(name, kt, ms):
        for m in ms:
            out.extend((name, k, m) for k in range(kt))

    def tm(name, kt, m0, n512):
        for c in range(n512):
            for k in range(kt):
                out.extend((name, k, m0 + 4 * c + i) for i in range(4))

    cm("even_w_in", 8, range(4, 8))
    cm("even_w_in", 8, range(0, 4))
    cm("even_w_in", 8, range(12, 16))
    tm("even_w_in", 8, 8, 1)
    cm("even_w_in", 8, range(16, 24))
    cm("even_w_out", 8, range(8))
    for l in range(2):
        if l == 1:
            cm("odd_w_in", 8, [24])
            tm("odd_w_in", 8, 16, 2)
            for j in range(8):
                cm("odd_w_in", 8, [j, 8 + j])
            cm("odd_w_out", 8, range(8))
        for j in range(22):
            cm(f"ffn_up{l}", 8, [j, 22 + j])
        cm(f"ffn_down{l}", 22, range(8))
    cm("w_mod0", 8, range(24))
    cm("w_mod1", 8, range(24))
    for j in range(8):
        cm("e_w_in", 8, [8 + j, 16 + j])
    cm("e_w_in", 8, range(0, 8))
    cm("e_w_in", 8, range(40, 42))
    for t in range(1):
        for k in range(8):
            out.extend(("e_w_in", k, 42 + i) for i in range(2))
    cm("e_w_in", 8, range(32, 40))
    cm("e_w_in", 8, range(24, 32))
    cm("e_w_in", 8, range(44, 52))
    cm("e_w_out", 16, range(8))
    cm("o_w_in", 8, [64])
    tm("o_w_in", 8, 16, 4)
    for j in range(8):
        cm("o_w_in", 8, [j, 8 + j])
    for j in range(16):
        cm("o_w_in", 8, [32 + j, 48 + j])
    cm("o_w_out", 16, range(8))
    return out


class Queue:

    def __init__(self, sem):
        self.sem, self.n, self.items, self.seen = sem, 0, [], {}

    def wait(self, *toks):
        for t in flat(toks):
            if self.seen.get(id(t[0]), 0) < t[1]:
                self.seen[id(t[0])] = t[1]
                self.items.append(("w", t[0], t[1]))

    def do(self, fn, *toks):
        self.wait(*toks)
        self.n += 1
        self.items.append(("i", fn, self.sem, 1))
        return (self.sem, self.n)

    def plain(self, fn, *toks):
        self.wait(*toks)
        self.items.append(("i", fn, None, 0))

    def dma(self, fn, sem, *toks):
        self.wait(*toks)
        self.items.append(("i", fn, sem, 16))

    def emit(self, eng):
        for it in self.items:
            if it[0] == "w":
                eng.wait_ge(it[1], it[2])
            else:
                ins = it[1](eng)
                if it[2] is not None:
                    ins.then_inc(it[2], it[3])


def flat(toks):
    for t in toks:
        if t is None:
            continue
        if isinstance(t, list):
            yield from flat(t)
        else:
            yield t


class Slots:

    def __init__(self, bufs):
        self.bufs, self.free, self.i = bufs, [None] * len(bufs), 0

    def take(self):
        s = self.i % len(self.bufs)
        self.i += 1
        return s, self.bufs[s], self.free[s]

    def give(self, s, *toks):
        self.free[s] = list(toks)


def build_program(nc, xT, ctxT, ws, pr, cs, rgw, fw, dec, out, stop=None, dbg=None):
    POFF, PN = param_layout()
    COFF, CN = const_layout()
    plan = weight_plan()
    nchunk = (len(plan) + TPC - 1) // TPC
    ctx = ExitStack()
    with ctx:
        def sb(name, *shape):
            return ctx.enter_context(nc.sbuf_tensor(name, [128, *shape], F32))

        def sem(name):
            return ctx.enter_context(nc.semaphore(name))

        X = sb("X", 8, 512)
        H = sb("H", 8, 512)
        WR = sb("WR", RING, TPC * 128)
        PR = sb("PR", PN)
        CS = sb("CS", CN)
        TMP = [sb(f"TMP{i}", 512) for i in range(6)]
        RB = [sb(f"RB{i}", 512) for i in range(2)]
        SM = sb("SM", 512)
        AR = sb("AR", 20736)
        ONE8 = sb("ONE8", 512)[0:8, :]
        banks = [ctx.enter_context(nc.psum_tensor(f"PS{i}", [128, 512], F32)) for i in range(8)]

        s_pe, s_act, s_dve, s_pool = sem("s_pe"), sem("s_act"), sem("s_dve"), sem("s_pool")
        s_w = [sem(f"s_w{i}") for i in range(RING)]
        s_cs, s_pr, s_x, s_rg, s_fw, s_dec, s_out = (sem(n) for n in
                                                     ("s_cs", "s_pr", "s_x", "s_rg", "s_fw", "s_dec", "s_out"))
        pe, act, dve, pool = Queue(s_pe), Queue(s_act), Queue(s_dve), Queue(s_pool)
        extra = []
        ps = Slots([b[:, :] for b in banks])
        tmp = Slots([t[:, :] for t in TMP])
        rbs = Slots([t[:, :] for t in RB])

        def C(name, rows=128):
            a, n = COFF[name]
            return CS[0:rows, a:a + n]

        def P(name, j=0, n=1):
            a = POFF[name] + j
            return PR[:, a:a + n]

        ident = C("ident")
        CCOL = COFF["cols"][0]
        c_eps, c_even, c_odd, c_m0 = (CS[:, CCOL + i:CCOL + i + 1] for i in range(4))
        T_CS, T_PR, T_X = (s_cs, 16), (s_pr, 16), (s_x, 32)

        def view(off, *shape):
            n = 1
            for d in shape:
                n *= d
            v = AR[:, off:off + n]
            assert off + n <= 20736
            if len(shape) == 1:
                return v
            if len(shape) == 2:
                return v.rearrange("p (a b) -> p a b", a=shape[0])
            return v.rearrange("p (a b c) -> p a b c", a=shape[0], b=shape[1])

        def A(out_, in_, func, *w, bias=None, scale=1.0, accum=None):
            kw = {"scale": scale}
            if bias is not None:
                kw["bias"] = bias
            if accum is not None:
                kw["accum_out"] = accum
            return act.do(lambda e: e.activation(out_, in_, func, **kw), *w)

        def TS(out_, in_, s1, s2, o0, o1, *w, q=None):
            q = q or dve
            if o1 is None:
                return q.do(lambda e: e.tensor_scalar(out_, in_, s1, None, o0), *w)
            return q.do(lambda e: e.tensor_scalar(out_, in_, s1, s2, o0, o1), *w)

        def TT(out_, a, b, op, *w, q=None):
            return (q or dve).do(lambda e: e.tensor_tensor(out_, a, b, op), *w)

        def STT(out_, a, s, b, o0, o1, *w):
            return dve.do(lambda e: e.scalar_tensor_tensor(out=out_, in0=a, scalar=s, in1=b, op0=o0, op1=o1), *w)

        def CP(out_, in_, *w, q=None):
            return (q or dve).do(lambda e: e.tensor_copy(out_, in_), *w)

        def REC(out_, in_, *w):
            return dve.do(lambda e: e.reciprocal(out_, in_), *w)

        def SCAN(out_, a, b, init, o0, o1, *w):
            return dve.do(lambda e: e.tensor_tensor_scan(out_, a, b, init, o0, o1), *w)

        def MM(groups, *w):
            pe.wait(*w)
            n = len(groups)
            for i, (o, l, r) in enumerate(groups):
                def f(e, o=o, l=l, r=r, i=i):
                    return e.matmul(o, l, r, start=(i == 0), stop=(i == n - 1))
                if i < n - 1:
                    pe.plain(f)
                else:
                    return pe.do(f)

        def TR(o, a, rows, *w):
            return pe.do(lambda e: e.transpose(o, a, ident[0:rows, 0:rows]), *w)

        state = {"t": 0, "rel": 0}
        release = [None] * nchunk

        def weights(names, ntile, w):
            t = state["t"]
            assert plan[t][0] == names, (plan[t], names)
            c = t // TPC
            pe.wait((s_w[c % RING], 16 * (c // RING + 1)))
            state["t"] = t + ntile
            o = (t % TPC) * 128
            return WR[:, c % RING, o:o + ntile * 128]

        def weights_read(tok):
            while (state["rel"] + 1) * TPC <= state["t"]:
                release[state["rel"]] = tok
                state["rel"] += 1

        def proj(name, kt, rhs, N, w):
            s, b, fr = ps.take()
            pe.wait(fr, w)
            for k in range(kt):
                wt = weights(name, 1, None)
                def f(e, wt=wt, k=k, b=b, x=rhs(k)):
                    return e.matmul(b[:, 0:N], wt, x, start=(k == 0), stop=(k == kt - 1))
                if k < kt - 1:
                    pe.plain(f)
            tok = pe.do(f)
            weights_read(tok)
            return s, b, tok

        def proj_tok(name, kt, lhs, nb, width, w):
            got = []
            for n in range(nb):
                s, b, fr = ps.take()
                pe.wait(fr, w)
                got.append((s, b))
            toks = []
            for k in range(kt):
                wt = weights(name, width // 128, None)
                for n in range(nb):
                    def f(e, wt=wt, k=k, o=got[n][1], x=lhs(k, n)):
                        return e.matmul(o[:, 0:width], x, wt, start=(k == 0), stop=(k == kt - 1))
                    if k < kt - 1:
                        pe.plain(f)
                    else:
                        toks.append(pe.do(f))
            weights_read(toks[-1])
            return [(s, b, t) for (s, b), t in zip(got, toks)]

        def inv_rms(src, nb, lo, N, mean, toks, sq):
            s, b, fr = ps.take()
            sqt = []
            for j in range(nb):
                sqt.append(A(sq(j), src(j), ACT.Square, toks[j] if isinstance(toks, list) and len(toks) == nb else toks))
            pe.wait(fr, T_CS)
            for j in range(nb):
                f = lambda e, j=j, x=sq(j): e.matmul(b[:, 0:N], mean, x, start=(j == 0), stop=(j == nb - 1))
                if j < nb - 1:
                    pe.plain(f, sqt[j])
                else:
                    t = pe.do(f, sqt[j])
            rs, r, rfr = rbs.take()
            t1 = A(r[:, 0:N], b[:, 0:N], ACT.Sqrt, t, rfr, bias=c_eps)
            ps.give(s, t1)
            t2 = REC(r[:, 0:N], r[:, 0:N], t1)
            return rs, r[:, 0:N], t2, t

        def log1p_exp_neg_abs(dst, x, a, b, tok):
            t = A(a, x, ACT.Abs, tok)
            t = A(a, a, ACT.Exp, t, scale=-1.0)
            t = TS(b, a, 2.0, None, ALU.add, None, t)
            t = REC(b, b, t)
            t = TT(a, a, b, ALU.mult, t)
            t = TT(b, a, a, ALU.mult, t)
            t = TS(dst, b, 1.0 / 19, None, ALU.mult, None, t)
            for n in (17, 15, 13, 11, 9, 7, 5, 3):
                t = STT(dst, dst, 1.0 / n, b, ALU.add, ALU.mult, t)
            t = STT(dst, dst, 1.0, a, ALU.add, ALU.mult, t)
            return TS(dst, dst, 2.0, None, ALU.mult, None, t)

        def log_sigmoid(dst, x, a, b, tok):
            t = log1p_exp_neg_abs(dst, x, a, b, tok)
            return STT(dst, x, 0.0, dst, ALU.min, ALU.subtract, t)

        def load(dst, src, sm, *toks):
            at = state["t"] // TPC + RING - 1 if state["t"] else 0
            extra.append((at, dst, src, sm, toks))

        def done(name, ap, *toks):
            if stop == name:
                load(dbg, ap, s_out, *toks)
                return True
            return False

        load(X[:, :, 0:256], xT, s_x)
        load(CS[:, :], cs, s_cs)
        load(PR[:, :], pr, s_pr)
        load(X[:, :, 256:512], ctxT, s_x)

        def conv_causal(b, tok, s, dst, K, taps, bias, *w):
            t = A(dst, b[:, 0:256], ACT.Identity, tok, *w, bias=bias, scale=taps(K - 1))
            for d in range(1, K):
                t = STT(dst[:, d:256], b[:, 0:256 - d], taps(K - 1 - d), dst[:, d:256], ALU.mult, ALU.add, t)
            ps.give(s, t)
            return t

        xt = [T_X] * 8

        def pre_norm(l, g, hfree):
            rs, r, t, _ = inv_rms(lambda j: X[:, j, 0:256], 8, 0, 256, C("mean"),
                                  [[xt[j], hfree] for j in range(8)], lambda j: H[:, j, 0:256])
            ht = [STT(H[:, j, 0:256], X[:, j, 0:256], P("ng", (l * 4 + g) * 8 + j), r, ALU.mult, ALU.mult,
                      t, xt[j], T_PR) for j in range(8)]
            rbs.give(rs, ht[-1])
            return ht

        def post_norm(l, g, MIX, mt, hfree):
            rs, r, t, _ = inv_rms(lambda j: MIX[:, j, :], 8, 0, 256, C("mean"),
                                  [[mt[j], hfree] for j in range(8)], lambda j: H[:, j, 0:256])
            for j in range(8):
                t1 = STT(MIX[:, j, :], MIX[:, j, :], P("ng", (l * 4 + g) * 8 + j), r, ALU.mult, ALU.mult, t)
                xt[j] = TT(X[:, j, 0:256], X[:, j, 0:256], MIX[:, j, :], ALU.add, t1, q=pool)
            rbs.give(rs, t1)
            return t

        def out_proj(name, kt, src, MIX, N, st, mfree):
            mt = []
            for m in range(8):
                s, b, t = proj(name, kt, src, N, st)
                mt.append(A(MIX[:, m, :], b[:, 0:N], ACT.Copy, t, mfree))
                ps.give(s, mt[-1])
            return mt

        def ffn(l, h_read):
            HID = view(0, 22, 256)
            MIX = view(22 * 256, 8, 256)
            GV = view(30 * 256, 4, 256)
            gfree = [None] * 4
            ht = pre_norm(l, 2, h_read)
            hid = []
            for j in range(22):
                pair = []
                for half in range(2):
                    i = (2 * j + half) % 4
                    s, b, t = proj(f"ffn_up{l}", 8, lambda k: H[:, k, 0:256], 256, ht)
                    m = j + 22 * half
                    t = conv_causal(b, t, s, GV[:, i, :], 3, lambda k, m=m: P("fcw", (l * 3 + k) * 44 + m),
                                    P("fcb", l * 44 + m), gfree[i], ar_free)
                    pair.append((i, t))
                (ig, tg), (iv, tv) = pair
                tg = A(GV[:, ig, :], GV[:, ig, :], ACT.Gelu_apprx_tanh, tg)
                t = TT(HID[:, j, :], GV[:, ig, :], GV[:, iv, :], ALU.mult, tg, tv, ar_free, q=pool)
                gfree[ig] = gfree[iv] = t
                hid.append(t)
            mt = out_proj(f"ffn_down{l}", 22, lambda k: HID[:, k, :], MIX, 256, hid, ar_free)
            post_norm(l, 3, MIX, mt, (s_pe, pe.n))

        ar_free = None

        def layer_even():
            Fb, Qb, Gb = view(0, 4, 256), view(1024, 4, 256), view(2048, 4, 256)
            Bc, E1, E2, E3 = (view(3072 + 1024 * i, 4, 256) for i in range(4))
            Vt = view(7168, 2, 512)
            SC = view(8192, 4, 2, 128)
            SS = view(9216, 4, 3 * 128)
            Y = view(10752, 8, 256)
            KT = view(12800, 4, 2, 128)
            KH = view(13824, 4, 256)
            XF = view(14848, 4, 256)
            RGW = view(15872, 8, 128)
            MIX = view(16896, 8, 256)
            lb, oml = SM[:, 0:4], SM[:, 4:8]
            load(RGW, rgw, s_rg)
            zt = dve.do(lambda e: e.memset(SC[:, :, :, :], 0.0))
            L = P("lbl", 0, 12)
            m_, e_, d_ = SM[:, 8:12], SM[:, 12:24], SM[:, 24:28]
            t = TT(m_, L[:, 0:4], L[:, 4:8], ALU.max, T_PR)
            t = TT(m_, m_, L[:, 8:12], ALU.max, t)
            for r in range(3):
                t1 = TT(e_[:, 4 * r:4 * r + 4], L[:, 4 * r:4 * r + 4], m_, ALU.subtract, t)
            t = A(e_, e_, ACT.Exp, t1)
            t = TT(d_, e_[:, 0:4], e_[:, 4:8], ALU.add, t)
            t = TT(d_, d_, e_[:, 8:12], ALU.add, t)
            t = REC(d_, d_, t)
            t = TT(lb, e_[:, 0:4], d_, ALU.mult, t)
            lbt = TS(oml, lb, -1.0, 1.0, ALU.mult, ALU.add, t)
            c8, nc8, sa, sb_ = SM[:, 32:36], SM[:, 36:40], SM[:, 40:44], SM[:, 44:48]
            lam = P("lam", 0, 4)
            t = log1p_exp_neg_abs(c8, lam, sa, sb_, T_PR)
            t = TS(sa, lam, -1.0, 0.0, ALU.mult, ALU.max, t)
            t = TT(c8, c8, sa, ALU.add, t)
            t = TS(c8, c8, 8.0, None, ALU.mult, None, t)
            c8t = TS(nc8, c8, -1.0, None, ALU.mult, None, t)

            ht = pre_norm(0, 0, None)
            rhs = lambda k: H[:, k, 0:256]
            ft, qt, gt = [], [], []
            for h in range(4):
                s, b, t = proj("even_w_in", 8, rhs, 256, ht)
                t = A(Fb[:, h, :], b[:, 0:256], ACT.Sigmoid, t)
                ps.give(s, t)
                ft.append(TS(Fb[:, h, :], Fb[:, h, :], oml[:, h:h + 1], lb[:, h:h + 1], ALU.mult, ALU.add, t, lbt))
            for h in range(4):
                s, b, t = proj("even_w_in", 8, rhs, 256, ht)
                t1 = A(Qb[:, h, :], b[:, 0:256], ACT.Sigmoid, t)
                t = TT(Qb[:, h, :], Qb[:, h, :], b[:, 0:256], ALU.mult, t1)
                ps.give(s, t)
                qt.append(t)
            for h in range(4):
                s, b, t = proj("even_w_in", 8, rhs, 256, ht)
                t = A(Gb[:, h, :], b[:, 0:256], ACT.Sigmoid, t)
                ps.give(s, t)
                gt.append(t)
            vt = []
            for n, (s, b, t) in enumerate(proj_tok("even_w_in", 8, lambda k, n: H[:, k, n * 128:n * 128 + 128],
                                                   2, 512, ht)):
                t = A(Vt[:, n, :], b[:, 0:512], ACT.Copy, t)
                ps.give(s, t)
                vt.append(t)
            kt_, bt = [], []
            for h in range(4):
                kt_.append(TS(KH[:, h, :], Fb[:, h, :], -1.0, 1.0, ALU.mult, ALU.add, ft[h]))
                t = A(Fb[:, h, :], Fb[:, h, :], ACT.Ln, ft[h], kt_[h])
                for n in range(4):
                    c = slice(64 * n, 64 * n + 64)
                    t1 = SCAN(Bc[:, h, c], C("ones")[:, 0:64], Fb[:, h, c], 0.0, ALU.mult, ALU.add, t, T_CS)
                bt.append(t1)
            qd, kd, kl, e1t = [], [], [], []
            for h in range(4):
                t1 = A(E1[:, h, :], Bc[:, h, :], ACT.Exp, bt[h])
                t2 = A(E2[:, h, :], Bc[:, h, :], ACT.Exp, bt[h], scale=-1.0)
                for n in range(4):
                    c = slice(64 * n, 64 * n + 64)
                    t3 = A(E3[:, h, c], Bc[:, h, c], ACT.Exp, bt[h], scale=-1.0,
                           bias=Bc[:, h, 64 * n + 63:64 * n + 64])
                e1t.append(t1)
                qd.append(TT(Qb[:, h, :], Qb[:, h, :], E1[:, h, :], ALU.mult, t1, qt[h]))
                kd.append(TT(E2[:, h, :], E2[:, h, :], KH[:, h, :], ALU.mult, t2, kt_[h]))
                kl.append(TT(E3[:, h, :], E3[:, h, :], KH[:, h, :], ALU.mult, t3, kt_[h]))
            yt = []
            for h in range(4):
                sct, ktt = [], []
                for p in range(2):
                    s, b, fr = ps.take()
                    for u in range(2):
                        c = slice(128 * p + 64 * u, 128 * p + 64 * u + 64)
                        r = slice(64 * u, 64 * u + 64)
                        t = MM([(b[r, r], E2[:, h, c], Qb[:, h, c])], fr, kd[h], qd[h])
                        t = A(SC[r, h, p, r], b[r, r], ACT.Copy, t, zt)
                    ps.give(s, t)
                    sc = SC[:, h, p, :]
                    sct.append(pool.do(lambda e, sc=sc: e.affine_select(
                        out=sc, in_=sc, compare_op=ALU.is_ge, fill=0.0, base=0, pattern=[[1, 128]],
                        channel_multiplier=-1), t))
                    s, b, fr = ps.take()
                    t = TR(b[:, 0:128], E3[:, h, 128 * p:128 * p + 128], 128, fr, kl[h], T_CS)
                    t = CP(KT[:, h, p, :], b[:, 0:128], t)
                    ps.give(s, t)
                    ktt.append(t)
                prev = None
                stt = []
                for n in range(3):
                    p, r = n // 2, slice(64 * (n % 2), 64 * (n % 2) + 64)
                    s, b, fr = ps.take()
                    t = MM([(b[:, 0:128], KT[r, h, p, :], Vt[r, p, 128 * h:128 * h + 128])], fr, ktt, vt)
                    o = SS[:, h, 128 * n:128 * n + 128]
                    if n == 0:
                        t = CP(o, b[:, 0:128], t)
                    else:
                        t = STT(o, SS[:, h, 128 * n - 128:128 * n], E1[:, h, 64 * n + 63:64 * n + 64], b[:, 0:128],
                                ALU.mult, ALU.add, t, prev, e1t[h])
                    ps.give(s, t)
                    prev = t
                    stt.append(t)
                s, b, fr = ps.take()
                for p in range(2):
                    g = [(b[:, 128 * p:128 * p + 128], Vt[:, p, 128 * h:128 * h + 128], SC[:, h, p, :])]
                    for n in (2 * p, 2 * p + 1):
                        if n:
                            g.append((b[:, 64 * n:64 * n + 64], SS[:, h, 128 * (n - 1):128 * n],
                                      Qb[:, h, 64 * n:64 * n + 64]))
                    t = MM(g, fr, sct, vt, stt, qd[h])
                t = CP(Y[:, h, :], b[:, 0:256], t)
                ps.give(s, t)
                yt.append(t)
            for h in range(4):
                q, tb, tf = tmp.take()
                rs, r, t, tq = inv_rms(lambda j: Y[:, h, :], 1, 0, 256, C("mean128"), [[yt[h], tf]],
                                       lambda j: tb[:, 0:256])
                tmp.give(q, tq)
                t = STT(Y[:, h, :], Y[:, h, :], P("hgn", h), r, ALU.mult, ALU.mult, t)
                rbs.give(rs, t)
                yt[h] = TT(Y[:, h, :], Y[:, h, :], Gb[:, h, :], ALU.mult, t, gt[h])
            xft = []
            for j in range(4):
                s, b, t = proj("even_w_in", 8, rhs, 256, ht)
                xft.append(conv_causal(b, t, s, XF[:, j, :], 4, lambda k, j=j: P("rcw", 4 * k + j), P("rcb", j)))
            read_r = (s_pe, pe.n)
            Rr, Ii, Tt, Aa = Fb, E1, E2, Bc
            rit = []
            for j in range(4):
                two = []
                for g, (dst, bn) in enumerate(((Rr, "rba"), (Ii, "rbx"))):
                    s, b, fr = ps.take()
                    t = MM([(b[:, 0:256], RGW[:, 4 * g + j, :], XF[:, j, :])], fr, xft[j], (s_rg, 16))
                    t = A(dst[:, j, :], b[:, 0:256], ACT.Sigmoid, t, stt, qd[j], kd[j], yt, (s_dve, dve.n), bias=P(bn, j))
                    ps.give(s, t)
                    two.append(t)
                rit.append(two)
            at_ = []
            for j in range(4):
                t1 = A(Tt[:, j, :], Rr[:, j, :], ACT.Tanh, rit[j], (s_pe, pe.n), scale=c8[:, j:j + 1])
                t2 = A(Aa[:, j, :], Rr[:, j, :], ACT.Exp, rit[j], c8t, scale=nc8[:, j:j + 1])
                at_.append((t1, t2))
            for j in range(4):
                t = TS(Rr[:, j, :], Tt[:, j, :], 1.0, None, ALU.add, None, at_[j][0], at_[j][1])
                t = REC(Rr[:, j, :], Rr[:, j, :], t)
                t = STT(Rr[:, j, :], Rr[:, j, :], 2.0, Tt[:, j, :], ALU.mult, ALU.mult, t)
                t = A(Rr[:, j, :], Rr[:, j, :], ACT.Sqrt, t)
                t1 = TT(Ii[:, j, :], Ii[:, j, :], XF[:, j, :], ALU.mult, rit[j], (s_pe, pe.n))
                t = TT(Rr[:, j, :], Rr[:, j, :], Ii[:, j, :], ALU.mult, t, t1)
                t = SCAN(Y[:, 4 + j, :], Aa[:, j, :], Rr[:, j, :], 0.0, ALU.mult, ALU.add, t, at_[j][1])
                yt.append(t)
            for j in range(4):
                s, b, t = proj("even_w_in", 8, rhs, 256, ht)
                q, tb, tf = tmp.take()
                t = A(tb[:, 0:256], b[:, 0:256], ACT.Gelu_apprx_tanh, t, tf)
                ps.give(s, t)
                yt[4 + j] = TT(Y[:, 4 + j, :], Y[:, 4 + j, :], tb[:, 0:256], ALU.mult, t, yt[4 + j])
                tmp.give(q, yt[4 + j])
            hread = (s_pe, pe.n)
            if done("hgrn", Y, yt):
                return True
            mt = out_proj("even_w_out", 8, lambda k: Y[:, k, :], MIX, 256, yt, None)
            post_norm(0, 1, MIX, mt, hread)
            return False

        def layer_fox():
            free = ar_free
            Vt = view(0, 2, 1024)
            Cc, Nc, La = view(2048, 256), view(2304, 256), view(2560, 256)
            Lb = view(2816, 256)
            Y = view(3072, 8, 256)
            QE = [view(5120 + 768 * i, 256) for i in range(2)]
            QO = [view(5120 + 768 * i + 256, 256) for i in range(2)]
            KK = [view(5120 + 768 * i + 512, 256) for i in range(2)]
            PP = Slots([view(6656 + 256 * i, 256) for i in range(4)])
            PT = Slots([view(7680 + 384 * i, 384) for i in range(3)])
            SEL = view(8960, 16, 256)
            MIX = view(13056, 8, 256)
            ht = pre_norm(1, 0, free)
            rhs = lambda k: H[:, k, 0:256]
            st = []
            for h in range(16):
                st.append(TS(SEL[:, h, :], C("ones"), ident[:, h:h + 1], None, ALU.mult, None, T_CS, free, q=pool))
            s, b, t = proj("odd_w_in", 8, rhs, 256, ht)
            t = A(Nc, b[:, 0:256], ACT.Identity, t, free, bias=P("fxb"))
            ps.give(s, t)
            t = log_sigmoid(Cc, Nc, La, Lb, t)
            t = SCAN(La, C("ones"), Cc, 0.0, ALU.mult, ALU.add, t)
            t1 = CP(Cc, La, t)
            ct = TS(Nc, La, -1.0, None, ALU.mult, None, t, t1)
            vt = []
            for c in range(2):
                for n, (s, b, t) in enumerate(proj_tok("odd_w_in", 8, lambda k, n: H[:, k, n * 128:n * 128 + 128],
                                                       2, 512, ht)):
                    t = A(Vt[:, n, 512 * c:512 * c + 512], b[:, 0:512], ACT.Copy, t, free)
                    ps.give(s, t)
                    vt.append(t)
            yt = []
            read = [None, None]
            for j in range(8):
                i = j % 2
                s, b, t = proj("odd_w_in", 8, rhs, 256, ht)
                t1 = TS(QE[i], b[:, 0:256], c_even, None, ALU.mult, None, t, read[i], free)
                t2 = TS(QO[i], b[:, 0:256], c_odd, None, ALU.mult, None, t)
                ps.give(s, t2)
                s, b, t = proj("odd_w_in", 8, rhs, 256, ht)
                t3 = A(KK[i], b[:, 0:256], ACT.Copy, t, read[i], free)
                ps.give(s, t3)
                for par, Q in ((0, QE[i]), (1, QO[i])):
                    h = 2 * j + par
                    qp, PTb, pf = PT.take()
                    ptt = []
                    for qb in range(2):
                        end = 128 * (qb + 1)
                        s, b, fr = ps.take()
                        t = MM([(b[:, 0:end], Q[:, 128 * qb:end], KK[i][:, 0:end]),
                                (b[:, 0:end], Cc[:, 128 * qb:end], SEL[:, h, 0:end]),
                                (b[:, 0:end], SEL[:, h, 0:128], Nc[:, 0:end]),
                                (b[:, 128 * qb:end], ident, C("maskd"))], fr, t1, t2, t3, ct, st, T_CS)
                        read[i] = t
                        ptt.append(softmax(s, b, t, end, 1.0, PP, free, pf,
                                           PTb[:, 128 * qb:128 + 256 * qb]))
                    s, b, fr = ps.take()
                    vc = slice(128 * j, 128 * j + 128)
                    t = MM([(b[:, 0:256], Vt[:, 0, vc], PTb[:, 0:256]),
                            (b[:, 128:256], Vt[:, 1, vc], PTb[:, 256:384])], fr, ptt, vt)
                    PT.give(qp, t)
                    r = slice(64 * par, 64 * par + 64)
                    t = CP(Y[r, j, :], b[r, 0:256], t, free)
                    ps.give(s, t)
                    yt.append(t)
            hread = (s_pe, pe.n)
            if done("fox", Y, yt):
                return True
            mt = out_proj("odd_w_out", 8, lambda k: Y[:, k, :], MIX, 256, yt, free)
            post_norm(1, 1, MIX, mt, hread)
            return False

        smc = [0]

        def softmax(s, b, t, end, scale, PP, free, pf, dst):
            col = 64 + 4 * (smc[0] % 32)
            smc[0] += 1
            nm, su, rs = (SM[:, col + i:col + i + 1] for i in range(3))
            q, p, f2 = PP.take()
            t = dve.do(lambda e: e.tensor_reduce(nm, b[:, 0:end], AXX, ALU.max, negate=True), t, smfree[smc[0] % 32])
            if scale != 1.0:
                t = TS(nm, nm, scale, None, ALU.mult, None, t)
            t = A(p[:, 0:end], b[:, 0:end], ACT.Exp, t, f2, free, bias=nm, scale=scale, accum=su)
            ps.give(s, t)
            t = REC(rs, su, t)
            t = TS(p[:, 0:end], p[:, 0:end], rs, None, ALU.mult, None, t)
            smfree[smc[0] % 32] = t
            s, b2, fr = ps.take()
            for k in range(end // 128):
                t = TR(b2[:, 128 * k:128 * k + 128], p[:, 128 * k:128 * k + 128], 128, fr, t)
            PP.give(q, t)
            if smc[0] % 2:
                t = CP(dst, b2[:, 0:end], t, pf, free)
            else:
                t = A(dst, b2[:, 0:end], ACT.Copy, t, pf, free)
            ps.give(s, t)
            return t

        smfree = [None] * 32

        def everything_read():
            return [(q.sem, q.n) for q in (pe, act, dve, pool) if q.n]

        MODC = view(19968, 192)
        SCC = view(20160, 16)
        MC = view(20176, 96)

        def mod(l, j, seq):
            return MODC[:, l * 96 + 2 * j + seq:l * 96 + 2 * j + seq + 1]

        def adaln():
            t0 = A(SCC, P("cc", 0, 16), ACT.Sigmoid, ar_free)
            t0 = TT(SCC, SCC, P("cc", 0, 16), ALU.mult, t0)
            for l in range(2):
                s, b, fr = ps.take()
                for m in range(24):
                    pe.wait(fr, t0)
                    for k in range(8):
                        wt = weights(f"w_mod{l}", 1, None)
                        f = lambda e, wt=wt, k=k, m=m, b=b: e.matmul(
                            b[:, 2 * m:2 * m + 2], wt, SCC[:, 2 * k:2 * k + 2], start=(k == 0), stop=(k == 7))
                        if k < 7:
                            pe.plain(f)
                    t = pe.do(f)
                    weights_read(t)
                t = TT(MODC[:, 96 * l:96 * l + 96][:, 0:48], b[:, 0:48], P("bmod", 48 * l, 48), ALU.add, t, ar_free)
                ps.give(s, t)
                for seq in range(2):
                    for j in range(8):
                        t1 = STT(MC[:, 32 * l + 2 * j + seq:32 * l + 2 * j + seq + 1], mod(l, 8 + j, seq), 1.0,
                                 P("gpre", 8 * l + j), ALU.add, ALU.mult, t)
                        t2 = TT(MC[:, 32 * l + 16 + 2 * j + seq:32 * l + 16 + 2 * j + seq + 1], mod(l, 16 + j, seq),
                                P("gpost", 8 * l + j), ALU.mult, t)
            return [t1, t2]

        def pre_norm2(l, mt, hfree):
            rs, r, t, _ = inv_rms(lambda j: X[:, j, :], 8, 0, 512, C("mean"),
                                  [[xt[j], hfree] for j in range(8)], lambda j: H[:, j, :])
            ht = []
            for j in range(8):
                for seq in range(2):
                    c = slice(256 * seq, 256 * seq + 256)
                    t1 = STT(H[:, j, c], X[:, j, c], MC[:, 32 * l + 2 * j + seq:32 * l + 2 * j + seq + 1], r[:, c],
                             ALU.mult, ALU.mult, t, mt)
                    ht.append(A(H[:, j, c], H[:, j, c], ACT.Identity, t1, bias=mod(l, j, seq)))
            rbs.give(rs, t1)
            return ht

        def post_norm2(l, MIX, mt, hfree, nseq):
            N = 256 * nseq
            rs, r, t, _ = inv_rms(lambda j: MIX[:, j, 0:N], 8, 0, N, C("mean"),
                                  [[mt[j], hfree] for j in range(8)], lambda j: H[:, j, 0:N])
            for j in range(8):
                both = []
                for seq in range(nseq):
                    c = slice(256 * seq, 256 * seq + 256)
                    t1 = STT(MIX[:, j, c], MIX[:, j, c], MC[:, 32 * l + 16 + 2 * j + seq:32 * l + 16 + 2 * j + seq + 1],
                             r[:, c], ALU.mult, ALU.mult, t)
                    both.append(TT(X[:, j, c], X[:, j, c], MIX[:, j, c], ALU.add, t1, q=pool))
                xt[j] = both
            rbs.give(rs, t1)

        def two(ap):
            return ap.rearrange("p (s t) -> p s t", s=2)

        def conv3(b, tok, s, dst, N, taps, bias, *w):
            t = A(dst, b[:, 0:N], ACT.Identity, tok, *w, bias=bias, scale=taps(1))
            d, x = (two(dst), two(b[:, 0:N])) if N == 512 else (dst, b[:, 0:N])
            if N == 512:
                t = STT(d[:, :, 1:256], x[:, :, 0:255], taps(0), d[:, :, 1:256], ALU.mult, ALU.add, t)
                t = STT(d[:, :, 0:255], x[:, :, 1:256], taps(2), d[:, :, 0:255], ALU.mult, ALU.add, t)
            else:
                t = STT(d[:, 1:256], x[:, 0:255], taps(0), d[:, 1:256], ALU.mult, ALU.add, t)
                t = STT(d[:, 0:255], x[:, 1:256], taps(2), d[:, 0:255], ALU.mult, ALU.add, t)
            ps.give(s, t)
            return t

        def sine(dst, x, k, tok):
            big = 12582912.0
            t = TS(k, x, 1.0 / (2 * math.pi), big, ALU.mult, ALU.add, tok)
            t = TS(k, k, big, None, ALU.subtract, None, t)
            c1 = 6.28125
            t = STT(x, k, -c1, x, ALU.mult, ALU.add, t)
            t = STT(x, k, -(2 * math.pi - c1), x, ALU.mult, ALU.add, t)
            t = TS(x, x, 3.1415925, -3.1415925, ALU.min, ALU.max, t)
            return A(dst, x, ACT.Sin, t)

        def hyena_filter():
            free = ar_free
            HF = view(0, 4, 1024)
            W3, DC = view(4096, 2048), view(6144, 2, 1024)
            FW = view(8192, 128)
            HD, HE, HK = view(8320, 256), view(8576, 256), view(8832, 256)
            HP, HM = view(9088, 2, 1024), view(11136, 2, 1024)
            NI = view(13184, 1024)
            h1 = Slots([view(14208 + 512 * i, 512) for i in range(4)])
            load(W3[0:64, :], fw[:, 128:2176], s_fw, free)
            load(FW[0:64, :], fw[:, 0:128], s_fw, free)
            load(DC, dec, s_dec, free)
            R = slice(0, 64)
            s, b, fr = ps.take()
            t = MM([(b[R, 0:256], FW[R, 0:64], CS[R, COFF["zT"][0]:COFF["zT"][0] + 256])], fr, (s_fw, 32))
            t = TS(HD[R], b[R, 0:256], P("fb1")[R], P("ffr")[R], ALU.add, ALU.mult, t, free)
            ps.give(s, t)
            t = sine(HE[R], HD[R], HK[R], t)
            s, b, fr = ps.take()
            t = MM([(b[R, 0:256], FW[R, 64:128], HE[R])], fr, t)
            t = TS(HD[R], b[R, 0:256], P("fb2")[R], P("ffr")[R], ALU.add, ALU.mult, t)
            ps.give(s, t)
            hd = sine(HE[R], HD[R], HK[R], t)
            norm = []
            for c in range(2):
                cc = slice(512 * c, 512 * c + 512)
                sN, bN, frN = ps.take()
                absn = []
                hpm = []
                for n in range(2):
                    q0, a0, f0 = h1.take()
                    q1, a1, f1 = h1.take()
                    s, b, fr = ps.take()
                    t = MM([(b[:, :], HE[R, 128 * n:128 * n + 128], W3[R, cc])], fr, hd)
                    t0 = TT(a0, b[:, :], DC[:, n, cc], ALU.mult, t, f0, free, (s_dec, 16))
                    ps.give(s, t0)
                    s, b, fr = ps.take()
                    t = MM([(b[:, :], HE[R, 128 * n:128 * n + 128], W3[R, 1024 + 512 * c:1536 + 512 * c])], fr)
                    if n == 0:
                        t1 = STT(a1, b[:, :], c_m0, DC[:, n, cc], ALU.mult, ALU.mult, t, f1, free)
                    else:
                        t1 = TT(a1, b[:, :], DC[:, n, cc], ALU.mult, t, f1, free)
                    ps.give(s, t1)
                    tp = TT(HP[:, n, cc], a0, a1, ALU.add, t0, t1, free)
                    tm_ = TT(HM[:, n, cc], a0, a1, ALU.subtract, t0, t1, free)
                    hpm += [tp, tm_]
                    t0 = A(a0, a0, ACT.Abs, tp, tm_)
                    t1 = A(a1, a1, ACT.Abs, tp, tm_)
                    absn += [(a0, t0), (a1, t1)]
                t = MM([(bN[:, :], C("ones")[:, 0:128], a) for a, _ in absn], frN, [x for _, x in absn])
                h1.give(0, t), h1.give(1, t), h1.give(2, t), h1.give(3, t)
                nt = REC(NI[:, cc], bN[:, :], t, free)
                ps.give(sN, nt)
                for f in range(4):
                    src = HP if f < 2 else HM
                    s, b, fr = ps.take()
                    t = MM([(b[:, :], C("dft")[:, 512 * n + 128 * f:512 * n + 128 * f + 128], src[:, n, cc])
                            for n in range(2)], fr, hpm)
                    t = TT(HF[:, f, cc], b[:, :], NI[:, cc], ALU.mult, t, nt, free)
                    ps.give(s, t)
                    norm.append(t)
            return HF, norm

        def layer_even2():
            mt = adaln()
            if done("mod", AR[:, 19968:20272], mt):
                return True
            HF, hft = hyena_filter()
            if done("filt", HF, hft):
                return True
            G = view(4096, 8, 512)
            Y = view(8192, 16, 512)
            KR = view(16384, 2, 512)
            VT = view(17408, 4, 256)
            free = everything_read()
            ht = pre_norm2(0, mt, None)
            rhs = lambda k: H[:, k, :]
            gt = []
            for j in range(8):
                q0, a0, f0 = tmp.take()
                s, b, t = proj("e_w_in", 8, rhs, 512, ht)
                t0 = conv3(b, t, s, a0, 512, lambda k, j=j: P("ecw", 24 * k + 8 + j), P("ecb", 8 + j), f0)
                s, b, t = proj("e_w_in", 8, rhs, 512, ht)
                t1 = conv3(b, t, s, G[:, j, :], 512, lambda k, j=j: P("ecw", 24 * k + 16 + j), P("ecb", 16 + j), free)
                gt.append(TT(G[:, j, :], G[:, j, :], a0, ALU.mult, t0, t1))
                tmp.give(q0, gt[-1])
            yt = []
            for j in range(8):
                s, b, t = proj("e_w_in", 8, rhs, 512, ht)
                yt.append(conv3(b, t, s, Y[:, j, :], 512, lambda k, j=j: P("ecw", 24 * k + j), P("ecb", j), free))

            def qk_norm(dst, gain, rot_scale):
                s, b, t = proj("e_w_in", 8, rhs, 512, ht)
                t0 = A(dst, b[:, :], ACT.Copy, t, free)
                ps.give(s, t0)
                q, tb, tf = tmp.take()
                rs, r, t, tq = inv_rms(lambda j: dst, 1, 0, 512, C("mean128"), [[t0, tf]], lambda j: tb)
                t = STT(dst, dst, gain, r, ALU.mult, ALU.mult, t)
                rbs.give(rs, t)
                s, b, fr = ps.take()
                t1 = MM([(b[:, 0:256], C("perm"), dst[:, 0:256])], fr, t)
                t2 = TT(tb[:, 0:256], b[:, 0:256], C("sin"), ALU.mult, t1, tq)
                ps.give(s, t2)
                t3 = TT(dst[:, 0:256], dst[:, 0:256], C("cos"), ALU.mult, t, t1)
                t4 = TT(dst[:, 0:256], dst[:, 0:256], tb[:, 0:256], ALU.add, t2, t3)
                tmp.give(q, t4)
                return t4

            kt = [qk_norm(KR[:, i, :], P("kn"), None) for i in range(2)]
            vt = []
            for n, (s, b, t) in enumerate(proj_tok("e_w_in", 8, lambda k, n: H[:, k, 128 * n:128 * n + 128],
                                                   4, 256, ht)):
                t = A(VT[:, n, :], b[:, 0:256], ACT.Copy, t, free)
                ps.give(s, t)
                vt.append(t)
            qt = [qk_norm(Y[:, 8 + h, :], P("qn"), None) for h in range(8)]
            if stop == "proj2" and done("proj2", Y, yt, qt):
                return True
            scale = 128 ** -0.5
            PTb = Slots([view(18432 + 512 * 0, 512), view(18432 + 512, 512), view(18432 + 1024, 512)])
            for h in range(8):
                Qh, Kh = Y[:, 8 + h, :], KR[:, h // 4, :]
                vc = slice(128 * (h // 4), 128 * (h // 4) + 128)
                for seq in range(2):
                    nk = 4 if seq == 0 else 2
                    k0 = 0 if seq == 0 else 2
                    s2, ob, ofr = None, None, None
                    for qb in range(2):
                        qc = slice(256 * seq + 128 * qb, 256 * seq + 128 * qb + 128)
                        s, b, fr = ps.take()
                        t = MM([(b[:, 0:128 * nk], Qh[:, qc], Kh[:, 128 * k0:512])], fr, kt, qt[h])
                        qp, pt, pf = PTb.take()
                        tt = softmax(s, b, t, 128 * nk, scale, tmp, None, [pf, free],
                                     pt[:, 0:128 * nk])
                        s, b, fr = ps.take()
                        t = MM([(b[:, 0:128], VT[:, k0 + k, vc], pt[:, 128 * k:128 * k + 128]) for k in range(nk)],
                               fr, tt, vt)
                        PTb.give(qp, t)
                        t1 = CP(Qh[:, qc], b[:, 0:128], t)
                        ps.give(s, t1)
                    qt[h] = t1
            GT = [view(16384, 2, 512), view(17408, 2, 512)]
            sp_free = everything_read()
            gtf = [sp_free, sp_free]
            n_ = 0
            for seq in range(2):
                for c in range(2):
                    g_ = GT[n_ % 2]
                    gf = gtf[n_ % 2]
                    trs = []
                    for tb in range(2):
                        s, b, fr = ps.take()
                        for jj in range(4):
                            t = TR(b[:, 128 * jj:128 * jj + 128],
                                   G[:, 4 * c + jj, 256 * seq + 128 * tb:256 * seq + 128 * tb + 128], 128, fr,
                                   gt[4 * c + jj])
                        t = CP(g_[:, tb, :], b[:, :], t, gf)
                        ps.give(s, t)
                        trs.append(t)
                    spec = []
                    for fb in range(2):
                        U = []
                        for part in range(2):
                            f = 2 * part + fb
                            s, b, fr = ps.take()
                            t = MM([(b[:, :], C("dft")[:, 512 * n + 128 * f:512 * n + 128 * f + 128], g_[:, n, :])
                                    for n in range(2)], fr, trs)
                            U.append((s, b, t))
                        cc = slice(512 * c, 512 * c + 512)
                        (sr, ur, tr_), (si, ui, ti_) = U
                        hr, hi = HF[:, fb, cc], HF[:, 2 + fb, cc]
                        qa, a_, fa = tmp.take()
                        qb_, b_, fb_ = tmp.take()
                        qc_, c_, fc_ = tmp.take()
                        t0 = TT(a_, ur, hr, ALU.mult, tr_, fa, hft)
                        t1 = TT(b_, ui, hi, ALU.mult, ti_, fb_)
                        t2 = TT(a_, a_, b_, ALU.subtract, t0, t1)
                        t3 = TT(c_, ur, hi, ALU.mult, tr_, fc_)
                        ps.give(sr, t3)
                        t4 = TT(b_, ui, hr, ALU.mult, ti_, t2)
                        ps.give(si, t4)
                        t5 = TT(c_, c_, b_, ALU.add, t3, t4)
                        tmp.give(qb_, t5)
                        spec.append((qa, a_, t2, qc_, c_, t5))
                    gtf[n_ % 2] = [U[1][2]]
                    for jj in range(4):
                        j = 4 * c + jj
                        s, b, fr = ps.take()
                        rows = [(spec[0][1], 0), (spec[1][1], 1), (spec[0][4], 2), (spec[1][4], 3)]
                        t = MM([(b[:, 0:256], a[:, 128 * jj:128 * jj + 128], C("idft")[:, 256 * f:256 * f + 256])
                                for a, f in rows], fr, [x[2] for x in spec], [x[5] for x in spec])
                        sc_ = slice(256 * seq, 256 * seq + 256)
                        t1 = STT(G[:, j, sc_], G[:, j, sc_], P("hyb", j), b[:, 0:256], ALU.mult, ALU.add, t)
                        ps.give(s, t1)
                        yt[j] = TT(Y[:, j, sc_], Y[:, j, sc_], G[:, j, sc_], ALU.mult, t1, yt[j])
                    for x in spec:
                        tmp.give(x[0], t)
                        tmp.give(x[3], t)
                    n_ += 1
            if stop == "mix2" and done("mix2", Y, yt, qt):
                return True
            yt = yt + qt
            for j in range(16):
                s, b, t = proj("e_w_in", 8, rhs, 512, ht)
                q, tb, tf = tmp.take()
                t = A(tb, b[:, :], ACT.Silu, t, tf)
                ps.give(s, t)
                yt[j] = TT(Y[:, j, :], Y[:, j, :], tb, ALU.mult, t, yt[j])
                tmp.give(q, yt[j])
            hread = (s_pe, pe.n)
            MIX = view(4096, 8, 512)
            mt_ = out_proj("e_w_out", 16, lambda k: Y[:, k, :], MIX, 512, yt, [(s_dve, dve.n), (s_pe, pe.n)])
            post_norm2(0, MIX, mt_, hread, 2)
            if done("x2", X[:, :, :], xt):
                return True
            return False

        def layer_odd2():
            free = everything_read()
            VT = view(0, 4, 2048)
            Y = view(8192, 16, 256)
            GI, GF, GA = view(12288, 512), view(12800, 512), view(13312, 512)
            LI, LF, LB, LM = (view(13824 + 1024 * i, 2, 512) for i in range(4))
            AN, NM, EM = view(17920, 2, 512), view(18944, 2, 256), view(19456, 2, 256)
            ht = pre_norm2(1, None, free)
            rhs = lambda k: H[:, k, :]
            s, b, t = proj("o_w_in", 8, rhs, 512, ht)
            tg = A(GI, b[:, :], ACT.Identity, t, free, bias=P("gtb"))
            ps.give(s, tg)
            q1, a1, f1 = tmp.take()
            q2, a2, f2 = tmp.take()
            t = log_sigmoid(GF, GI, a1, a2, [tg, f1, f2])
            tmp.give(q1, t), tmp.give(q2, t)
            R8 = slice(0, 8)
            lat, cx = slice(0, 256), slice(256, 512)
            for d in range(2):
                for dst, src, row in ((LI, GI, 64 * d), (LF, GF, 64 * d + 32)):
                    for o, c in ((0, cx), (256, lat)):
                        sv = src[row:row + 8, c]
                        if d:
                            sv = sv[:, ::-1]
                        t1 = CP(dst[R8, d, o:o + 256], sv, t, tg, free)
            for d in range(2):
                t = SCAN(LB[R8, d, :], ONE8, LF[R8, d, :], 0.0, ALU.mult, ALU.add, t1, on8)
                t = TT(LI[R8, d, :], LI[R8, d, :], LB[R8, d, :], ALU.subtract, t)
                t = SCAN(LM[R8, d, :], LI[R8, d, :], LI[R8, d, :], 0.0, ALU.max, ALU.max, t)
                t = TT(LB[R8, d, :], LB[R8, d, :], LM[R8, d, :], ALU.add, t)
                v = (lambda x: x[:, ::-1]) if d else (lambda x: x)
                t2 = CP(AN[R8, d, 0:256], v(LI[R8, d, 256:512]), t, free)
                t3 = CP(AN[R8, d, 256:512], v(LI[R8, d, 0:256]), t)
                t4 = TS(NM[R8, d, :], v(LM[R8, d, 256:512]), -1.0, None, ALU.mult, None, t, free)
                t5 = TS(EM[R8, d, :], v(LB[R8, d, 256:512]), -1.0, None, ALU.mult, None, t, free)
                et = A(EM[R8, d, :], EM[R8, d, :], ACT.Exp, t5)
            AC = SM[:, 256:320]
            s, b, fr = ps.take()
            for d in range(2):
                for k in range(4):
                    t = TR(b[:, 8 * (4 * d + k):8 * (4 * d + k) + 8], AN[R8, d, 128 * k:128 * k + 128], 8, fr, t3)
            act_ = CP(AC, b[:, 0:64], t)
            ps.give(s, act_)
            rows_t = [act_, et, t4]
            if stop == "gates" and done("gates", AR[0:8, 17920:19968], rows_t, t3):
                return True
            vt = []
            for c in range(4):
                for n, (s, b, t) in enumerate(proj_tok("o_w_in", 8, lambda k, n: H[:, k, 128 * n:128 * n + 128],
                                                       4, 512, ht)):
                    t = A(VT[:, n, 512 * c:512 * c + 512], b[:, :], ACT.Copy, t, free)
                    ps.give(s, t)
                    vt.append(t)
            QK = [view(12288, 256), view(12544, 512)]
            ST, WW = view(13056, 4, 256), view(14080, 4, 256)
            DEN = Slots([view(15104, 256), view(15360, 256)])
            EMS = Slots([view(15616, 512), view(16128, 512)])
            qk_read, st_read, ww_read = rows_t, rows_t, rows_t
            yt = []
            for h in range(8):
                s, b, t = proj("o_w_in", 8, lambda k: H[:, k, 0:256], 256, ht)
                t = conv3(b, t, s, QK[0], 256, lambda k, h=h: P("ocw", 16 * k + h), P("ocb", h), qk_read, free)
                tq = A(QK[0], QK[0], ACT.Silu, t)
                s, b, t = proj("o_w_in", 8, rhs, 512, ht)
                t = conv3(b, t, s, QK[1], 512, lambda k, h=h: P("ocw", 16 * k + 8 + h), P("ocb", 8 + h), qk_read)
                tk = A(QK[1], QK[1], ACT.Silu, t)
                stt = []
                for pr_ in range(2):
                    s, b, fr = ps.take()
                    for i in range(2):
                        k = 2 * pr_ + i
                        t = MM([(b[:, 256 * i:256 * i + 256], QK[1][:, 128 * k:128 * k + 128], QK[0])], fr, tq, tk)
                    o = ST[:, 2 * pr_:2 * pr_ + 2, :]
                    t1 = A(o, two(b[:, :]), ACT.Copy, t, st_read, scale=128 ** -0.5)
                    ps.give(s, t1)
                    stt.append(t1)
                qk_read = t
                for d in range(2):
                    s, b, fr = ps.take()
                    sel = C("sel8", 8)[:, 128 * h:128 * h + 128]
                    t = MM([(b[:, 0:256], sel, NM[R8, d, :])], fr, rows_t)
                    t = MM([(b[:, 256:512], sel, EM[R8, d, :])])
                    qe, ems, ef = EMS.take()
                    te = A(ems, b[:, :], ACT.Copy, t, ef)
                    ps.give(s, te)
                    nm, em = ems[:, 0:256], ems[:, 256:512]
                    wt = []
                    for k in range(4):
                        col = AC[:, 8 * (4 * d + k) + h:8 * (4 * d + k) + h + 1]
                        if k < 2:
                            mk = C("maskb" if d else "maskf")[:, 256 * k:256 * k + 256]
                            t1 = STT(WW[:, k, :], nm, col, mk, ALU.add, ALU.add, te, ww_read)
                            t1 = A(WW[:, k, :], WW[:, k, :], ACT.Exp, t1)
                        else:
                            t1 = A(WW[:, k, :], nm, ACT.Exp, te, ww_read, bias=col)
                        wt.append(t1)
                    t1 = TT(WW[:, 0:2, :], WW[:, 0:2, :], ST[:, 0:2, :], ALU.mult, wt[0:2], stt)
                    t2 = TT(WW[:, 2:4, :], WW[:, 2:4, :], ST[:, 2:4, :], ALU.mult, wt[2:4], stt, q=pool)
                    sd, bd, frd = ps.take()
                    td = MM([(bd[:, 0:256], C("ones")[:, 0:128], WW[:, k, :]) for k in (2, 3, 0, 1)], frd, t1, t2)
                    sn, bn, frn = ps.take()
                    for vb in range(2):
                        c = 256 * h + 128 * vb
                        tn = MM([(bn[:, 256 * vb:256 * vb + 256], VT[:, k, c:c + 128], WW[:, k, :])
                                 for k in (2, 3, 0, 1)], frn, vt)
                    ww_read = tn
                    qd_, den, df = DEN.take()
                    t = A(den, bd[:, 0:256], ACT.Abs, td, df)
                    ps.give(sd, t)
                    t = TT(den, den, em, ALU.max, t, te)
                    EMS.give(qe, t, wt)
                    t = REC(den, den, t)
                    for vb in range(2):
                        yv = Y[:, 2 * h + vb, :]
                        if d == 0:
                            t1 = TT(yv, bn[:, 256 * vb:256 * vb + 256], den, ALU.mult, t, tn, free)
                            if vb == 0:
                                ta = t1
                            else:
                                tb_ = t1
                        else:
                            q, x_, f = tmp.take()
                            t1 = TT(x_[:, 0:256], bn[:, 256 * vb:256 * vb + 256], den, ALU.mult, t, tn, f)
                            t2 = TT(yv, yv, x_[:, 0:256], ALU.add, t1, ta, tb_, q=pool)
                            tmp.give(q, t2)
                            yt.append(t2)
                    ps.give(sn, t1)
                    DEN.give(qd_, t1)
                st_read = ww_read
            if stop == "mlstm" and done("mlstm", Y, yt):
                return True
            ZZ = view(0, 16, 256)
            zfree = (s_pe, pe.n)
            zt = []
            for j in range(16):
                s, b, t = proj("o_w_in", 8, lambda k: H[:, k, 0:256], 256, ht)
                q, x_, f = tmp.take()
                t = A(x_[:, 0:256], b[:, 0:256], ACT.Sigmoid, t, f)
                ps.give(s, t)
                yt[j] = TT(Y[:, j, :], Y[:, j, :], x_[:, 0:256], ALU.mult, t, yt[j])
                tmp.give(q, yt[j])
                s, b, t = proj("o_w_in", 8, lambda k: H[:, k, 0:256], 256, ht)
                t1 = A(ZZ[:, j, :], b[:, 0:256], ACT.Sigmoid, t, zfree)
                t = TT(ZZ[:, j, :], ZZ[:, j, :], b[:, 0:256], ALU.mult, t1)
                ps.give(s, t)
                zt.append(t)
            hread = (s_pe, pe.n)
            for h in range(8):
                sq = [tmp.take(), tmp.take()]
                rs, r, t, tq = inv_rms(lambda j: Y[:, 2 * h + j, :], 2, 0, 256, C("mean256"),
                                       [[yt[2 * h], sq[0][2]], [yt[2 * h + 1], sq[1][2]]],
                                       lambda j: sq[j][1][:, 0:256])
                tmp.give(sq[0][0], tq), tmp.give(sq[1][0], tq)
                for j in (2 * h, 2 * h + 1):
                    t1 = STT(Y[:, j, :], Y[:, j, :], P("ohn", j), r, ALU.mult, ALU.mult, t)
                    yt[j] = TT(Y[:, j, :], Y[:, j, :], ZZ[:, j, :], ALU.mult, t1, zt[j])
                rbs.give(rs, t1)
            MIX = view(4096, 8, 256)
            mt_ = out_proj("o_w_out", 16, lambda k: Y[:, k, :], MIX, 256, yt, zfree)
            post_norm2(1, MIX, mt_, hread, 1)
            return False

        on8 = pool.do(lambda e: e.memset(ONE8, 1.0))

        def whole():
            nonlocal ar_free
            if layer_even():
                return
            if done("x0a", X[:, :, :], xt):
                return
            ar_free = everything_read()
            ffn(0, (s_pe, pe.n))
            if done("x0", X[:, :, :], xt):
                return
            ar_free = everything_read()
            if layer_fox():
                return
            ar_free = everything_read()
            ffn(1, (s_pe, pe.n))
            if done("x1", X[:, :, :], xt):
                return
            ar_free = everything_read()
            if layer_even2():
                return
            if layer_odd2():
                return
            assert state["t"] == len(plan)
            load(out, X[:, :, 0:256], s_out, xt)

        whole()
        used = (state["t"] + TPC - 1) // TPC
        ld = Queue(None)
        for c in range(used):
            while extra and extra[0][0] <= c:
                _, dst, src, sm, toks = extra.pop(0)
                ld.dma(lambda e, dst=dst, src=src: e.dma_start(dst, src), sm, *toks)
            w = release[c - RING] if c >= RING else None
            ld.dma(lambda e, c=c: e.dma_start(WR[:, c % RING, :], ws[c]), s_w[c % RING], w)
        for _, dst, src, sm, toks in extra:
            ld.dma(lambda e, dst=dst, src=src: e.dma_start(dst, src), sm, *toks)
        ld.wait((s_out, 16))

        block = ctx.enter_context(nc.Block())

        @block.sync
        def _(eng):
            ld.emit(eng)

        @block.tensor
        def _(eng):
            pe.emit(eng)

        @block.scalar
        def _(eng):
            act.emit(eng)

        @block.vector
        def _(eng):
            dve.emit(eng)

        @block.gpsimd
        def _(eng):
            pool.emit(eng)


def constants():
    off, n = const_layout()
    c = np.zeros((128, n), np.float64)

    def put(name, a):
        o, w = off[name]
        c[:a.shape[0], o:o + a.shape[1]] = a

    p, f = np.arange(128)[:, None], np.arange(256)[None, :]
    put("ident", np.eye(128))
    put("mean", np.full((128, 128), 1 / 1024))
    put("mean128", np.full((128, 128), 1 / 128))
    put("mean256", np.full((128, 128), 1 / 256))
    put("ones", np.ones((128, 256)))
    perm = np.zeros((128, 128))
    for base in (0, 64):
        for i in range(32):
            perm[base + 32 + i, base + i] = -1
            perm[base + i, base + 32 + i] = 1
    put("perm", perm)
    inv = (np.float32(10000.0) ** (-np.arange(32, dtype=np.float32) / np.float32(32))).astype(np.float32)
    pos = [np.arange(256) // 64, np.arange(256) % 64]
    ang = np.stack([(pos[d // 64].astype(np.float32) * inv[d % 32]).astype(np.float32) for d in range(128)])
    put("cos", np.cos(ang.astype(np.float64)))
    put("sin", np.sin(ang.astype(np.float64)))
    put("maskd", np.where(np.arange(128)[None] <= p, 0, NEG))
    put("maskf", np.concatenate([np.where(p + 128 * k <= f, 0, NEG) for k in range(2)], 1))
    put("maskb", np.concatenate([np.where(p + 128 * k >= f, 0, NEG) for k in range(2)], 1))
    put("sel8", np.kron(np.eye(8), np.ones((1, 128))))
    cols = np.zeros((128, 8))
    cols[:, 0] = EPS
    cols[0:64, 1] = 0.125
    cols[64:, 2] = 0.125
    cols[1:, 3] = 1
    put("cols", cols)
    th = np.pi * (2 * np.arange(256) + 1) / 512
    t = np.arange(256)
    fwd = np.concatenate([np.cos(np.outer(t, th)), -np.sin(np.outer(t, th))], 1)
    put("dft", np.concatenate([fwd[:128], fwd[128:]], 1))
    bwd = np.concatenate([np.cos(np.outer(th, t)), -np.sin(np.outer(th, t))], 0) / 256
    put("idft", np.concatenate([bwd[128 * i:128 * i + 128] for i in range(4)], 1))
    n_ = 256
    tt = np.linspace(0.0, 1.0, n_, dtype=np.float32)[:, None]
    bands = np.linspace(1e-4, 15, 16, dtype=np.float32)
    a = (np.float32(2 * math.pi / n_) * np.arange(n_, dtype=np.float32)[:, None] * bands).astype(np.float32)
    z = np.concatenate([tt, np.cos(a), -np.sin(a)], 1)
    put("zT", z.T)
    lo, hi = math.log(1e-2) / 1.5, math.log(1e-2) / 0.3
    deltas = np.linspace(lo, hi, 1024, dtype=np.float32)
    decay = np.exp((-tt * np.abs(deltas)).astype(np.float32).astype(np.float64))
    dec = decay.reshape(2, 128, 1024).transpose(1, 0, 2)
    return c.astype(np.float32), np.ascontiguousarray(dec.astype(np.float32))


def columns(v):
    v = np.asarray(v)
    return v.reshape(-1, 128).T


def padded(v):
    o = np.zeros((128, 1), v.dtype)
    o[:v.size, 0] = v.reshape(-1)
    return o


def lay_out(i):
    a = {k: np.asarray(v) for k, v in i.items()}
    fT = lambda x: np.ascontiguousarray(x.reshape(256, 8, 128).transpose(2, 1, 0))
    gb = a["o_gate_b_2"][0].reshape(4, 8)
    gtb = np.zeros((128, 1), gb.dtype)
    for g in range(4):
        gtb[32 * g:32 * g + 8, 0] = gb[g]
    parts = {
        "ng": columns(a["norm_gains"]), "lbl": columns(a["hgrn_lb_logits"]), "hgn": columns(a["hgrn_norm"]),
        "rcw": columns(a["rg_conv_w"]), "rcb": columns(a["rg_conv_b"]), "rba": columns(a["rg_ba"]),
        "rbx": columns(a["rg_bx"]), "lam": columns(a["rg_lambda"]), "fxb": padded(a["fox_f_bias"]),
        "fcw": columns(a["ffn_conv_w"]), "fcb": columns(a["ffn_conv_b"]),
        "cc": np.stack([columns(a["c_2"]), columns(a["c_ctx_2"])], 2).reshape(128, 16),
        "bmod": np.repeat(columns(a["b_mod_2"]), 2, axis=1),
        "gpre": columns(a["g_pre_2"]), "gpost": columns(a["g_post_2"]),
        "ecw": columns(a["e_conv_w_2"]), "ecb": columns(a["e_conv_b_2"]),
        "fb1": padded(a["e_filt_b1_2"]), "ffr": padded(a["e_filt_freq_2"]), "fb2": padded(a["e_filt_b2_2"]),
        "hyb": columns(a["e_hy_bias_2"]), "qn": columns(a["e_q_norm_2"]), "kn": columns(a["e_k_norm_2"]),
        "ocw": columns(a["o_conv_w_2"]), "ocb": columns(a["o_conv_b_2"]), "gtb": gtb,
        "ohn": columns(a["o_head_norm_2"]),
    }
    off, n = param_layout()
    pr = np.zeros((128, n), np.float32)
    for k, v in parts.items():
        pr[:, off[k]:off[k] + v.shape[1]] = v
    ow = a["o_w_in_2"][0]
    gates = np.zeros((1024, 128), ow.dtype)
    for g in range(4):
        gates[:, 32 * g:32 * g + 8] = ow[:, 8192 + 8 * g:8192 + 8 * g + 8]
    od = a["odd_w_in"][0]
    od = np.concatenate([od, np.zeros((1024, 3200 - od.shape[1]), od.dtype)], 1)
    mats = {
        "even_w_in": a["even_w_in"][0], "even_w_out": a["even_w_out"][0], "odd_w_in": od,
        "odd_w_out": a["odd_w_out"][0], "e_w_in": a["e_w_in_2"][0], "e_w_out": a["e_w_out_2"][0],
        "o_w_in": np.concatenate([ow[:, 0:8192], gates], 1), "o_w_out": a["o_w_out_2"][0],
    }
    for l in range(2):
        mats[f"ffn_up{l}"] = a["ffn_w_up"][l]
        mats[f"ffn_down{l}"] = a["ffn_w_down"][l]
        mats[f"w_mod{l}"] = a["w_mod_2"][l]
    plan = weight_plan()
    nchunk = (len(plan) + TPC - 1) // TPC
    ws = np.zeros((nchunk, 128, TPC, 128), np.float32)
    for t, (name, k, m) in enumerate(plan):
        ws[t // TPC, :, t % TPC, :] = mats[name][128 * k:128 * k + 128, 128 * m:128 * m + 128]
    ws = ws.reshape(nchunk, 128, TPC * 128)
    rgw = np.zeros((128, 8, 128), np.float32)
    for g, name in enumerate(("rg_wa", "rg_wx")):
        for b in range(8):
            o = 64 * (b % 2)
            rgw[o:o + 64, 4 * g + b // 2, o:o + 64] = a[name][0, b]
    fw = np.zeros((64, 2176), np.float32)
    fw[0:33, 0:64] = a["e_filt_w1_2"][0]
    fw[:, 64:128] = a["e_filt_w2_2"][0]
    fw[:, 128:] = a["e_filt_w3_2"][0]
    cs, dec = constants()
    return {"xT": fT(a["x"]), "ctxT": fT(a["ctx_2"]), "ws": ws, "pr": pr, "cs": cs, "rgw": rgw, "fw": fw, "dec": dec}


def kernel(**inputs):
    import concourse.bacc as _bacc
    from concourse.bass_utils import run_bass_kernel_spmd as _run

    arrays = lay_out(inputs)
    nc = _bacc.Bacc("TRN2", target_bir_lowering=False, num_devices=1)
    args = [nc.dram_tensor(k, v.shape, mybir.dt.from_np(v.dtype), kind="ExternalInput").ap()
            for k, v in arrays.items()]
    out = nc.dram_tensor("outT", (128, 8, 256), F32, kind="ExternalOutput").ap()
    build_program(nc, *args, out)
    r = _run(nc, [arrays], core_ids=[0])
    return np.ascontiguousarray(r.results[0]["outT"].transpose(2, 1, 0).reshape(1, 256, 1024))
```

```python
from contextlib import ExitStack
import math

import numpy as np
import concourse.bass as bass
from concourse import mybir

F32 = mybir.dt.float32
F32R = mybir.dt.float32r
ALU = mybir.AluOpType
ACT = mybir.ActivationFunctionType
AXX = mybir.AxisListType.X

EPS = 1e-6
RAW = 4
SPL = 3
TPC = 8
NA = 13600
NEG = -1e30


def param_layout():
    sizes = [("ng", 64), ("lbl", 12), ("hgn", 4), ("rcw", 16), ("rcb", 4), ("rba", 4), ("rbx", 4), ("lam", 4),
             ("fxb", 1), ("fcw", 264), ("fcb", 88), ("cc", 16), ("bmod", 96), ("gpre", 32), ("gpost", 32),
             ("ecw", 72), ("ecb", 24), ("fb1", 1), ("ffr", 1), ("fb2", 1), ("hyb", 8), ("qn", 1), ("kn", 1),
             ("ocw", 48), ("ocb", 16), ("gtb", 1), ("ohn", 16)]
    at, out = 0, {}
    for name, n in sizes:
        out[name] = at
        at += n
    return out, at


def const_layout():
    sizes = [("ident", 128), ("ones", 256), ("perm", 128), ("cos", 256), ("sin", 256), ("trif", 128), ("trib", 128),
             ("cols", 8), ("dft", 1024), ("idft", 1024)]
    at, out = 0, {}
    for name, n in sizes:
        out[name] = (at, n)
        at += n
    return out, at


class Queue:

    def __init__(self, sem):
        self.sem, self.n, self.items, self.seen = sem, 0, [], {}

    def wait(self, *toks):
        for t in flat(toks):
            if self.seen.get(id(t[0]), 0) < t[1]:
                self.seen[id(t[0])] = t[1]
                self.items.append(("w", t[0], t[1]))

    def do(self, fn, *toks):
        self.wait(*toks)
        self.n += 1
        self.items.append(("i", fn, self.sem, 1))
        return (self.sem, self.n)

    def plain(self, fn, *toks):
        self.wait(*toks)
        self.items.append(("i", fn, None, 0))

    def dma(self, fn, sem, *toks):
        self.wait(*toks)
        self.items.append(("i", fn, sem, 16))

    def emit(self, eng):
        for it in self.items:
            if it[0] == "w":
                eng.wait_ge(it[1], it[2])
            else:
                ins = it[1](eng)
                if it[2] is not None:
                    ins.then_inc(it[2], it[3])


def flat(toks):
    for t in toks:
        if t is None:
            continue
        if isinstance(t, list):
            yield from flat(t)
        else:
            yield t


class Slots:

    def __init__(self, bufs):
        self.bufs, self.free, self.idle = bufs, [None] * len(bufs), list(range(len(bufs)))

    def take(self):
        s = self.idle.pop(0)
        return s, self.bufs[s], self.free[s]

    def give(self, s, *toks):
        assert s not in self.idle
        self.idle.append(s)
        self.free[s] = list(toks)


def pipeline(gens, oldest=False):
    active = []
    for g in gens:
        active.insert(len(active) if oldest else 0, g)
        active = [x for x in active if next(x, "end") != "end"]
    while active:
        active = [x for x in active if next(x, "end") != "end"]


def record(bufs, sems, dram, kinds):
    X, RH, RAWB, WH, WL, PR, CS, TMPS, RBS, SM, MODB, AR, PSUM = bufs
    s_pe, s_act, s_dve, s_pool, s_w, s_cs, s_pr, s_x, s_rg, s_fw, s_dec, s_out = sems
    xT, ctxT, ws, pr, cs, rgw, fw, dec, out = dram
    POFF, PN = param_layout()
    COFF, CN = const_layout()
    pe, act, dve, pool = Queue(s_pe), Queue(s_act), Queue(s_dve), Queue(s_pool)
    extra = []
    ps = Slots([b[:, :] for b in PSUM])
    tmp = Slots([t[:, :] for t in TMPS])
    rbs = Slots([t[:, :] for t in RBS])

    def C(name, rows=128):
        a, n = COFF[name]
        return CS[0:rows, a:a + n]

    def P(name, j=0, n=1):
        a = POFF[name] + j
        return PR[:, a:a + n]

    ident, ones = C("ident"), C("ones")[:, 0:128]
    CCOL = COFF["cols"][0]
    c_eps, c_even, c_odd, c_m0 = (CS[:, CCOL + i:CCOL + i + 1] for i in range(4))
    T_CS, T_PR, T_X, T_XC = (s_cs, 16), (s_pr, 16), (s_x, 16), (s_x, 32)
    ar_free = [None]

    def shaped(base, off, *shape):
        n = 1
        for d in shape:
            n *= d
        v = base[:, off:off + n]
        if len(shape) == 1:
            return v
        if len(shape) == 2:
            return v.rearrange("p (a b) -> p a b", a=shape[0])
        return v.rearrange("p (a b c) -> p a b c", a=shape[0], b=shape[1])

    def view(off, *shape):
        assert off + int(np.prod(shape)) <= NA, (off, shape)
        return shaped(AR, off, *shape)

    def rview(off, *shape):
        n = int(np.prod(shape))
        assert off + 2 * n <= 16384
        return shaped(RH, off, *shape), shaped(RH, off + n, *shape)

    def A(out_, in_, func, *w, bias=None, scale=1.0, accum=None):
        kw = {"scale": scale}
        if bias is not None:
            kw["bias"] = bias
        if accum is not None:
            kw["accum_out"] = accum
        return act.do(lambda e: e.activation(out_, in_, func, **kw), *w)

    def TS(out_, in_, s1, s2, o0, o1, *w, q=None):
        q = q or dve
        if o1 is None:
            return q.do(lambda e: e.tensor_scalar(out_, in_, s1, None, o0), *w)
        return q.do(lambda e: e.tensor_scalar(out_, in_, s1, s2, o0, o1), *w)

    def TT(out_, a, b, op, *w, q=None):
        return (q or dve).do(lambda e: e.tensor_tensor(out_, a, b, op), *w)

    def STT(out_, a, s, b, o0, o1, *w):
        return dve.do(lambda e: e.scalar_tensor_tensor(out=out_, in0=a, scalar=s, in1=b, op0=o0, op1=o1), *w)

    def CP(out_, in_, *w, q=None):
        return (q or dve).do(lambda e: e.tensor_copy(out_, in_), *w)

    def REC(out_, in_, *w):
        return dve.do(lambda e: e.reciprocal(out_, in_), *w)

    def SCAN(out_, a, b, init, o0, o1, *w):
        return dve.do(lambda e: e.tensor_tensor_scan(out_, a, b, init, o0, o1), *w)

    def tables(name):
        act.plain(lambda e: e.preload_act_table_set(name))

    def MM(groups, *w):
        pe.wait(*w)
        n = len(groups)
        for i, (o, l, r) in enumerate(groups):
            def f(e, o=o, l=l, r=r, i=i):
                return e.matmul(o, l, r, start=(i == 0), stop=(i == n - 1))
            if i < n - 1:
                pe.plain(f)
            else:
                return pe.do(f)

    def TR(o, a, rows, *w):
        return pe.do(lambda e: e.transpose(o, a, ident[0:rows, 0:rows]), *w)

    def split(hl, x, tok, *w):
        hi, lo = hl
        t1 = A(hi, x, ACT.Copy, tok, *w)
        t2 = TT(lo, x, hi.bitcast(F32), ALU.subtract, t1, tok)
        return [t1, t2]

    def everything_read():
        return [(q.sem, q.n) for q in (pe, act, dve, pool) if q.n]

    plan, mine = [], []
    raw_free, spl_free, spl_tok = {}, {}, {}

    def split_chunk(c):
        raw = RAWB[:, c % RAW, :]
        hi, lo = WH[:, c % SPL, :], WL[:, c % SPL, :]
        got = (s_w[c % RAW], 16 * (c // RAW + 1))
        prev = max([x for x in spl_tok if x <= c - SPL and x % SPL == c % SPL], default=None)
        fr = spl_free[prev] if prev is not None else None
        t1 = act.do(lambda e: e.copy(hi, raw), got, fr)
        t2 = TT(lo, raw, hi.bitcast(F32), ALU.subtract, t1, got)
        raw_free[c] = [t1, t2]
        spl_tok[c] = [t1, t2]

    def fetch(kind, name, k, m, n):
        t = len(plan)
        c, o = t // TPC, t % TPC
        if o == 0:
            mine.append(kind)
            for d in range(SPL):
                if c + d < len(kinds) and kinds[c + d] and c + d not in spl_tok:
                    split_chunk(c + d)
                elif not kinds and d == 0 and kind:
                    split_chunk(c)
        assert mine[c] == kind and o + n <= TPC
        plan.extend((name, k, m + i) for i in range(n))
        sl = slice(o * 128, (o + n) * 128)
        end = c if o + n == TPC else None
        if kind:
            pe.wait(spl_tok[c])
            return (WH[:, c % SPL, sl], WL[:, c % SPL, sl]), end
        pe.wait((s_w[c % RAW], 16 * (c // RAW + 1)))
        return RAWB[:, c % RAW, sl], end

    def fetched(end, tok):
        if end is not None:
            if mine[end]:
                spl_free[end] = tok
            else:
                raw_free[end] = tok

    def mm3(o, l, r, first, last, want):
        (lh, ll), (rh, rl) = l, r
        for i, (a, b) in enumerate(((lh, rh), (lh, rl), (ll, rh))):
            def f(e, a=a, b=b, i=i):
                return e.matmul(o, a, b, start=(first and i == 0), stop=(last and i == 2))
            if i < 2 or not want:
                pe.plain(f)
            else:
                return pe.do(f)

    def proj(name, kt, m, rhs, N, w, k0=0):
        s, b, fr = ps.take()
        pe.wait(fr)
        for k in range(kt):
            wt, end = fetch(True, name, k0 + k, m, 1)
            pe.wait(w[k])
            tok = mm3(b[:, 0:N], wt, rhs(k), k == 0, k == kt - 1, end is not None or k == kt - 1)
            fetched(end, tok)
        step_tail()
        return s, b, tok

    def proj_tok(name, kt, m, lhs, nb, width, w):
        got = []
        for n in range(nb):
            s, b, fr = ps.take()
            pe.wait(fr, w[0:kt])
            got.append((s, b))
        toks = []
        for k in range(kt):
            wt, end = fetch(True, name, k, m, width // 128)
            for n in range(nb):
                last = k == kt - 1
                tok = mm3(got[n][1][:, 0:width], lhs(k, n), wt, k == 0, last, last or (end is not None and n == nb - 1))
                if last:
                    toks.append(tok)
            fetched(end, tok)
        return [(s, b, t) for (s, b), t in zip(got, toks)]

    MODC, MC, SCC = MODB[:, 0:192], MODB[:, 192:256], MODB[:, 256:272]
    filler = {"l": 0, "c": 0, "t": None, "toks": [], "tails": []}

    def mod(l, j, seq):
        return MODC[:, l * 96 + 2 * j + seq:l * 96 + 2 * j + seq + 1]

    def fill(n=1):
        for _ in range(n):
            l, c = filler["l"], filler["c"]
            if l == 2:
                return
            if filler["t"] is None:
                t = A(SCC, P("cc", 0, 16), ACT.Sigmoid, T_PR)
                filler["t"] = TT(SCC, SCC, P("cc", 0, 16), ALU.mult, t)
            s, b, fr = ps.take()
            pe.wait(fr, filler["t"])
            for k in range(8):
                wt, end = fetch(False, f"w_mod{l}", k, 4 * c, 4)
                def f(e, wt=wt, k=k, b=b):
                    return e.matmul(b[0:2, :], SCC[:, 2 * k:2 * k + 2], wt, start=(k == 0), stop=(k == 7))
                if end is None and k < 7:
                    pe.plain(f)
                else:
                    t = pe.do(f)
                    fetched(end, t)
            filler["c"] += 1
            if filler["c"] == 6:
                filler["c"] = 0
                filler["l"] += 1
            filler["tails"].append(fill_tail(l, c, s, b, t))

    def fill_tail(l, c, s, b, t):
        q, row, tf = tmp.take()
        t = CP(row[0:2, :], b[0:2, :], t, tf)
        ps.give(s, t)
        yield
        s, b, fr = ps.take()
        for i in range(4):
            t = TR(b[:, 2 * i:2 * i + 2], row[0:2, 128 * i:128 * i + 128], 2, fr, t, T_CS)
        tmp.give(q, t)
        t = TT(MODC[:, 96 * l + 8 * c:96 * l + 8 * c + 8], b[:, 0:8], P("bmod", 48 * l + 8 * c, 8), ALU.add, t, T_PR)
        ps.give(s, t)
        filler["toks"].append(t)
        if c == 5:
            a = 96 * l
            t1 = STT(MC[:, 32 * l:32 * l + 16], MODC[:, a + 16:a + 32], 1.0, P("gpre", 16 * l, 16), ALU.add, ALU.mult,
                     filler["toks"])
            t2 = TT(MC[:, 32 * l + 16:32 * l + 32], MODC[:, a + 32:a + 48], P("gpost", 16 * l, 16), ALU.mult)
            filler["toks"] += [t1, t2]
        yield

    def step_tail():
        if filler["tails"] and next(filler["tails"][0], "end") == "end":
            filler["tails"].pop(0)

    def fill_all(l):
        while filler["l"] <= l:
            fill()
        while filler["tails"]:
            step_tail()

    def rstd(b, s, N, n, tok, fillers=0):
        rs, r, rfr = rbs.take()
        tables("natural_log_exp_and_others")
        q, v, f = tmp.take()
        r, v = r[:, 0:N], v[:, 0:N]
        t = A(r, b[:, 0:N], ACT.Ln, tok, rfr, bias=c_eps, scale=1.0 / n)
        tv = TS(v, b[:, 0:N], 1.0 / n, EPS, ALU.mult, ALU.add, t, f)
        ps.give(s, tv)
        t = A(r, r, ACT.Exp, t, scale=-0.5)
        t = STT(v, v, -0.5, r, ALU.mult, ALU.mult, t, tv)
        t = TT(v, v, r, ALU.mult, t)
        t = STT(r, v, 1.5, r, ALU.add, ALU.mult, t)
        tmp.give(q, t)
        fill(fillers)
        return rs, r, t

    def square_sum(src, nb, N, toks, scale=1.0):
        s, b, fr = ps.take()
        for j in range(nb):
            q, x, f = tmp.take()
            t = A(x[:, 0:N], src(j), ACT.Square, toks[j], f, scale=scale)
            g = lambda e, j=j, x=x: e.matmul(b[:, 0:N], ones, x[:, 0:N], start=(j == 0), stop=(j == nb - 1))
            t = pe.do(g, t, fr, T_CS)
            tmp.give(q, t)
        return s, b, t

    xt = [[T_X, T_XC]] * 8

    def pre_norm(gains, N, hfree, shift=None, fillers=0, after=None):
        s, b, t = square_sum(lambda j: X[:, j, 0:N], 8, N, xt)
        rs, r, t = rstd(b, s, N, 1024, t, fillers)
        if after:
            after()
        HH = rview(0, 8, N)
        ht = [None] * 8

        def block(j):
            q, x, f = tmp.take()
            last = []
            for seq in range(N // 256):
                c = slice(256 * seq, 256 * seq + 256)
                t1 = STT(x[:, c], X[:, j, c], gains(j, seq), r[:, c], ALU.mult, ALU.mult, t, xt[j], T_PR, f, filler["toks"])
                last.append(A(x[:, c], x[:, c], ACT.Identity, t1, bias=shift(j, seq)) if shift else t1)
            hi, lo = HH[0][:, j, :], HH[1][:, j, :]
            th = A(hi, x[:, 0:N], ACT.Copy, last, hfree)
            yield
            tl = TT(lo, x[:, 0:N], hi.bitcast(F32), ALU.subtract, th, last, hfree, q=pool if j % 3 == 1 else dve)
            ht[j] = [th, tl]
            tmp.give(q, ht[j])

        pipeline(block(j) for j in range(8))
        rbs.give(rs, ht)
        return (lambda k: (HH[0][:, k, :], HH[1][:, k, :])), ht

    def out_and_norm(parts, MIX, N, gains, mfree, fillers=0):
        prev = None
        mt = [None] * 8
        for i, (name, kt, k0, rhs, st) in enumerate(parts):
            last = i == len(parts) - 1
            if last:
                ss, sb_, sf = ps.take()
                sq = []

                def add_square(j):
                    q, x, t = sq[j]
                    g = lambda e, x=x: e.matmul(sb_[:, 0:N], ones, x[:, 0:N], start=(j == 0), stop=(j == 7))
                    t = pe.do(g, t, sf)
                    tmp.give(q, t)
                    return t
            for m in range(8):
                s, b, t = proj(name, kt, m, rhs, N, st, k0)
                if i == 0:
                    mt[m] = A(MIX[:, m, :], b[:, 0:N], ACT.Copy, t, mfree)
                else:
                    mt[m] = TT(MIX[:, m, :], MIX[:, m, :], b[:, 0:N], ALU.add, t, mt[m])
                ps.give(s, mt[m])
                if last:
                    q, x, f = tmp.take()
                    sq.append((q, x, A(x[:, 0:N], MIX[:, m, :], ACT.Square, mt[m], f)))
                    if m:
                        add_square(m - 1)
        t = add_square(7)
        rs, r, t = rstd(sb_, ss, N, 1024, t, fillers)
        for j in range(8):
            both = []
            for seq in range(N // 256):
                c = slice(256 * seq, 256 * seq + 256)
                t1 = STT(MIX[:, j, c], MIX[:, j, c], gains(j, seq), r[:, c], ALU.mult, ALU.mult, t, mt[j])
                both.append(TT(X[:, j, c], X[:, j, c], MIX[:, j, c], ALU.add, t1, T_XC, q=pool if j % 2 else dve))
            xt[j] = both
        rbs.give(rs, t1)

    def log1p_exp_neg_abs(dst, x, a, b, tok):
        t = A(a, x, ACT.Abs, tok)
        t = A(a, a, ACT.Exp, t, scale=-1.0)
        t = TS(b, a, 2.0, None, ALU.add, None, t)
        t = REC(b, b, t)
        t = TT(a, a, b, ALU.mult, t)
        t = TT(b, a, a, ALU.mult, t)
        t = TS(dst, b, 1.0 / 19, None, ALU.mult, None, t)
        for n in (17, 15, 13, 11, 9, 7, 5, 3):
            t = STT(dst, dst, 1.0 / n, b, ALU.add, ALU.mult, t)
        t = STT(dst, dst, 1.0, a, ALU.add, ALU.mult, t)
        return TS(dst, dst, 2.0, None, ALU.mult, None, t)

    def log_sigmoid(dst, x, a, b, tok):
        t = log1p_exp_neg_abs(dst, x, a, b, tok)
        return STT(dst, x, 0.0, dst, ALU.min, ALU.subtract, t)

    def load(dst, src, sm, *toks):
        extra.append((len(plan) // TPC + RAW - 1 if plan else 0, dst, src, sm, toks))

    load(X[:, :, 0:256], xT, s_x)
    load(CS[:, :], cs, s_cs)
    load(PR[:, :], pr, s_pr)
    load(X[:, :, 256:512], ctxT, s_x)

    def conv_causal(b, tok, s, dst, K, taps, bias, *w):
        t = A(dst, b[:, 0:256], ACT.Identity, tok, *w, bias=bias, scale=taps(K - 1))
        for d in range(1, K):
            t = STT(dst[:, d:256], b[:, 0:256 - d], taps(K - 1 - d), dst[:, d:256], ALU.mult, ALU.add, t)
        ps.give(s, t)
        return t

    def operand(hl):
        return lambda k: (hl[0][:, k, :], hl[1][:, k, :])

    def blocks(rhs):
        return lambda k, n: tuple(v[:, n * 128:n * 128 + 128] for v in rhs(k))

    def ffn(l, fillers=0):
        free = everything_read()
        hid = rview(4096, 22, 256)
        MIX = view(0, 8, 256)
        GV = Slots([view(2048 + 256 * i, 256) for i in range(8)])
        rhs, ht = pre_norm(lambda j, s: P("ng", (l * 4 + 2) * 8 + j), 256, free, fillers=fillers)
        hidt = []

        def unit(j):
            pair = []
            for half in range(2):
                q, g, f = GV.take()
                m = j + 22 * half
                s, b, t = proj(f"ffn_up{l}", 8, m, rhs, 256, ht)
                t = conv_causal(b, t, s, g, 3, lambda k: P("fcw", (l * 3 + k) * 44 + m), P("fcb", l * 44 + m), f, free)
                pair.append((q, g, t))
            yield
            (qg, g, tg), (qv, v, tv) = pair
            tg = A(g, g, ACT.Gelu_apprx_tanh, tg)
            t = TT(g, g, v, ALU.mult, tg, tv, q=pool)
            GV.give(qv, t)
            yield
            t = split((hid[0][:, j, :], hid[1][:, j, :]), g, t, free)
            GV.give(qg, t)
            hidt.append(t)

        pipeline(unit(j) for j in range(22))
        out_and_norm([(f"ffn_down{l}", 22, 0, operand(hid), hidt)], MIX, 256, lambda j, s: P("ng", (l * 4 + 3) * 8 + j),
                     free, fillers)

    def layer_even():
        E1, Qb, Gb = view(0, 4, 256), view(1024, 4, 256), view(2048, 4, 256)
        Fb = E1
        Bc, E2, E3 = (view(3072 + 1024 * i, 4, 256) for i in range(3))
        Vt = view(6144, 2, 512)
        KH = view(7168, 4, 256)
        SC = view(8192, 4, 2, 128)
        KT = view(9216, 4, 2, 128)
        SS = view(10240, 2, 3 * 128)
        XF = view(11008, 4, 256)
        RGW = view(12032, 8, 128)
        OH = Slots([view(13056 + 256 * i, 256) for i in range(2)])
        Y = rview(4096, 8, 256)
        MIX = view(4096, 8, 256)
        lb, oml = SM[:, 0:4], SM[:, 4:8]
        load(RGW, rgw, s_rg)
        zt = dve.do(lambda e: e.memset(SC[:, :, :, :], 0.0))
        L = P("lbl", 0, 12)
        m_, e_, d_ = SM[:, 8:12], SM[:, 12:24], SM[:, 24:28]
        t = TT(m_, L[:, 0:4], L[:, 4:8], ALU.max, T_PR)
        t = TT(m_, m_, L[:, 8:12], ALU.max, t)
        for r in range(3):
            t1 = TT(e_[:, 4 * r:4 * r + 4], L[:, 4 * r:4 * r + 4], m_, ALU.subtract, t)
        t = A(e_, e_, ACT.Exp, t1)
        t = TT(d_, e_[:, 0:4], e_[:, 4:8], ALU.add, t)
        t = TT(d_, d_, e_[:, 8:12], ALU.add, t)
        t = REC(d_, d_, t)
        t = TT(lb, e_[:, 0:4], d_, ALU.mult, t)
        lbt = TS(oml, lb, -1.0, 1.0, ALU.mult, ALU.add, t)
        c8, nc8, sa, sb_ = SM[:, 32:36], SM[:, 36:40], SM[:, 40:44], SM[:, 44:48]
        lam = P("lam", 0, 4)
        t = log1p_exp_neg_abs(c8, lam, sa, sb_, T_PR)
        t = TS(sa, lam, -1.0, 0.0, ALU.mult, ALU.max, t)
        t = TT(c8, c8, sa, ALU.add, t)
        t = TS(c8, c8, 8.0, None, ALU.mult, None, t)
        c8t = TS(nc8, c8, -1.0, None, ALU.mult, None, t)

        rhs, ht = pre_norm(lambda j, s: P("ng", j), 256, None, fillers=1)
        ft, qt, gt = [], [], []
        for h in range(4):
            s, b, t = proj("even_w_in", 8, 4 + h, rhs, 256, ht)
            t = A(Fb[:, h, :], b[:, 0:256], ACT.Sigmoid, t)
            ps.give(s, t)
            ft.append(TS(Fb[:, h, :], Fb[:, h, :], oml[:, h:h + 1], lb[:, h:h + 1], ALU.mult, ALU.add, t, lbt))
        for h in range(4):
            s, b, t = proj("even_w_in", 8, h, rhs, 256, ht)
            t1 = A(Qb[:, h, :], b[:, 0:256], ACT.Sigmoid, t)
            t = TT(Qb[:, h, :], Qb[:, h, :], b[:, 0:256], ALU.mult, t1)
            ps.give(s, t)
            qt.append(t)
        for h in range(4):
            s, b, t = proj("even_w_in", 8, 12 + h, rhs, 256, ht)
            t = A(Gb[:, h, :], b[:, 0:256], ACT.Sigmoid, t)
            ps.give(s, t)
            gt.append(t)
        tables("natural_log_exp_and_others")
        kt_, bt, lt = [], [], []
        for h in range(4):
            kt_.append(TS(KH[:, h, :], Fb[:, h, :], -1.0, 1.0, ALU.mult, ALU.add, ft[h]))
            lt.append(A(Fb[:, h, :], Fb[:, h, :], ACT.Ln, ft[h], kt_[h]))
        for h in range(4):
            for n in range(4):
                c = slice(64 * n, 64 * n + 64)
                t1 = SCAN(Bc[:, h, c], C("ones")[:, 0:64], Fb[:, h, c], 0.0, ALU.mult, ALU.add, lt[h], T_CS)
            bt.append(t1)
        vt = []
        for n, (s, b, t) in enumerate(proj_tok("even_w_in", 8, 8, blocks(rhs), 2, 512, ht)):
            t = A(Vt[:, n, :], b[:, 0:512], ACT.Copy, t)
            ps.give(s, t)
            vt.append(t)
        qd, kd, kl, e1t = [], [], [], []
        for h in range(4):
            t1 = A(E1[:, h, :], Bc[:, h, :], ACT.Exp, bt[h])
            t2 = A(E2[:, h, :], Bc[:, h, :], ACT.Exp, bt[h], scale=-1.0)
            for n in range(4):
                c = slice(64 * n, 64 * n + 64)
                t3 = A(E3[:, h, c], Bc[:, h, c], ACT.Exp, bt[h], scale=-1.0,
                       bias=Bc[:, h, 64 * n + 63:64 * n + 64])
            e1t.append(t1)
            qd.append(TT(Qb[:, h, :], Qb[:, h, :], E1[:, h, :], ALU.mult, t1, qt[h]))
            kd.append(TT(E2[:, h, :], E2[:, h, :], KH[:, h, :], ALU.mult, t2, kt_[h]))
            kl.append(TT(E3[:, h, :], E3[:, h, :], KH[:, h, :], ALU.mult, t3, kt_[h]))
        xft = []
        for j in range(4):
            s, b, t = proj("even_w_in", 8, 16 + j, rhs, 256, ht)
            xft.append(conv_causal(b, t, s, XF[:, j, :], 4, lambda k, j=j: P("rcw", 4 * k + j), P("rcb", j)))
        yt = [None] * 8
        ssr = Slots([0, 1])

        def head(h):
            sct, ktt = [], []
            for p in range(2):
                s, b, fr = ps.take()
                for u in range(2):
                    c = slice(128 * p + 64 * u, 128 * p + 64 * u + 64)
                    r = slice(64 * u, 64 * u + 64)
                    t = MM([(b[r, r], E2[:, h, c], Qb[:, h, c])], fr, kd[h], qd[h])
                    t = A(SC[r, h, p, r], b[r, r], ACT.Copy, t, zt)
                ps.give(s, t)
                sc = SC[:, h, p, :]
                sct.append(pool.do(lambda e, sc=sc: e.affine_select(
                    out=sc, in_=sc, compare_op=ALU.is_ge, fill=0.0, base=0, pattern=[[1, 128]],
                    channel_multiplier=-1), t))
                s, b, fr = ps.take()
                t = TR(b[:, 0:128], E3[:, h, 128 * p:128 * p + 128], 128, fr, kl[h], T_CS)
                t = CP(KT[:, h, p, :], b[:, 0:128], t)
                ps.give(s, t)
                ktt.append(t)
            yield
            prev, stt = None, []
            sr, u_, sfr = ssr.take()
            for n in range(3):
                p, r = n // 2, slice(64 * (n % 2), 64 * (n % 2) + 64)
                s, b, fr = ps.take()
                t = MM([(b[:, 0:128], KT[r, h, p, :], Vt[r, p, 128 * h:128 * h + 128])], fr, ktt, vt)
                o = SS[:, u_, 128 * n:128 * n + 128]
                if n == 0:
                    t = CP(o, b[:, 0:128], t, sfr)
                else:
                    t = STT(o, SS[:, u_, 128 * n - 128:128 * n], E1[:, h, 64 * n + 63:64 * n + 64], b[:, 0:128],
                            ALU.mult, ALU.add, t, prev, e1t[h])
                ps.give(s, t)
                prev = t
                stt.append(t)
            yield
            s, b, fr = ps.take()
            for p in range(2):
                g = [(b[:, 128 * p:128 * p + 128], Vt[:, p, 128 * h:128 * h + 128], SC[:, h, p, :])]
                for n in (2 * p, 2 * p + 1):
                    if n:
                        g.append((b[:, 64 * n:64 * n + 64], SS[:, u_, 128 * (n - 1):128 * n],
                                  Qb[:, h, 64 * n:64 * n + 64]))
                t = MM(g, fr, sct, vt, stt, qd[h])
            ssr.give(sr, t)
            q, o, f = OH.take()
            to = CP(o, b[:, 0:256], t, f)
            ps.give(s, to)
            yield
            s, b, t = square_sum(lambda j: o, 1, 256, [to])
            rs, r, t = rstd(b, s, 256, 128, t)
            t = STT(o, o, P("hgn", h), r, ALU.mult, ALU.mult, t)
            rbs.give(rs, t)
            t = TT(o, o, Gb[:, h, :], ALU.mult, t, gt[h])
            yt[h] = split((Y[0][:, h, :], Y[1][:, h, :]), o, t)
            OH.give(q, yt[h])

        pipeline([head(0), head(1), head(2), head(3)])
        free = everything_read()
        Rr, Ii, Tt, Aa = E2, E3, KH, Bc
        rit = []
        for j in range(4):
            pair = []
            for g, (dst, bn) in enumerate(((Rr, "rba"), (Ii, "rbx"))):
                s, b, fr = ps.take()
                t = MM([(b[:, 0:256], RGW[:, 4 * g + j, :], XF[:, j, :])], fr, xft[j], (s_rg, 16))
                t = A(dst[:, j, :], b[:, 0:256], ACT.Sigmoid, t, free, bias=P(bn, j))
                ps.give(s, t)
                pair.append(t)
            rit.append(pair)
        yg = []
        for j in range(4):
            s, b, t = proj("even_w_in", 8, 20 + j, rhs, 256, ht)
            yg.append((s, b, t))
        at_ = []
        for j in range(4):
            t1 = A(Tt[:, j, :], Rr[:, j, :], ACT.Tanh, rit[j], scale=c8[:, j:j + 1])
            t2 = A(Aa[:, j, :], Rr[:, j, :], ACT.Exp, rit[j], c8t, scale=nc8[:, j:j + 1])
            at_.append((t1, t2))
        rt = []
        for j in range(4):
            t = TS(Rr[:, j, :], Tt[:, j, :], 1.0, None, ALU.add, None, at_[j][0], at_[j][1])
            t = REC(Rr[:, j, :], Rr[:, j, :], t)
            rt.append(STT(Rr[:, j, :], Rr[:, j, :], 2.0, Tt[:, j, :], ALU.mult, ALU.mult, t))
        rt = [A(Rr[:, j, :], Rr[:, j, :], ACT.Sqrt, rt[j]) for j in range(4)]
        fill(1)
        for j in range(4):
            t1 = TT(Ii[:, j, :], Ii[:, j, :], XF[:, j, :], ALU.mult, rit[j])
            t = TT(Rr[:, j, :], Rr[:, j, :], Ii[:, j, :], ALU.mult, rt[j], t1)
            t = SCAN(Ii[:, j, :], Aa[:, j, :], Rr[:, j, :], 0.0, ALU.mult, ALU.add, t, at_[j][1])
            s, b, tb = yg[j]
            q, tb_, tf = tmp.take()
            tg = A(tb_[:, 0:256], b[:, 0:256], ACT.Gelu_apprx_tanh, tb, tf)
            ps.give(s, tg)
            t = TT(Ii[:, j, :], Ii[:, j, :], tb_[:, 0:256], ALU.mult, t, tg)
            tmp.give(q, t)
            yt[4 + j] = split((Y[0][:, 4 + j, :], Y[1][:, 4 + j, :]), Ii[:, j, :], t)
        out_and_norm([("even_w_out", 8, 0, operand(Y), yt)], MIX, 256, lambda j, s: P("ng", 8 + j),
                     everything_read(), 1)

    smc = [0]
    smfree = [None] * 16

    def soft_first(s, b, t, end, scale, PP):
        i = smc[0] % 16
        smc[0] += 1
        nm, su, rs = (SM[:, 64 + 4 * i + k:64 + 4 * i + k + 1] for k in range(3))
        q, p, f = PP.take()
        t = dve.do(lambda e: e.tensor_reduce(nm, b[:, 0:end], AXX, ALU.max, negate=True), t, smfree[i])
        if scale != 1.0:
            t = TS(nm, nm, scale, None, ALU.mult, None, t)
        t = A(p[:, 0:end], b[:, 0:end], ACT.Exp, t, f, bias=nm, scale=scale, accum=su)
        ps.give(s, t)
        t = REC(rs, su, t)
        t = TS(p[:, 0:end], p[:, 0:end], rs, None, ALU.mult, None, t)
        smfree[i] = t
        return q, p, t

    def soft_turn(q, p, t, end, PP, pf, dst, on_act):
        s, b2, fr = ps.take()
        for k in range(end // 128):
            t = TR(b2[:, 128 * k:128 * k + 128], p[:, 128 * k:128 * k + 128], 128, fr, t)
        PP.give(q, t)
        t = A(dst, b2[:, 0:end], ACT.Copy, t, pf) if on_act else CP(dst, b2[:, 0:end], t, pf)
        ps.give(s, t)
        return t

    def layer_fox():
        free = everything_read()
        Vt = view(0, 2, 1024)
        Cc, Nc, La, Lb = (view(2048 + 256 * i, 256) for i in range(4))
        QK = Slots([tuple(view(3072 + 768 * i + 256 * k, 256) for k in range(3)) for i in range(2)])
        PP = Slots([view(4608 + 256 * i, 256) for i in range(6)])
        PT = Slots([view(6144 + 384 * i, 384) for i in range(4)])
        YS = Slots([view(7680 + 256 * i, 256) for i in range(3)])
        MIX = view(8448, 8, 256)
        Y = rview(4096, 8, 256)
        rhs, ht = pre_norm(lambda j, s: P("ng", 32 + j), 256, free, fillers=1)
        s, b, t = proj("odd_w_in", 8, 24, rhs, 256, ht)
        t = A(Nc, b[:, 0:256], ACT.Identity, t, free, bias=P("fxb"))
        ps.give(s, t)
        t = log_sigmoid(Cc, Nc, La, Lb, t)
        t = SCAN(La, C("ones"), Cc, 0.0, ALU.mult, ALU.add, t)
        t1 = CP(Cc, La, t)
        ct = TS(Nc, La, -1.0, None, ALU.mult, None, t, t1)
        vt = []
        for c in range(2):
            for n, (s, b, t) in enumerate(proj_tok("odd_w_in", 8, 16 + 4 * c, blocks(rhs), 2, 512, ht)):
                t = A(Vt[:, n, 512 * c:512 * c + 512], b[:, 0:512], ACT.Copy, t, free)
                ps.give(s, t)
                vt.append(t)
        yt = [None] * 8
        state = {}

        def qk(j):
            qq, (qe, qo, kk), f = QK.take()
            s, b, t = proj("odd_w_in", 8, j, rhs, 256, ht)
            t1 = TS(qe, b[:, 0:256], c_even, None, ALU.mult, None, t, f, free)
            t2 = TS(qo, b[:, 0:256], c_odd, None, ALU.mult, None, t)
            ps.give(s, t2)
            s, b, t = proj("odd_w_in", 8, 8 + j, rhs, 256, ht)
            t3 = A(kk, b[:, 0:256], ACT.Copy, t, f, free)
            ps.give(s, t3)
            state[j] = (qq, qe, qo, kk, [t1, t2, t3])

        def head(h):
            j, par = h // 2, h % 2
            if par == 0:
                qk(j)
            yield
            qq, qe, qo, kk, tq = state[j]
            Q = qo if par else qe
            sel = ident[:, h:h + 1]
            soft = []
            for qb in range(2):
                end = 128 * (qb + 1)
                s, b, fr = ps.take()
                t = MM([(b[:, 0:end], Q[:, 128 * qb:end], kk[:, 0:end]),
                        (b[:, 0:end], Cc[:, 128 * qb:end], sel.to_broadcast([128, end])),
                        (b[:, 0:end], sel.to_broadcast([128, 128]), Nc[:, 0:end]),
                        (b[:, 128 * qb:end], ident, C("trib"))], fr, tq, ct, T_CS)
                soft.append((soft_first(s, b, t, end, 1.0, PP), end))
            if par:
                QK.give(qq, t)
            yield
            qp, pt, pf = PT.take()
            ptt = [soft_turn(*x, end, PP, [pf, free], pt[:, end - 128:2 * end - 128], (h + i) % 2)
                   for i, (x, end) in enumerate(soft)]
            yield
            s, b, fr = ps.take()
            vc = slice(128 * j, 128 * j + 128)
            t = MM([(b[:, 0:256], Vt[:, 0, vc], pt[:, 0:256]),
                    (b[:, 128:256], Vt[:, 1, vc], pt[:, 256:384])], fr, ptt, vt)
            PT.give(qp, t)
            r = slice(64 * par, 64 * par + 64)
            if par == 0:
                q, y, f = YS.take()
                t = CP(y[r], b[r, 0:256], t, f, free)
                state[j, "y"] = (q, y, t)
                ps.give(s, t)
            else:
                q, y, t0 = state[j, "y"]
                t = CP(y[r], b[r, 0:256], t)
                ps.give(s, t)
                yt[j] = split((Y[0][:, j, :], Y[1][:, j, :]), y, [t0, t], free)
                YS.give(q, yt[j])

        pipeline(head(h) for h in range(16))
        out_and_norm([("odd_w_out", 8, 0, operand(Y), yt)], MIX, 256, lambda j, s: P("ng", 40 + j), free, 1)

    def two(ap):
        return ap.rearrange("p (s t) -> p s t", s=2)

    def conv3(b, tok, s, dst, N, taps, bias, *w):
        t = A(dst, b[:, 0:N], ACT.Identity, tok, *w, bias=bias, scale=taps(1))
        if N == 512:
            d, x = two(dst), two(b[:, 0:N])
            t = STT(d[:, :, 1:256], x[:, :, 0:255], taps(0), d[:, :, 1:256], ALU.mult, ALU.add, t)
            t = STT(d[:, :, 0:255], x[:, :, 1:256], taps(2), d[:, :, 0:255], ALU.mult, ALU.add, t)
        else:
            t = STT(dst[:, 1:256], b[:, 0:255], taps(0), dst[:, 1:256], ALU.mult, ALU.add, t)
            t = STT(dst[:, 0:255], b[:, 1:256], taps(2), dst[:, 0:255], ALU.mult, ALU.add, t)
        ps.give(s, t)
        return t

    def sine(dst, x, k, tok):
        big = 12582912.0
        t = TS(k, x, 1.0 / (2 * math.pi), big, ALU.mult, ALU.add, tok)
        t = TS(k, k, big, None, ALU.subtract, None, t)
        c1 = 6.28125
        t = STT(x, k, -c1, x, ALU.mult, ALU.add, t)
        t = STT(x, k, -(2 * math.pi - c1), x, ALU.mult, ALU.add, t)
        t = TS(x, x, 3.1415925, -3.1415925, ALU.min, ALU.max, t)
        return A(dst, x, ACT.Sin, t)

    def hyena_filter(free):
        HF = view(0, 4, 1024)
        FW, ZT = view(4096, 128), view(4224, 256)
        HD, HE, HK = (view(4480 + 256 * i, 256) for i in range(3))
        W3 = [view(5248 + 1024 * c, 2, 512) for c in range(2)]
        DC = [view(7296 + 1024 * c, 2, 512) for c in range(2)]
        HP, HM = view(9344, 2, 512), view(10368, 2, 512)
        NI = view(11392, 512)
        h1 = Slots([view(11904, 512), view(12416, 512)])
        R = slice(0, 64)
        load(FW[R, :], fw[:, 0:128], s_fw, free)
        load(ZT[R, :], fw[:, 2176:2432], s_fw, free)
        fww = fw[:, 128:2176].rearrange("p (a b) -> p a b", a=2)
        for c in range(2):
            load(W3[c][R], fww[:, :, 512 * c:512 * c + 512], s_fw, free)
            load(DC[c], dec[:, :, 512 * c:512 * c + 512], s_dec, free)
        s, b, fr = ps.take()
        t = MM([(b[R, 0:256], FW[R, 0:64], ZT[R])], fr, (s_fw, 64))
        t = TS(HD[R], b[R, 0:256], P("fb1")[R], P("ffr")[R], ALU.add, ALU.mult, t, free)
        ps.give(s, t)
        t = sine(HE[R], HD[R], HK[R], t)
        fill(1)
        s, b, fr = ps.take()
        t = MM([(b[R, 0:256], FW[R, 64:128], HE[R])], fr, t)
        t = TS(HD[R], b[R, 0:256], P("fb2")[R], P("ffr")[R], ALU.add, ALU.mult, t)
        ps.give(s, t)
        hd = sine(HE[R], HD[R], HK[R], t)
        fill(1)
        norm = []
        tD = None
        for c in range(2):
            cc = slice(512 * c, 512 * c + 512)
            sN, bN, frN = ps.take()
            hpm = []
            nm = []
            for n in range(2):
                q0, a0, f0 = h1.take()
                q1, a1, f1 = h1.take()
                s, b, fr = ps.take()
                t = MM([(b[:, :], HE[R, 128 * n:128 * n + 128], W3[c][R, 0, :])], fr, hd)
                t0 = TT(a0, b[:, :], DC[c][:, n, :], ALU.mult, t, f0, free, (s_dec, 32))
                ps.give(s, t0)
                s, b, fr = ps.take()
                t = MM([(b[:, :], HE[R, 128 * n:128 * n + 128], W3[c][R, 1, :])], fr)
                if n == 0:
                    t1 = STT(a1, b[:, :], c_m0, DC[c][:, n, :], ALU.mult, ALU.mult, t, f1, free)
                else:
                    t1 = TT(a1, b[:, :], DC[c][:, n, :], ALU.mult, t, f1, free)
                ps.give(s, t1)
                tp = TT(HP[:, n, :], a0, a1, ALU.add, t0, t1, free, tD)
                tm_ = TT(HM[:, n, :], a0, a1, ALU.subtract, t0, t1, free, tD)
                hpm += [tp, tm_]
                t0 = A(a0, a0, ACT.Abs, tp, tm_)
                t1 = A(a1, a1, ACT.Abs, tp, tm_)
                for i, (a, ta) in enumerate(((a0, t0), (a1, t1))):
                    g = lambda e, a=a, first=(n == 0 and i == 0), last=(n == 1 and i == 1), bN=bN: e.matmul(
                        bN[:, :], ones, a, start=first, stop=last)
                    t = pe.do(g, ta, frN)
                    h1.give(q1 if i else q0, t)
            tD = []
            nt = REC(NI, bN[:, :], t, free, norm)
            ps.give(sN, nt)
            for f in range(4):
                src = HP if f < 2 else HM
                s, b, fr = ps.take()
                t = MM([(b[:, :], C("dft")[:, 512 * n + 128 * f:512 * n + 128 * f + 128], src[:, n, :])
                        for n in range(2)], fr, hpm)
                tD.append(t)
                t = TT(HF[:, f, cc], b[:, :], NI, ALU.mult, t, nt, free)
                ps.give(s, t)
                norm.append(t)
        return HF, norm

    def layer_even2():
        fill_all(0)
        free = everything_read()
        got = {}

        def filt():
            got["f"] = hyena_filter(free)

        rhs, ht = pre_norm(lambda j, s: MC[:, 2 * j + s:2 * j + s + 1], 512, free, shift=lambda j, s: mod(0, j, s),
                           after=filt)
        HF, hft = got["f"]
        G = view(4096, 8, 512)
        free = everything_read()
        gt = [None] * 8

        def gunit(j):
            q0, a0, f0 = tmp.take()
            s, b, t = proj("e_w_in", 8, 8 + j, rhs, 512, ht)
            t0 = conv3(b, t, s, a0, 512, lambda k: P("ecw", 24 * k + 8 + j), P("ecb", 8 + j), f0)
            s, b, t = proj("e_w_in", 8, 16 + j, rhs, 512, ht)
            t1 = conv3(b, t, s, G[:, j, :], 512, lambda k: P("ecw", 24 * k + 16 + j), P("ecb", 16 + j), free)
            gt[j] = TT(G[:, j, :], G[:, j, :], a0, ALU.mult, t0, t1)
            tmp.give(q0, gt[j])
            yield

        pipeline(gunit(j) for j in range(8))
        GT = Slots([view(8192 + 1024 * i, 2, 512) for i in range(2)])
        SPC = Slots([view(10240 + 512 * i, 512) for i in range(6)])

        def cunit(seq, c):
            qg, g_, gf = GT.take()
            trs = []
            for tb in range(2):
                s, b, fr = ps.take()
                for jj in range(4):
                    t = TR(b[:, 128 * jj:128 * jj + 128],
                           G[:, 4 * c + jj, 256 * seq + 128 * tb:256 * seq + 128 * tb + 128], 128, fr, gt[4 * c + jj])
                t = A(g_[:, tb, :], b[:, :], ACT.Copy, t, gf, free)
                ps.give(s, t)
                trs.append(t)
            yield
            spec = []
            for fb in range(2):
                U = []
                for part in range(2):
                    f = 2 * part + fb
                    s, b, fr = ps.take()
                    t = MM([(b[:, :], C("dft")[:, 512 * n + 128 * f:512 * n + 128 * f + 128], g_[:, n, :])
                            for n in range(2)], fr, trs)
                    U.append((s, b, t))
                cc = slice(512 * c, 512 * c + 512)
                (sr, ur, tr_), (si, ui, ti_) = U
                hr, hi = HF[:, fb, cc], HF[:, 2 + fb, cc]
                qa, a_, fa = SPC.take()
                ring = tmp if fb else SPC
                qc_, c_, fc_ = ring.take()
                qb_, b_, fb_ = tmp.take()
                t0 = TT(a_, ur, hr, ALU.mult, tr_, fa, hft, free)
                t1 = TT(b_, ui, hi, ALU.mult, ti_, fb_)
                t2 = TT(a_, a_, b_, ALU.subtract, t0, t1)
                t3 = TT(c_, ur, hi, ALU.mult, tr_, fc_, free)
                ps.give(sr, t3)
                t4 = TT(b_, ui, hr, ALU.mult, ti_, t2)
                ps.give(si, t4)
                t5 = TT(c_, c_, b_, ALU.add, t3, t4)
                tmp.give(qb_, t5)
                spec.append((qa, a_, t2, qc_, c_, t5, ring))
            GT.give(qg, U[1][2])
            yield
            for jj in range(4):
                j = 4 * c + jj
                s, b, fr = ps.take()
                rows = [(spec[0][1], 0), (spec[1][1], 1), (spec[0][4], 2), (spec[1][4], 3)]
                t = MM([(b[:, 0:256], a[:, 128 * jj:128 * jj + 128], C("idft")[:, 256 * f:256 * f + 256])
                        for a, f in rows], fr, [x[2] for x in spec], [x[5] for x in spec])
                sc_ = slice(256 * seq, 256 * seq + 256)
                t1 = STT(G[:, j, sc_], G[:, j, sc_], P("hyb", j), b[:, 0:256], ALU.mult, ALU.add, t)
                ps.give(s, t1)
                ct_.append(t1)
            for x in spec:
                SPC.give(x[0], t)
                x[6].give(x[3], t)

        ct_ = []
        pipeline(cunit(seq, c) for c in range(2) for seq in range(2))
        free = everything_read()
        Q = view(0, 8, 512)
        KR = view(8192, 2, 512)
        VT = view(9216, 4, 256)
        PTb = Slots([view(10240 + 512 * i, 512) for i in range(6)])
        kt, qt, vt = [None] * 2, [None] * 8, []

        def qk_norm(dst, m, gain, toks, i):
            s, b, t = proj("e_w_in", 8, m, rhs, 512, ht)
            t0 = A(dst, b[:, :], ACT.Copy, t, free)
            ps.give(s, t0)
            q, x, f = tmp.take()
            t = A(x, dst, ACT.Square, t0, f)
            yield
            s, b, fr = ps.take()
            t = MM([(b[:, :], ones, x)], fr, t, T_CS)
            tmp.give(q, t)
            rs, r, t = rstd(b, s, 512, 128, t)
            t = STT(dst, dst, gain, r, ALU.mult, ALU.mult, t)
            rbs.give(rs, t)
            yield
            s, b, fr = ps.take()
            t1 = MM([(b[:, 0:256], C("perm"), dst[:, 0:256])], fr, t)
            q, tb, tf = tmp.take()
            t2 = TT(tb[:, 0:256], b[:, 0:256], C("sin"), ALU.mult, t1, tf)
            ps.give(s, t2)
            t3 = TT(dst[:, 0:256], dst[:, 0:256], C("cos"), ALU.mult, t, t1)
            t4 = TT(dst[:, 0:256], dst[:, 0:256], tb[:, 0:256], ALU.add, t2, t3)
            tmp.give(q, t4)
            toks[i] = t4

        def vproj():
            for n, (s, b, t) in enumerate(proj_tok("e_w_in", 8, 42, blocks(rhs), 4, 256, ht)):
                t = A(VT[:, n, :], b[:, 0:256], ACT.Copy, t, free)
                ps.give(s, t)
                vt.append(t)
            yield

        scale = 128 ** -0.5

        def att(h, seq):
            Qh, Kh = Q[:, h, :], KR[:, h // 4, :]
            vc = slice(128 * (h // 4), 128 * (h // 4) + 128)
            nk, k0 = (4, 0) if seq == 0 else (2, 2)
            soft = []
            for qb in range(2):
                qc = slice(256 * seq + 128 * qb, 256 * seq + 128 * qb + 128)
                s, b, fr = ps.take()
                t = MM([(b[:, 0:128 * nk], Qh[:, qc], Kh[:, 128 * k0:512])], fr, kt, qt[h])
                soft.append((soft_first(s, b, t, 128 * nk, scale, tmp), t))
            yield
            turned = []
            for i, (x, _) in enumerate(soft):
                qp, pt, pf = PTb.take()
                turned.append((qp, pt, soft_turn(*x, 128 * nk, tmp, [pf, free], pt[:, 0:128 * nk], i)))
            yield
            s, b, fr = ps.take()
            for qb, (qp, pt, tt) in enumerate(turned):
                t = MM([(b[:, 128 * qb:128 * qb + 128], VT[:, k0 + k, vc], pt[:, 128 * k:128 * k + 128])
                        for k in range(nk)], fr, tt, vt)
                PTb.give(qp, t)
            t1 = CP(Qh[:, 256 * seq:256 * seq + 256], b[:, 0:256], t)
            ps.give(s, t1)
            ot[h].append(t1)

        ot = [[] for _ in range(8)]
        Y = rview(8192, 8, 512)
        yt = [None] * 8

        def gated(src, m, j, toks):
            s, b, t = proj("e_w_in", 8, m, rhs, 512, ht)
            q, x, f = tmp.take()
            t1 = A(x, b[:, :], ACT.Tanh, t, f, scale=0.5)
            t = STT(x, x, 1.0, b[:, :], ALU.add, ALU.mult, t1, t)
            ps.give(s, t)
            t = STT(src, x, 0.5, src, ALU.mult, ALU.mult, t, toks)
            tmp.give(q, t)
            return split((Y[0][:, j, :], Y[1][:, j, :]), src, t, free)

        def agate(h):
            yt[h] = gated(Q[:, h, :], 44 + h, h, ot[h])
            yield

        units = [qk_norm(KR[:, 0, :], 40, P("kn"), kt, 0), qk_norm(KR[:, 1, :], 41, P("kn"), kt, 1), vproj()]
        units += [qk_norm(Q[:, h, :], 32 + h, P("qn"), qt, h) for h in range(2)]
        pipeline(units)
        units = []
        for h in range(8):
            units.append(att(h, 0))
            if h < 6:
                units.append(qk_norm(Q[:, h + 2, :], 34 + h, P("qn"), qt, h + 2))
            units.append(att(h, 1))
            if h > 1:
                units.append(agate(h - 2))
        pipeline(units)
        pipeline([agate(6), agate(7)])
        MIX = Q
        free2 = everything_read()
        y2t = [None] * 8

        def hy():
            for j in range(8):
                q, x, f = tmp.take()
                s, b, t = proj("e_w_in", 8, j, rhs, 512, ht)
                t = conv3(b, t, s, x, 512, lambda k: P("ecw", 24 * k + j), P("ecb", j), f)
                t = TT(G[:, j, :], G[:, j, :], x, ALU.mult, t, ct_)
                tmp.give(q, t)
                y2t[j] = gated(G[:, j, :], 24 + j, j, t)

        first_half("e_w_out", 8, 8, operand(Y), yt, MIX, 512, free2)
        free = everything_read()
        hy()
        second_half("e_w_out", 8, 0, operand(Y), y2t, MIX, 512, lambda j, s: MC[:, 16 + 2 * j + s:16 + 2 * j + s + 1])

    halves = {}

    def first_half(name, kt, k0, rhs, st, MIX, N, mfree):
        halves["m"] = []
        for m in range(8):
            s, b, t = proj(name, kt, m, rhs, N, st, k0)
            halves["m"].append(A(MIX[:, m, :], b[:, 0:N], ACT.Copy, t, mfree))
            ps.give(s, halves["m"][-1])

    def second_half(name, kt, k0, rhs, st, MIX, N, gains):
        mt = halves["m"]
        ss, sb_, sf = ps.take()
        sq = []

        def add_square(j):
            q, x, t = sq[j]
            t = pe.do(lambda e: e.matmul(sb_[:, 0:N], ones, x[:, 0:N], start=(j == 0), stop=(j == 7)), t, sf)
            tmp.give(q, t)
            return t
        for m in range(8):
            s, b, t = proj(name, kt, m, rhs, N, st, k0)
            mt[m] = TT(MIX[:, m, :], MIX[:, m, :], b[:, 0:N], ALU.add, t, mt[m])
            ps.give(s, mt[m])
            q, x, f = tmp.take()
            sq.append((q, x, A(x[:, 0:N], MIX[:, m, :], ACT.Square, mt[m], f)))
            if m:
                add_square(m - 1)
        t = add_square(7)
        rs, r, t = rstd(sb_, ss, N, 1024, t)
        for j in range(8):
            both_ = []
            for seq in range(N // 256):
                c = slice(256 * seq, 256 * seq + 256)
                t1 = STT(MIX[:, j, c], MIX[:, j, c], gains(j, seq), r[:, c], ALU.mult, ALU.mult, t, mt[j])
                both_.append(TT(X[:, j, c], X[:, j, c], MIX[:, j, c], ALU.add, t1, q=pool if j % 2 else dve))
            xt[j] = both_
        rbs.give(rs, t1)

    def layer_odd2():
        fill_all(1)
        free = everything_read()
        VT = [view(2048 * i, 4, 512) for i in range(2)]
        NM, EM = view(4096, 2, 256), view(4608, 2, 256)
        LI, LF, LB, LM = (view(5120 + 1024 * i, 2, 512) for i in range(4))
        AN = view(9216, 2, 512)
        GI, GF = view(10240, 512), view(10752, 512)
        a1, a2 = view(11264, 512), view(11776, 512)
        AC = SM[:, 256:320]
        rhs, ht = pre_norm(lambda j, s: MC[:, 32 + 2 * j + s:32 + 2 * j + s + 1], 512, free,
                           shift=lambda j, s: mod(1, j, s))
        rhs1 = lambda k: tuple(v[:, 0:256] for v in rhs(k))
        s, b, t = proj("o_w_in", 8, 64, rhs, 512, ht)
        tg = A(GI, b[:, :], ACT.Identity, t, free, bias=P("gtb"))
        ps.give(s, tg)
        vtt = {}

        def vproj(p, w):
            vtt[p] = []
            for n, (s, b, t) in enumerate(proj_tok("o_w_in", 8, 16 + 4 * p, blocks(rhs), 4, 512, ht)):
                t = A(VT[p % 2][:, n, :], b[:, :], ACT.Copy, t, free, w)
                ps.give(s, t)
                vtt[p].append(t)

        t = log_sigmoid(GF, GI, a1, a2, [tg, free])
        R8 = slice(0, 8)
        one8 = C("ones", 8)
        lat, cx = slice(0, 256), slice(256, 512)
        for d in range(2):
            for dst, src, row in ((LI, GI, 64 * d), (LF, GF, 64 * d + 32)):
                for o, c in ((0, cx), (256, lat)):
                    sv = src[row:row + 8, c]
                    if d:
                        sv = sv[:, ::-1]
                    t1 = CP(dst[R8, d, o:o + 256], sv, t, tg, free)
        ets = []
        for d in range(2):
            t = SCAN(LB[R8, d, 0:256], one8, LF[R8, d, 0:256], 0.0, ALU.mult, ALU.add, t1)
            t = SCAN(LB[R8, d, 256:512], one8, LF[R8, d, 256:512], LB[R8, d, 255:256], ALU.mult, ALU.add, t)
            t = TT(LI[R8, d, :], LI[R8, d, :], LB[R8, d, :], ALU.subtract, t)
            t = SCAN(LM[R8, d, :], LI[R8, d, :], LI[R8, d, :], 0.0, ALU.max, ALU.max, t)
            t = TT(LB[R8, d, :], LB[R8, d, :], LM[R8, d, :], ALU.add, t)
            v = (lambda x: x[:, ::-1]) if d else (lambda x: x)
            t2 = CP(AN[R8, d, 0:256], v(LI[R8, d, 256:512]), t, free)
            t3 = CP(AN[R8, d, 256:512], v(LI[R8, d, 0:256]), t)
            t4 = TS(NM[R8, d, :], v(LM[R8, d, 256:512]), -1.0, None, ALU.mult, None, t, free)
            t5 = TS(EM[R8, d, :], v(LB[R8, d, 256:512]), -1.0, None, ALU.mult, None, t, free)
            ets.append(A(EM[R8, d, :], EM[R8, d, :], ACT.Exp, t5))
        vproj(0, None)
        vproj(1, None)
        s, b, fr = ps.take()
        for d in range(2):
            for k in range(4):
                t = TR(b[:, 8 * (4 * d + k):8 * (4 * d + k) + 8], AN[R8, d, 128 * k:128 * k + 128], 8, fr, t3)
        act_ = CP(AC, b[:, 0:64], t)
        ps.give(s, act_)
        rows_t = [act_, ets, t4, (s_dve, dve.n)]
        QK = Slots([(view(5120 + 768 * i, 256), view(5376 + 768 * i, 512)) for i in range(2)])
        ST = Slots([view(6656 + 1024 * i, 4, 256) for i in range(2)])
        WW = Slots([view(8704 + 1024 * i, 4, 256) for i in range(2)])
        EMS = Slots([view(10752 + 512 * i, 512) for i in range(2)])
        HS = Slots([view(11776 + 512 * i, 2, 256) for i in range(3)])
        Y = rview(8192, 16, 256)
        yt = [None] * 16
        vread = {}

        def head(h):
            qq, (qh, kh), f = QK.take()
            s, b, t = proj("o_w_in", 8, h, rhs1, 256, ht)
            t = conv3(b, t, s, qh, 256, lambda k: P("ocw", 16 * k + h), P("ocb", h), rows_t, f)
            q1, x1, f1 = tmp.take()
            t1 = A(x1[:, 0:256], qh, ACT.Tanh, t, f1, scale=0.5)
            tq = STT(qh, x1[:, 0:256], 1.0, qh, ALU.add, ALU.mult, t1)
            tmp.give(q1, tq)
            s, b, t = proj("o_w_in", 8, 8 + h, rhs, 512, ht)
            t = conv3(b, t, s, kh, 512, lambda k: P("ocw", 16 * k + 8 + h), P("ocb", 8 + h), rows_t, f)
            q1, x1, f1 = tmp.take()
            t1 = A(x1, kh, ACT.Tanh, t, f1, scale=0.5)
            tk = STT(kh, x1, 1.0, kh, ALU.add, ALU.mult, t1)
            tmp.give(q1, tk)
            yield
            qs, st, sf = ST.take()
            stt = []
            for p in range(2):
                s, b, fr = ps.take()
                for i in range(2):
                    k = 2 * p + i
                    t = MM([(b[:, 256 * i:256 * i + 256], kh[:, 128 * k:128 * k + 128], qh)], fr, tq, tk)
                t1 = A(st[:, 2 * p:2 * p + 2, :], two(b[:, :]), ACT.Copy, t, sf, rows_t, scale=0.25 * 128 ** -0.5)
                ps.give(s, t1)
                stt.append(t1)
            QK.give(qq, t)
            sel = ident[R8, h:h + 1].to_broadcast([8, 128])
            hsq, hs, hf = HS.take()
            ha = None
            for d in range(2):
                s, b, fr = ps.take()
                t = MM([(b[:, 0:256], sel, NM[R8, d, :])], fr, rows_t)
                t = MM([(b[:, 256:512], sel, EM[R8, d, :])])
                qe, ems, ef = EMS.take()
                te = A(ems, b[:, :], ACT.Copy, t, ef, rows_t)
                ps.give(s, te)
                nm, em = ems[:, 0:256], ems[:, 256:512]
                qw, W, wf = WW.take()
                col = [AC[:, 8 * (4 * d + k) + h:8 * (4 * d + k) + h + 1] for k in range(4)]
                tri = C("trib" if d else "trif")
                rng = []
                wt = []
                for k in range(2):
                    dg = slice(128 * k, 128 * k + 128)
                    t1 = STT(W[:, k, dg], nm[:, dg], col[k], tri, ALU.add, ALU.add, te, wf, rows_t)
                    full = (d == 0 and k == 0) or (d == 1 and k == 1)
                    if full:
                        oc = slice(128, 256) if k == 0 else slice(0, 128)
                        wt.append(A(W[:, k, oc], nm[:, oc], ACT.Exp, te, wf, rows_t, bias=col[k]))
                    wt.append(A(W[:, k, dg], W[:, k, dg], ACT.Exp, t1))
                    rng.append(slice(0, 256) if full else dg)
                for k in (2, 3):
                    wt.append(A(W[:, k, :], nm, ACT.Exp, te, wf, rows_t, bias=col[k]))
                t1 = [TT(W[:, k, rng[k]], W[:, k, rng[k]], st[:, k, rng[k]], ALU.mult, wt, stt) for k in range(2)]
                t2 = TT(W[:, 2:4, :], W[:, 2:4, :], st[:, 2:4, :], ALU.mult, wt, stt, q=pool)
                if d == 1:
                    ST.give(qs, t1, t2)
                yield
                seq = [(2, slice(0, 256)), (3, slice(0, 256)), (0, rng[0]), (1, rng[1])]
                sd, bd, frd = ps.take()
                td = MM([(bd[:, c], ones, W[:, k, c]) for k, c in seq], frd, t1, t2)
                sn, bn, frn = ps.take()
                V = VT[(h // 2) % 2]
                for vb in range(2):
                    vc = 256 * (h % 2) + 128 * vb
                    tn = MM([(bn[:, 256 * vb + c.start:256 * vb + c.stop], V[:, k, vc:vc + 128], W[:, k, c])
                             for k, c in seq], frn, vtt[h // 2])
                WW.give(qw, tn)
                qd_, den, df = tmp.take()
                den = den[:, 0:256]
                t = A(den, bd[:, 0:256], ACT.Abs, td, df, rows_t)
                ps.give(sd, t)
                t = TT(den, den, em, ALU.max, t, te)
                EMS.give(qe, t, wt)
                t = REC(den, den, t)
                if d == 0:
                    for vb in range(2):
                        ha = TT(hs[:, vb, :], bn[:, 256 * vb:256 * vb + 256], den, ALU.mult, t, tn, hf, rows_t)
                else:
                    q, x_, f = tmp.take()
                    for vb in range(2):
                        t1 = TT(x_[:, 256 * vb:256 * vb + 256], bn[:, 256 * vb:256 * vb + 256], den, ALU.mult, t, tn, f)
                    ha = TT(hs[:, :, :], hs[:, :, :], two(x_), ALU.add, t1, ha)
                    tmp.give(q, ha)
                ps.give(sn, ha)
                tmp.give(qd_, ha)
                if d == 1:
                    vread[h] = tn
            yield
            if h % 2 and h // 2 < 2:
                vproj(h // 2 + 2, [vread[h - 1], vread[h]])
            for vb in range(2):
                s, b, t = proj("o_w_in", 8, 32 + 2 * h + vb, rhs1, 256, ht)
                q, x_, f = tmp.take()
                t = A(x_[:, 0:256], b[:, 0:256], ACT.Tanh, t, f, scale=0.5)
                ps.give(s, t)
                ho = STT(hs[:, vb, :], x_[:, 0:256], 1.0, hs[:, vb, :], ALU.add, ALU.mult, t, ha)
                tmp.give(q, ho)
            z = []
            for vb in range(2):
                s, b, t = proj("o_w_in", 8, 48 + 2 * h + vb, rhs1, 256, ht)
                q, x_, f = tmp.take()
                t = A(x_[:, 0:256], b[:, 0:256], ACT.Tanh, t, f, scale=0.5)
                t = STT(x_[:, 0:256], x_[:, 0:256], 1.0, b[:, 0:256], ALU.add, ALU.mult, t)
                ps.give(s, t)
                z.append((q, x_, t))
            s, b, t = square_sum(lambda j: hs[:, j, :], 2, 256, [ho, ho], scale=0.5)
            rs, r, t = rstd(b, s, 256, 256, t)
            for vb in range(2):
                j = 2 * h + vb
                q, x_, tz = z[vb]
                t1 = STT(hs[:, vb, :], hs[:, vb, :], P("ohn", j), r, ALU.mult, ALU.mult, t)
                t1 = STT(hs[:, vb, :], hs[:, vb, :], 0.25, x_[:, 0:256], ALU.mult, ALU.mult, t1, tz)
                tmp.give(q, t1)
                yt[j] = split((Y[0][:, j, :], Y[1][:, j, :]), hs[:, vb, :], t1, free)
            rbs.give(rs, t1)
            HS.give(hsq, yt[2 * h], yt[2 * h + 1])

        pipeline((head(h) for h in range(8)), oldest=True)
        MIX = view(0, 8, 256)
        out_and_norm([("o_w_out", 16, 0, operand(Y), yt)], MIX, 256, lambda j, s: MC[:, 48 + 2 * j:48 + 2 * j + 1],
                     everything_read())

    def whole():
        layer_even()
        ffn(0, 1)
        layer_fox()
        ffn(1, 1)
        layer_even2()
        layer_odd2()
        load(out, X[:, :, 0:256], s_out, xt)

    whole()
    assert len(plan) == NTILES
    ld = Queue(None)
    for c in range((len(plan) + TPC - 1) // TPC):
        while extra and extra[0][0] <= c:
            _, dst, src, sm, toks = extra.pop(0)
            ld.dma(lambda e, dst=dst, src=src: e.dma_start(dst, src), sm, *toks)
        ld.dma(lambda e, c=c: e.dma_start(RAWB[:, c % RAW, :], ws[c]), s_w[c % RAW], raw_free.get(c - RAW))
    for _, dst, src, sm, toks in extra:
        ld.dma(lambda e, dst=dst, src=src: e.dma_start(dst, src), sm, *toks)
    ld.wait((s_out, 16))
    return pe, act, dve, pool, ld, plan, mine


NTILES = 3152


def build_program(nc, xT, ctxT, ws, pr, cs, rgw, fw, dec, out):
    _, PN = param_layout()
    _, CN = const_layout()
    ctx = ExitStack()
    with ctx:
        def sb(name, *shape, dt=F32):
            return ctx.enter_context(nc.sbuf_tensor(name, [128, *shape], dt))

        def sem(name):
            return ctx.enter_context(nc.semaphore(name))

        bufs = (sb("X", 8, 512), sb("RH", 16384, dt=F32R), sb("RAWB", RAW, TPC * 128),
                sb("WH", SPL, TPC * 128, dt=F32R), sb("WL", SPL, TPC * 128, dt=F32R), sb("PR", PN), sb("CS", CN),
                [sb(f"TMP{i}", 512) for i in range(6)], [sb(f"RB{i}", 512) for i in range(2)], sb("SM", 320),
                sb("MODB", 272), sb("AR", NA), [ctx.enter_context(nc.psum_tensor(f"PS{i}", [128, 512], F32))
                                                for i in range(8)])
        sems = (sem("s_pe"), sem("s_act"), sem("s_dve"), sem("s_pool"), [sem(f"s_w{i}") for i in range(RAW)],
                *(sem(n) for n in ("s_cs", "s_pr", "s_x", "s_rg", "s_fw", "s_dec", "s_out")))
        dram = (xT, ctxT, ws, pr, cs, rgw, fw, dec, out)
        kinds = record(bufs, sems, dram, [])[6]
        pe, act, dve, pool, ld, plan, again = record(bufs, sems, dram, kinds)
        assert kinds == again
        block = ctx.enter_context(nc.Block())

        @block.sync
        def _(eng):
            ld.emit(eng)

        @block.tensor
        def _(eng):
            pe.emit(eng)

        @block.scalar
        def _(eng):
            act.emit(eng)

        @block.vector
        def _(eng):
            dve.emit(eng)

        @block.gpsimd
        def _(eng):
            pool.emit(eng)
    return plan


def constants():
    off, n = const_layout()
    c = np.zeros((128, n), np.float64)

    def put(name, a):
        o, w = off[name]
        c[:a.shape[0], o:o + a.shape[1]] = a

    p = np.arange(128)[:, None]
    put("ident", np.eye(128))
    put("ones", np.ones((128, 256)))
    perm = np.zeros((128, 128))
    for base in (0, 64):
        for i in range(32):
            perm[base + 32 + i, base + i] = -1
            perm[base + i, base + 32 + i] = 1
    put("perm", perm)
    inv = (np.float32(10000.0) ** (-np.arange(32, dtype=np.float32) / np.float32(32))).astype(np.float32)
    pos = [np.arange(256) // 64, np.arange(256) % 64]
    ang = np.stack([(pos[d // 64].astype(np.float32) * inv[d % 32]).astype(np.float32) for d in range(128)])
    put("cos", np.cos(ang.astype(np.float64)))
    put("sin", np.sin(ang.astype(np.float64)))
    put("trif", np.where(p <= np.arange(128)[None], 0, NEG))
    put("trib", np.where(p >= np.arange(128)[None], 0, NEG))
    cols = np.zeros((128, 8))
    cols[:, 0] = EPS
    cols[0:64, 1] = 0.125
    cols[64:, 2] = 0.125
    cols[1:, 3] = 1
    put("cols", cols)
    th = np.pi * (2 * np.arange(256) + 1) / 512
    t = np.arange(256)
    fwd = np.concatenate([np.cos(np.outer(t, th)), -np.sin(np.outer(t, th))], 1)
    put("dft", np.concatenate([fwd[:128], fwd[128:]], 1))
    bwd = np.concatenate([np.cos(np.outer(th, t)), -np.sin(np.outer(th, t))], 0) / 256
    put("idft", np.concatenate([bwd[128 * i:128 * i + 128] for i in range(4)], 1))
    n_ = 256
    tt = np.linspace(0.0, 1.0, n_, dtype=np.float32)[:, None]
    bands = np.linspace(1e-4, 15, 16, dtype=np.float32)
    a = (np.float32(2 * math.pi / n_) * np.arange(n_, dtype=np.float32)[:, None] * bands).astype(np.float32)
    z = np.concatenate([tt, np.cos(a), -np.sin(a)], 1)
    lo, hi = math.log(1e-2) / 1.5, math.log(1e-2) / 0.3
    deltas = np.linspace(lo, hi, 1024, dtype=np.float32)
    decay = np.exp((-tt * np.abs(deltas)).astype(np.float32).astype(np.float64))
    dec = decay.reshape(2, 128, 1024).transpose(1, 0, 2)
    zT = np.zeros((64, 256), np.float32)
    zT[0:33] = z.T
    return c.astype(np.float32), np.ascontiguousarray(dec.astype(np.float32)), zT


def columns(v):
    v = np.asarray(v)
    return v.reshape(-1, 128).T


def padded(v):
    o = np.zeros((128, 1), v.dtype)
    o[:v.size, 0] = v.reshape(-1)
    return o


def lay_out(i, plan):
    a = {k: np.asarray(v) for k, v in i.items()}
    fT = lambda x: np.ascontiguousarray(x.reshape(256, 8, 128).transpose(2, 1, 0))
    gb = a["o_gate_b_2"][0].reshape(4, 8)
    gtb = np.zeros((128, 1), gb.dtype)
    for g in range(4):
        gtb[32 * g:32 * g + 8, 0] = gb[g]
    parts = {
        "ng": columns(a["norm_gains"]), "lbl": columns(a["hgrn_lb_logits"]), "hgn": columns(a["hgrn_norm"]),
        "rcw": columns(a["rg_conv_w"]), "rcb": columns(a["rg_conv_b"]), "rba": columns(a["rg_ba"]),
        "rbx": columns(a["rg_bx"]), "lam": columns(a["rg_lambda"]), "fxb": padded(a["fox_f_bias"]),
        "fcw": columns(a["ffn_conv_w"]), "fcb": columns(a["ffn_conv_b"]),
        "cc": np.stack([columns(a["c_2"]), columns(a["c_ctx_2"])], 2).reshape(128, 16),
        "bmod": np.repeat(columns(a["b_mod_2"]), 2, axis=1),
        "gpre": np.repeat(columns(a["g_pre_2"]), 2, axis=1), "gpost": np.repeat(columns(a["g_post_2"]), 2, axis=1),
        "ecw": columns(a["e_conv_w_2"]), "ecb": columns(a["e_conv_b_2"]),
        "fb1": padded(a["e_filt_b1_2"]), "ffr": padded(a["e_filt_freq_2"]), "fb2": padded(a["e_filt_b2_2"]),
        "hyb": columns(a["e_hy_bias_2"]), "qn": columns(a["e_q_norm_2"]), "kn": columns(a["e_k_norm_2"]),
        "ocw": columns(a["o_conv_w_2"]), "ocb": columns(a["o_conv_b_2"]), "gtb": gtb,
        "ohn": columns(a["o_head_norm_2"]),
    }
    off, n = param_layout()
    pr = np.zeros((128, n), np.float32)
    for k, v in parts.items():
        pr[:, off[k]:off[k] + v.shape[1]] = v
    ow = a["o_w_in_2"][0]
    gates = np.zeros((1024, 128), ow.dtype)
    for g in range(4):
        gates[:, 32 * g:32 * g + 8] = ow[:, 8192 + 8 * g:8192 + 8 * g + 8]
    od = a["odd_w_in"][0]
    od = np.concatenate([od, np.zeros((1024, 3200 - od.shape[1]), od.dtype)], 1)
    mats = {
        "even_w_in": a["even_w_in"][0], "even_w_out": a["even_w_out"][0], "odd_w_in": od,
        "odd_w_out": a["odd_w_out"][0], "e_w_in": a["e_w_in_2"][0], "e_w_out": a["e_w_out_2"][0],
        "o_w_in": np.concatenate([ow[:, 0:8192], gates], 1), "o_w_out": a["o_w_out_2"][0],
    }
    for l in range(2):
        mats[f"ffn_up{l}"] = a["ffn_w_up"][l]
        mats[f"ffn_down{l}"] = a["ffn_w_down"][l]
        mats[f"w_mod{l}"] = a["w_mod_2"][l]
    nchunk = (len(plan) + TPC - 1) // TPC
    ws = np.zeros((nchunk, 128, TPC, 128), np.float32)
    for t, (name, k, m) in enumerate(plan):
        ws[t // TPC, :, t % TPC, :] = mats[name][128 * k:128 * k + 128, 128 * m:128 * m + 128]
    ws = ws.reshape(nchunk, 128, TPC * 128)
    rgw = np.zeros((128, 8, 128), np.float32)
    for g, name in enumerate(("rg_wa", "rg_wx")):
        for b in range(8):
            o = 64 * (b % 2)
            rgw[o:o + 64, 4 * g + b // 2, o:o + 64] = a[name][0, b]
    fw = np.zeros((64, 2432), np.float32)
    fw[0:33, 0:64] = a["e_filt_w1_2"][0]
    fw[:, 64:128] = a["e_filt_w2_2"][0]
    fw[:, 128:2176] = a["e_filt_w3_2"][0]
    cs, dec, fw[:, 2176:] = constants()
    return {"xT": fT(a["x"]), "ctxT": fT(a["ctx_2"]), "ws": ws, "pr": pr, "cs": cs, "rgw": rgw, "fw": fw, "dec": dec}


SHAPES = {"xT": (128, 8, 256), "ctxT": (128, 8, 256), "ws": (NTILES // TPC, 128, TPC * 128),
          "pr": (128, param_layout()[1]), "cs": (128, const_layout()[1]), "rgw": (128, 8, 128), "fw": (64, 2432),
          "dec": (128, 2, 1024)}


def kernel(**inputs):
    import concourse.bacc as _bacc
    from concourse.bass_utils import run_bass_kernel_spmd as _run

    nc = _bacc.Bacc("TRN2", target_bir_lowering=False, num_devices=1)
    args = [nc.dram_tensor(k, v, F32, kind="ExternalInput").ap() for k, v in SHAPES.items()]
    out = nc.dram_tensor("outT", (128, 8, 256), F32, kind="ExternalOutput").ap()
    plan = build_program(nc, *args, out)
    r = _run(nc, [lay_out(inputs, plan)], core_ids=[0])
    return np.ascontiguousarray(r.results[0]["outT"].transpose(2, 1, 0).reshape(1, 256, 1024))
```

```python
from contextlib import ExitStack
import math

import numpy as np
import concourse.bass as bass
from concourse import mybir

F32 = mybir.dt.float32
F32R = mybir.dt.float32r
ALU = mybir.AluOpType
ACT = mybir.ActivationFunctionType
AXX = mybir.AxisListType.X

EPS = 1e-6
RAW = 4
SPL = 3
TPC = 8
NA = 13600
NEG = -1e30


def param_layout():
    sizes = [("ng", 64), ("lbl", 12), ("hgn", 4), ("rcw", 16), ("rcb", 4), ("rba", 4), ("rbx", 4), ("lam", 4),
             ("fxb", 1), ("fcw", 264), ("fcb", 88), ("cc", 16), ("bmod", 96), ("gpre", 32), ("gpost", 32),
             ("ecw", 72), ("ecb", 24), ("fb1", 1), ("ffr", 1), ("fb2", 1), ("hyb", 8), ("qn", 1), ("kn", 1),
             ("ocw", 48), ("ocb", 16), ("gtb", 1), ("ohn", 16)]
    at, out = 0, {}
    for name, n in sizes:
        out[name] = at
        at += n
    return out, at


def const_layout():
    sizes = [("ident", 128), ("ones", 256), ("cols", 8), ("perm", 128), ("cos", 256), ("sin", 256), ("trif", 128),
             ("trib", 128), ("dft", 1024), ("idft", 1024)]
    at, out = 0, {}
    for name, n in sizes:
        out[name] = (at, n)
        at += n
    return out, at


class Queue:

    def __init__(self, sem):
        self.sem, self.n, self.items, self.seen = sem, 0, [], {}

    def wait(self, *toks):
        for t in flat(toks):
            if self.seen.get(id(t[0]), 0) < t[1]:
                self.seen[id(t[0])] = t[1]
                self.items.append(("w", t[0], t[1]))

    def do(self, fn, *toks):
        self.wait(*toks)
        self.n += 1
        self.items.append(("i", fn, self.sem, 1))
        return (self.sem, self.n)

    def plain(self, fn, *toks):
        self.wait(*toks)
        self.items.append(("i", fn, None, 0))

    def dma(self, fn, sem, *toks):
        self.wait(*toks)
        self.items.append(("i", fn, sem, 16))

    def emit(self, eng):
        for it in self.items:
            if it[0] == "w":
                eng.wait_ge(it[1], it[2])
            else:
                ins = it[1](eng)
                if it[2] is not None:
                    ins.then_inc(it[2], it[3])


def flat(toks):
    for t in toks:
        if t is None:
            continue
        if isinstance(t, list):
            yield from flat(t)
        else:
            yield t


class Slots:

    def __init__(self, bufs):
        self.bufs, self.free, self.idle = bufs, [None] * len(bufs), list(range(len(bufs)))

    def take(self):
        s = self.idle.pop(0)
        return s, self.bufs[s], self.free[s]

    def give(self, s, *toks):
        assert s not in self.idle
        self.idle.append(s)
        self.free[s] = list(toks)


def pipeline(gens):
    active = []
    for g in gens:
        active.insert(0, g)
        active = [x for x in active if next(x, "end") != "end"]
    while active:
        active = [x for x in active if next(x, "end") != "end"]


def record(bufs, sems, dram, kinds):
    X, RH, RAWB, WH, WL, PR, CS, TMPS, RBS, SM, MODB, AR, PSUM = bufs
    s_pe, s_act, s_dve, s_pool, s_w, s_cs, s_cs2, s_pr, s_x, s_xc, s_rg, s_fw, s_fw2, s_dec, s_out = sems
    xT, ctxT, ws, pr, cs, rgw, fw, dec, out = dram
    POFF, PN = param_layout()
    COFF, CN = const_layout()
    pe, act, dve, pool = Queue(s_pe), Queue(s_act), Queue(s_dve), Queue(s_pool)
    extra = []
    ps = Slots([b[:, :] for b in PSUM])
    tmp = Slots([t[:, :] for t in TMPS])
    rbs = Slots([t[:, :] for t in RBS])

    def C(name, rows=128):
        a, n = COFF[name]
        return CS[0:rows, a:a + n]

    def P(name, j=0, n=1):
        a = POFF[name] + j
        return PR[:, a:a + n]

    ident, ones = C("ident"), C("ones")[:, 0:128]
    CCOL = COFF["cols"][0]
    c_eps, c_even, c_odd, c_m0 = (CS[:, CCOL + i:CCOL + i + 1] for i in range(4))
    T_CS, T_CS2, T_PR, T_X, T_XC = (s_cs, 16), (s_cs2, 16), (s_pr, 16), (s_x, 16), (s_xc, 16)
    ar_free = [None]

    def shaped(base, off, *shape):
        n = 1
        for d in shape:
            n *= d
        v = base[:, off:off + n]
        if len(shape) == 1:
            return v
        if len(shape) == 2:
            return v.rearrange("p (a b) -> p a b", a=shape[0])
        return v.rearrange("p (a b c) -> p a b c", a=shape[0], b=shape[1])

    def view(off, *shape):
        assert off + int(np.prod(shape)) <= NA, (off, shape)
        return shaped(AR, off, *shape)

    def rview(off, *shape):
        n = int(np.prod(shape))
        assert off + 2 * n <= 16384
        return shaped(RH, off, *shape), shaped(RH, off + n, *shape)

    def A(out_, in_, func, *w, bias=None, scale=1.0, accum=None):
        kw = {"scale": scale}
        if bias is not None:
            kw["bias"] = bias
        if accum is not None:
            kw["accum_out"] = accum
        return act.do(lambda e: e.activation(out_, in_, func, **kw), *w)

    def TS(out_, in_, s1, s2, o0, o1, *w, q=None):
        q = q or dve
        if o1 is None:
            return q.do(lambda e: e.tensor_scalar(out_, in_, s1, None, o0), *w)
        return q.do(lambda e: e.tensor_scalar(out_, in_, s1, s2, o0, o1), *w)

    def TT(out_, a, b, op, *w, q=None):
        return (q or dve).do(lambda e: e.tensor_tensor(out_, a, b, op), *w)

    def STT(out_, a, s, b, o0, o1, *w):
        return dve.do(lambda e: e.scalar_tensor_tensor(out=out_, in0=a, scalar=s, in1=b, op0=o0, op1=o1), *w)

    def CP(out_, in_, *w, q=None):
        return (q or dve).do(lambda e: e.tensor_copy(out_, in_), *w)

    def REC(out_, in_, *w):
        return dve.do(lambda e: e.reciprocal(out_, in_), *w)

    def SCAN(out_, a, b, init, o0, o1, *w):
        return dve.do(lambda e: e.tensor_tensor_scan(out_, a, b, init, o0, o1), *w)

    def tables(name):
        act.plain(lambda e: e.preload_act_table_set(name))

    def MM(groups, *w):
        pe.wait(*w)
        n = len(groups)
        for i, (o, l, r) in enumerate(groups):
            def f(e, o=o, l=l, r=r, i=i):
                return e.matmul(o, l, r, start=(i == 0), stop=(i == n - 1))
            if i < n - 1:
                pe.plain(f)
            else:
                return pe.do(f)

    def TR(pairs, rows, *w):
        pe.wait(*w)
        for i, (o, a) in enumerate(pairs):
            f = lambda e, o=o, a=a: e.transpose(o, a, ident[0:rows, 0:rows])
            if i < len(pairs) - 1:
                pe.plain(f)
            else:
                return pe.do(f)

    def split(hl, x, tok, *w):
        hi, lo = hl
        t1 = A(hi, x, ACT.Copy, tok, *w)
        t2 = TT(lo, x, hi.bitcast(F32), ALU.subtract, t1, tok)
        return [t1, t2]

    def everything_read():
        return [(q.sem, q.n) for q in (pe, act, dve, pool) if q.n]

    plan, mine, background = [], [], []
    raw_free, spl_free, spl_tok = {}, {}, {}

    def split_chunk(c):
        raw = RAWB[:, c % RAW, :]
        hi, lo = WH[:, c % SPL, :], WL[:, c % SPL, :]
        got = (s_w[c % RAW], 16 * (c // RAW + 1))
        prev = max([x for x in spl_tok if x <= c - SPL and x % SPL == c % SPL], default=None)
        fr = spl_free[prev] if prev is not None else None
        t1 = act.do(lambda e: e.copy(hi, raw), got, fr)
        t2 = TT(lo, raw, hi.bitcast(F32), ALU.subtract, t1, got)
        raw_free[c] = [t1, t2]
        spl_tok[c] = [t1, t2]

    def fetch(kind, name, k, m, n):
        t = len(plan)
        c, o = t // TPC, t % TPC
        if o == 0:
            mine.append(kind)
            for d in range(SPL):
                if c + d < len(kinds) and kinds[c + d] and c + d not in spl_tok:
                    split_chunk(c + d)
                elif not kinds and d == 0 and kind:
                    split_chunk(c)
        assert mine[c] == kind and o + n <= TPC
        plan.extend((name, k, m + i) for i in range(n))
        sl = slice(o * 128, (o + n) * 128)
        end = c if o + n == TPC else None
        if kind:
            pe.wait(spl_tok[c])
            return (WH[:, c % SPL, sl], WL[:, c % SPL, sl]), end
        pe.wait((s_w[c % RAW], 16 * (c // RAW + 1)))
        return RAWB[:, c % RAW, sl], end

    def fetched(end, tok):
        if end is not None:
            if mine[end]:
                spl_free[end] = tok
            else:
                raw_free[end] = tok

    def mm3(o, l, r, first, last, want):
        (lh, ll), (rh, rl) = l, r
        for i, (a, b) in enumerate(((lh, rh), (lh, rl), (ll, rh))):
            def f(e, a=a, b=b, i=i):
                return e.matmul(o, a, b, start=(first and i == 0), stop=(last and i == 2))
            if i < 2 or not want:
                pe.plain(f)
            else:
                return pe.do(f)

    def proj(name, kt, m, rhs, N, w, k0=0):
        s, b, fr = ps.take()
        pe.wait(fr)
        for k in range(kt):
            wt, end = fetch(True, name, k0 + k, m, 1)
            pe.wait(w[k])
            tok = mm3(b[:, 0:N], wt, rhs(k), k == 0, k == kt - 1, end is not None or k == kt - 1)
            fetched(end, tok)
        step()
        return s, b, tok

    def proj_tok(name, kt, m, lhs, nb, width, w):
        got = []
        for n in range(nb):
            s, b, fr = ps.take()
            pe.wait(fr, w[0:kt])
            got.append((s, b))
        toks = []
        for k in range(kt):
            wt, end = fetch(True, name, k, m, width // 128)
            for n in range(nb):
                last = k == kt - 1
                tok = mm3(got[n][1][:, 0:width], lhs(k, n), wt, k == 0, last, last or (end is not None and n == nb - 1))
                if last:
                    toks.append(tok)
            fetched(end, tok)
            step()
        return [(s, b, t) for (s, b), t in zip(got, toks)]

    MODC, MC, SCC = MODB[:, 0:192], MODB[:, 192:256], MODB[:, 256:272]
    filler = {"l": 0, "c": 0, "t": None, "toks": [], "done": 0}

    def mod(l, j, seq):
        return MODC[:, l * 96 + 2 * j + seq:l * 96 + 2 * j + seq + 1]

    def unit():
        l, c = filler["l"], filler["c"]
        if l == 2:
            return
        if filler["t"] is None:
            t = A(SCC, P("cc", 0, 16), ACT.Sigmoid, T_PR)
            filler["t"] = TT(SCC, SCC, P("cc", 0, 16), ALU.mult, t)
        filler["l"], filler["c"] = (l + 1, 0) if c == 5 else (l, c + 1)
        s, b, fr = ps.take()
        pe.wait(fr, filler["t"])
        for k in range(8):
            wt, end = fetch(False, f"w_mod{l}", k, 4 * c, 4)
            def f(e, wt=wt, k=k, b=b):
                return e.matmul(b[0:2, :], SCC[:, 2 * k:2 * k + 2], wt, start=(k == 0), stop=(k == 7))
            if end is None and k < 7:
                pe.plain(f)
            else:
                t = pe.do(f)
                fetched(end, t)
            if k % 2 and k < 7:
                yield
        background.append(fill_tail(l, c, s, b, t))

    def fill(n=1):
        for _ in range(n):
            for _ in unit():
                pass

    def trickle():
        while filler["l"] < 2:
            yield from unit()
            yield

    def fill_tail(l, c, s, b, t):
        q, row, tf = tmp.take()
        t = CP(row[0:2, :], b[0:2, :], t, tf)
        ps.give(s, t)
        yield
        s, b, fr = ps.take()
        t = TR([(b[:, 2 * i:2 * i + 2], row[0:2, 128 * i:128 * i + 128]) for i in range(4)], 2, fr, t, T_CS)
        tmp.give(q, t)
        t = TT(MODC[:, 96 * l + 8 * c:96 * l + 8 * c + 8], b[:, 0:8], P("bmod", 48 * l + 8 * c, 8), ALU.add, t, T_PR)
        ps.give(s, t)
        filler["toks"].append(t)
        if c == 5:
            a = 96 * l
            t1 = STT(MC[:, 32 * l:32 * l + 16], MODC[:, a + 16:a + 32], 1.0, P("gpre", 16 * l, 16), ALU.add, ALU.mult,
                     filler["toks"])
            t2 = TT(MC[:, 32 * l + 16:32 * l + 32], MODC[:, a + 32:a + 48], P("gpost", 16 * l, 16), ALU.mult)
            filler["toks"] += [t1, t2]
            filler["done"] += 1
        yield

    def step():
        if background and next(background[0], "end") == "end":
            background.pop(0)

    def finish():
        while background:
            step()

    def fill_all(l):
        while filler["l"] <= l:
            fill()
        while filler["done"] <= l:
            step()

    def rstd(b, s, N, n, tok, fillers=0):
        rs, r, rfr = rbs.take()
        tables("natural_log_exp_and_others")
        q, v, f = tmp.take()
        r, v = r[:, 0:N], v[:, 0:N]
        t = A(r, b[:, 0:N], ACT.Ln, tok, rfr, bias=c_eps, scale=1.0 / n)
        tv = TS(v, b[:, 0:N], 1.0 / n, EPS, ALU.mult, ALU.add, t, f)
        ps.give(s, tv)
        t = A(r, r, ACT.Exp, t, scale=-0.5)
        t = STT(v, v, -0.5, r, ALU.mult, ALU.mult, t, tv)
        t = TT(v, v, r, ALU.mult, t)
        t = STT(r, v, 1.5, r, ALU.add, ALU.mult, t)
        tmp.give(q, t)
        fill(fillers)
        return rs, r, t

    def square_sum(src, nb, N, toks, scale=1.0):
        s, b, fr = ps.take()
        for j in range(nb):
            q, x, f = tmp.take()
            t = A(x[:, 0:N], src(j), ACT.Square, toks[j], f, scale=scale)
            g = lambda e, j=j, x=x: e.matmul(b[:, 0:N], ones, x[:, 0:N], start=(j == 0), stop=(j == nb - 1))
            t = pe.do(g, t, fr, T_CS)
            tmp.give(q, t)
        return s, b, t

    xt = [T_X] * 8

    def pre_norm(gains, N, hfree, shift=None, fillers=0, behind=None):
        s, b, t = square_sum(lambda j: X[:, j, 0:N], 8, N, xt)
        rs, r, t = rstd(b, s, N, 1024, t, fillers)
        HH = rview(0, 8, N)
        ht = [None] * 8

        def block(j):
            q, x, f = tmp.take()
            last = []
            for seq in range(N // 256):
                c = slice(256 * seq, 256 * seq + 256)
                t1 = STT(x[:, c], X[:, j, c], gains(j, seq), r[:, c], ALU.mult, ALU.mult, t, xt[j], T_PR, f, filler["toks"])
                last.append(A(x[:, c], x[:, c], ACT.Identity, t1, bias=shift(j, seq)) if shift else t1)
            hi, lo = HH[0][:, j, :], HH[1][:, j, :]
            th = A(hi, x[:, 0:N], ACT.Copy, last, hfree)
            yield
            if behind:
                next(behind), next(behind)
            tl = TT(lo, x[:, 0:N], hi.bitcast(F32), ALU.subtract, th, last, hfree, q=pool if j % 3 == 1 else dve)
            ht[j] = [th, tl]
            tmp.give(q, ht[j])

        pipeline(block(j) for j in range(8))
        rbs.give(rs, ht)
        if behind:
            at_once(behind)
        return (lambda k: (HH[0][:, k, :], HH[1][:, k, :])), ht

    def out_and_norm(name, kt, k0, rhs, st, MIX, N, gains, mfree, fillers=0, half=None):
        mt, acc = [], None
        for m in range(8):
            s, b, t = proj(name, kt, m, rhs, N, st, k0)
            if half:
                mt.append(TT(MIX[:, m, :], MIX[:, m, :], b[:, 0:N], ALU.add, t, half[m]))
            else:
                mt.append(A(MIX[:, m, :], b[:, 0:N], ACT.Copy, t, mfree))
            ps.give(s, mt[m])
            q, x, f = tmp.take()
            t = A(x[:, 0:N], MIX[:, m, :], ACT.Square, mt[m], f)
            if acc is None:
                acc = (q, x, t)
            elif m < 7:
                q0, x0, t0 = acc
                acc = (q0, x0, TT(x0[:, 0:N], x0[:, 0:N], x[:, 0:N], ALU.add, t, t0, q=pool))
                tmp.give(q, acc[2])
        s, b, fr = ps.take()
        t0 = pe.do(lambda e, x=acc[1]: e.matmul(b[:, 0:N], ones, x[:, 0:N], start=True, stop=False), acc[2], fr)
        tmp.give(acc[0], t0)
        t = pe.do(lambda e, x=x: e.matmul(b[:, 0:N], ones, x[:, 0:N], start=False, stop=True), t)
        tmp.give(q, t)
        rs, r, t = rstd(b, s, N, 1024, t, fillers)
        for j in range(8):
            both = []
            for seq in range(N // 256):
                c = slice(256 * seq, 256 * seq + 256)
                t1 = STT(MIX[:, j, c], MIX[:, j, c], gains(j, seq), r[:, c], ALU.mult, ALU.mult, t, mt[j])
                both.append(TT(X[:, j, c], X[:, j, c], MIX[:, j, c], ALU.add, t1, T_XC, q=pool if j % 2 else dve))
            xt[j] = both
        rbs.give(rs, t1)

    def log1p_exp_neg_abs(dst, x, a, b, tok):
        t = A(a, x, ACT.Abs, tok)
        t = A(a, a, ACT.Exp, t, scale=-1.0)
        t = TS(b, a, 2.0, None, ALU.add, None, t)
        t = REC(b, b, t)
        yield
        t = TT(a, a, b, ALU.mult, t)
        t = TT(b, a, a, ALU.mult, t)
        t = TS(dst, b, 1.0 / 19, None, ALU.mult, None, t)
        yield
        for n in (17, 15, 13, 11, 9, 7, 5, 3):
            t = STT(dst, dst, 1.0 / n, b, ALU.add, ALU.mult, t)
            if n in (13, 7):
                yield
        t = STT(dst, dst, 1.0, a, ALU.add, ALU.mult, t)
        return TS(dst, dst, 2.0, None, ALU.mult, None, t)

    def log_sigmoid(dst, x, a, b, tok):
        t = yield from log1p_exp_neg_abs(dst, x, a, b, tok)
        return STT(dst, x, 0.0, dst, ALU.min, ALU.subtract, t)

    def at_once(gen):
        while True:
            try:
                next(gen)
            except StopIteration as e:
                return e.value

    def load(dst, src, sm, *toks, at=None):
        extra.append((len(plan) // TPC + RAW - 1 if at is None else at, dst, src, sm, toks))

    N1 = CCOL + 8
    load(X[:, :, 0:256], xT, s_x, at=0)
    load(CS[:, 0:N1], cs[:, 0:N1], s_cs, at=0)
    load(PR[:, :], pr, s_pr, at=0)
    load(CS[:, N1:CN], cs[:, N1:CN], s_cs2, at=9)
    load(X[:, :, 256:512], ctxT, s_xc, at=12)

    def conv_causal(b, tok, s, dst, K, taps, bias, *w):
        t = A(dst, b[:, 0:256], ACT.Identity, tok, *w, bias=bias, scale=taps(K - 1))
        for d in range(1, K):
            t = STT(dst[:, d:256], b[:, 0:256 - d], taps(K - 1 - d), dst[:, d:256], ALU.mult, ALU.add, t)
        ps.give(s, t)
        return t

    def operand(hl):
        return lambda k: (hl[0][:, k, :], hl[1][:, k, :])

    def blocks(rhs):
        return lambda k, n: tuple(v[:, n * 128:n * 128 + 128] for v in rhs(k))

    def ffn(l, fillers=0):
        free = everything_read()
        hid = rview(4096, 22, 256)
        MIX = view(0, 8, 256)
        GV = Slots([view(2048 + 256 * i, 256) for i in range(8)])
        rhs, ht = pre_norm(lambda j, s: P("ng", (l * 4 + 2) * 8 + j), 256, free, fillers=fillers)
        hidt = []
        if l == 1:
            background.append(hyena_head(free))

        def unit(j):
            pair = []
            for half in range(2):
                q, g, f = GV.take()
                m = j + 22 * half
                s, b, t = proj(f"ffn_up{l}", 8, m, rhs, 256, ht)
                t = conv_causal(b, t, s, g, 3, lambda k: P("fcw", (l * 3 + k) * 44 + m), P("fcb", l * 44 + m), f, free)
                pair.append((q, g, t))
            yield
            (qg, g, tg), (qv, v, tv) = pair
            tg = A(g, g, ACT.Gelu_apprx_tanh, tg)
            t = TT(g, g, v, ALU.mult, tg, tv, q=pool)
            GV.give(qv, t)
            yield
            t = split((hid[0][:, j, :], hid[1][:, j, :]), g, t, free)
            GV.give(qg, t)
            hidt.append(t)

        pipeline(unit(j) for j in range(22))
        out_and_norm(f"ffn_down{l}", 22, 0, operand(hid), hidt, MIX, 256, lambda j, s: P("ng", (l * 4 + 3) * 8 + j),
                     free, fillers)

    def layer_even():
        E1, Qb, Gb = view(0, 4, 256), view(1024, 4, 256), view(2048, 4, 256)
        Fb = E1
        Bc, E2, E3 = (view(3072 + 1024 * i, 4, 256) for i in range(3))
        Vt = view(6144, 2, 512)
        KH = view(7168, 4, 256)
        SC = view(8192, 4, 2, 128)
        KT = view(9216, 4, 2, 128)
        SS = view(10240, 2, 3 * 128)
        XF = view(11008, 4, 256)
        RGW = view(12032, 8, 128)
        OH = Slots([view(13056 + 256 * i, 256) for i in range(2)])
        Y = rview(4096, 8, 256)
        MIX = view(4096, 8, 256)
        lb, oml = SM[:, 0:4], SM[:, 4:8]
        load(RGW, rgw, s_rg, at=15)
        zt = dve.do(lambda e: e.memset(SC[:, :, :, :], 0.0))
        L = P("lbl", 0, 12)
        m_, e_, d_ = SM[:, 8:12], SM[:, 12:24], SM[:, 24:28]
        t = TT(m_, L[:, 0:4], L[:, 4:8], ALU.max, T_PR)
        t = TT(m_, m_, L[:, 8:12], ALU.max, t)
        for r in range(3):
            t1 = TT(e_[:, 4 * r:4 * r + 4], L[:, 4 * r:4 * r + 4], m_, ALU.subtract, t)
        t = A(e_, e_, ACT.Exp, t1)
        t = TT(d_, e_[:, 0:4], e_[:, 4:8], ALU.add, t)
        t = TT(d_, d_, e_[:, 8:12], ALU.add, t)
        t = REC(d_, d_, t)
        t = TT(lb, e_[:, 0:4], d_, ALU.mult, t)
        lbt = TS(oml, lb, -1.0, 1.0, ALU.mult, ALU.add, t)
        c8, nc8, sa, sb_ = SM[:, 32:36], SM[:, 36:40], SM[:, 40:44], SM[:, 44:48]
        lam = P("lam", 0, 4)
        t = at_once(log1p_exp_neg_abs(c8, lam, sa, sb_, T_PR))
        t = TS(sa, lam, -1.0, 0.0, ALU.mult, ALU.max, t)
        t = TT(c8, c8, sa, ALU.add, t)
        t = TS(c8, c8, 8.0, None, ALU.mult, None, t)
        c8t = TS(nc8, c8, -1.0, None, ALU.mult, None, t)

        rhs, ht = pre_norm(lambda j, s: P("ng", j), 256, None, fillers=1)
        ft, qt, gt = [], [], []
        for h in range(4):
            s, b, t = proj("even_w_in", 8, 4 + h, rhs, 256, ht)
            t = A(Fb[:, h, :], b[:, 0:256], ACT.Sigmoid, t)
            ps.give(s, t)
            ft.append(TS(Fb[:, h, :], Fb[:, h, :], oml[:, h:h + 1], lb[:, h:h + 1], ALU.mult, ALU.add, t, lbt))
        for h in range(4):
            s, b, t = proj("even_w_in", 8, h, rhs, 256, ht)
            t1 = A(Qb[:, h, :], b[:, 0:256], ACT.Sigmoid, t)
            t = TT(Qb[:, h, :], Qb[:, h, :], b[:, 0:256], ALU.mult, t1)
            ps.give(s, t)
            qt.append(t)
        for h in range(4):
            s, b, t = proj("even_w_in", 8, 12 + h, rhs, 256, ht)
            t = A(Gb[:, h, :], b[:, 0:256], ACT.Sigmoid, t)
            ps.give(s, t)
            gt.append(t)
        tables("natural_log_exp_and_others")
        kt_, bt, lt = [], [], []
        for h in range(4):
            kt_.append(TS(KH[:, h, :], Fb[:, h, :], -1.0, 1.0, ALU.mult, ALU.add, ft[h]))
            lt.append(A(Fb[:, h, :], Fb[:, h, :], ACT.Ln, ft[h], kt_[h]))
        for h in range(4):
            for n in range(4):
                c = slice(64 * n, 64 * n + 64)
                t1 = SCAN(Bc[:, h, c], C("ones")[:, 0:64], Fb[:, h, c], 0.0, ALU.mult, ALU.add, lt[h], T_CS)
            bt.append(t1)
        vt = []
        for n, (s, b, t) in enumerate(proj_tok("even_w_in", 8, 8, blocks(rhs), 2, 512, ht)):
            t = A(Vt[:, n, :], b[:, 0:512], ACT.Copy, t)
            ps.give(s, t)
            vt.append(t)
        qd, kd, kl, e1t = [], [], [], []
        for h in range(4):
            t1 = A(E1[:, h, :], Bc[:, h, :], ACT.Exp, bt[h])
            t2 = A(E2[:, h, :], Bc[:, h, :], ACT.Exp, bt[h], scale=-1.0)
            for n in range(4):
                c = slice(64 * n, 64 * n + 64)
                t3 = A(E3[:, h, c], Bc[:, h, c], ACT.Exp, bt[h], scale=-1.0,
                       bias=Bc[:, h, 64 * n + 63:64 * n + 64])
            e1t.append(t1)
            qd.append(TT(Qb[:, h, :], Qb[:, h, :], E1[:, h, :], ALU.mult, t1, qt[h]))
            kd.append(TT(E2[:, h, :], E2[:, h, :], KH[:, h, :], ALU.mult, t2, kt_[h]))
            kl.append(TT(E3[:, h, :], E3[:, h, :], KH[:, h, :], ALU.mult, t3, kt_[h]))
        xft, yg = [None] * 4, [None] * 4
        YG = KH

        def xproj(j):
            s, b, t = proj("even_w_in", 8, 16 + j, rhs, 256, ht)
            xft[j] = conv_causal(b, t, s, XF[:, j, :], 4, lambda k: P("rcw", 4 * k + j), P("rcb", j))
            yield

        def yproj(j):
            s, b, t = proj("even_w_in", 8, 20 + j, rhs, 256, ht)
            yg[j] = A(YG[:, j, :], b[:, 0:256], ACT.Copy, t, kl, kd)
            ps.give(s, yg[j])
            yield

        yt = [None] * 8
        ssr = Slots([0, 1])

        def head(h):
            sct, ktt = [], []
            for p in range(2):
                s, b, fr = ps.take()
                for u in range(2):
                    c = slice(128 * p + 64 * u, 128 * p + 64 * u + 64)
                    r = slice(64 * u, 64 * u + 64)
                    t = MM([(b[r, r], E2[:, h, c], Qb[:, h, c])], fr, kd[h], qd[h])
                    t = A(SC[r, h, p, r], b[r, r], ACT.Copy, t, zt)
                ps.give(s, t)
                sc = SC[:, h, p, :]
                sct.append(pool.do(lambda e, sc=sc: e.affine_select(
                    out=sc, in_=sc, compare_op=ALU.is_ge, fill=0.0, base=0, pattern=[[1, 128]],
                    channel_multiplier=-1), t))
                s, b, fr = ps.take()
                t = TR([(b[:, 0:128], E3[:, h, 128 * p:128 * p + 128])], 128, fr, kl[h], T_CS)
                t = CP(KT[:, h, p, :], b[:, 0:128], t)
                ps.give(s, t)
                ktt.append(t)
            yield
            prev, stt = None, []
            sr, u_, sfr = ssr.take()
            for n in range(3):
                p, r = n // 2, slice(64 * (n % 2), 64 * (n % 2) + 64)
                s, b, fr = ps.take()
                t = MM([(b[:, 0:128], KT[r, h, p, :], Vt[r, p, 128 * h:128 * h + 128])], fr, ktt, vt)
                o = SS[:, u_, 128 * n:128 * n + 128]
                if n == 0:
                    t = CP(o, b[:, 0:128], t, sfr)
                else:
                    t = STT(o, SS[:, u_, 128 * n - 128:128 * n], E1[:, h, 64 * n + 63:64 * n + 64], b[:, 0:128],
                            ALU.mult, ALU.add, t, prev, e1t[h])
                ps.give(s, t)
                prev = t
                stt.append(t)
            yield
            s, b, fr = ps.take()
            for p in range(2):
                g = [(b[:, 128 * p:128 * p + 128], Vt[:, p, 128 * h:128 * h + 128], SC[:, h, p, :])]
                for n in (2 * p, 2 * p + 1):
                    if n:
                        g.append((b[:, 64 * n:64 * n + 64], SS[:, u_, 128 * (n - 1):128 * n],
                                  Qb[:, h, 64 * n:64 * n + 64]))
                t = MM(g, fr, sct, vt, stt, qd[h])
            ssr.give(sr, t)
            q, o, f = OH.take()
            to = CP(o, b[:, 0:256], t, f)
            ps.give(s, to)
            yield
            s, b, t = square_sum(lambda j: o, 1, 256, [to])
            rs, r, t = rstd(b, s, 256, 128, t)
            t = STT(o, o, P("hgn", h), r, ALU.mult, ALU.mult, t)
            rbs.give(rs, t)
            t = TT(o, o, Gb[:, h, :], ALU.mult, t, gt[h])
            yt[h] = split((Y[0][:, h, :], Y[1][:, h, :]), o, t)
            OH.give(q, yt[h])

        pipeline([xproj(0), xproj(1), head(0), xproj(2), head(1), xproj(3), head(2), yproj(0), head(3), yproj(1),
                  yproj(2), yproj(3)])
        free = everything_read()
        Rr, Ii, Tt, Aa = E2, E3, Gb, Bc
        rit = []
        for j in range(4):
            pair = []
            for g, (dst, bn) in enumerate(((Rr, "rba"), (Ii, "rbx"))):
                s, b, fr = ps.take()
                t = MM([(b[:, 0:256], RGW[:, 4 * g + j, :], XF[:, j, :])], fr, xft[j], (s_rg, 16))
                t = A(dst[:, j, :], b[:, 0:256], ACT.Sigmoid, t, free, bias=P(bn, j))
                ps.give(s, t)
                pair.append(t)
            rit.append(pair)
        at_ = []
        for j in range(4):
            t1 = A(Tt[:, j, :], Rr[:, j, :], ACT.Tanh, rit[j], scale=c8[:, j:j + 1])
            t2 = A(Aa[:, j, :], Rr[:, j, :], ACT.Exp, rit[j], c8t, scale=nc8[:, j:j + 1])
            at_.append((t1, t2))
        rt = []
        for j in range(4):
            t = TS(Rr[:, j, :], Tt[:, j, :], 1.0, None, ALU.add, None, at_[j][0], at_[j][1])
            t = REC(Rr[:, j, :], Rr[:, j, :], t)
            rt.append(STT(Rr[:, j, :], Rr[:, j, :], 2.0, Tt[:, j, :], ALU.mult, ALU.mult, t))
        rt = [A(Rr[:, j, :], Rr[:, j, :], ACT.Sqrt, rt[j]) for j in range(4)]
        fill(2)
        for j in range(4):
            t1 = TT(Ii[:, j, :], Ii[:, j, :], XF[:, j, :], ALU.mult, rit[j])
            t = TT(Rr[:, j, :], Rr[:, j, :], Ii[:, j, :], ALU.mult, rt[j], t1)
            t = SCAN(Ii[:, j, :], Aa[:, j, :], Rr[:, j, :], 0.0, ALU.mult, ALU.add, t, at_[j][1])
            tg = A(YG[:, j, :], YG[:, j, :], ACT.Gelu_apprx_tanh, yg[j])
            t = TT(Ii[:, j, :], Ii[:, j, :], YG[:, j, :], ALU.mult, t, tg)
            yt[4 + j] = split((Y[0][:, 4 + j, :], Y[1][:, 4 + j, :]), Ii[:, j, :], t)
        out_and_norm("even_w_out", 8, 0, operand(Y), yt, MIX, 256, lambda j, s: P("ng", 8 + j),
                     everything_read(), 1)

    smc = [0]
    smfree = [None] * 16

    def soft_first(s, b, t, end, scale, PP):
        i = smc[0] % 16
        smc[0] += 1
        nm, su, rs = (SM[:, 64 + 4 * i + k:64 + 4 * i + k + 1] for k in range(3))
        q, p, f = PP.take()
        t = dve.do(lambda e: e.tensor_reduce(nm, b[:, 0:end], AXX, ALU.max, negate=True), t, smfree[i])
        if scale != 1.0:
            t = TS(nm, nm, scale, None, ALU.mult, None, t)
        t = A(p[:, 0:end], b[:, 0:end], ACT.Exp, t, f, bias=nm, scale=scale, accum=su)
        ps.give(s, t)
        t = REC(rs, su, t)
        t = TS(p[:, 0:end], p[:, 0:end], rs, None, ALU.mult, None, t)
        smfree[i] = t
        return q, p, t

    def soft_turn(q, p, t, end, PP, pf, dst, on_act):
        s, b2, fr = ps.take()
        blk = [slice(128 * k, 128 * k + 128) for k in range(end // 128)]
        t = TR([(b2[:, c], p[:, c]) for c in blk], 128, fr, t)
        PP.give(q, t)
        t = A(dst, b2[:, 0:end], ACT.Copy, t, pf) if on_act else CP(dst, b2[:, 0:end], t, pf)
        ps.give(s, t)
        return t

    def layer_fox():
        for q in (pe, act, dve, pool):
            q.wait(T_CS2)
        free = everything_read()
        Vt = view(0, 2, 1024)
        Cc, Nc, La, Lb = (view(2048 + 256 * i, 256) for i in range(4))
        QK = Slots([tuple(view(3072 + 768 * i + 256 * k, 256) for k in range(3)) for i in range(2)])
        PP = Slots([view(4608 + 256 * i, 256) for i in range(6)])
        PT = Slots([view(6144 + 384 * i, 384) for i in range(4)])
        YS = Slots([view(7680 + 256 * i, 256) for i in range(3)])
        MIX = view(8448, 8, 256)
        Y = rview(4096, 8, 256)
        rhs, ht = pre_norm(lambda j, s: P("ng", 32 + j), 256, free, fillers=1)
        s, b, t = proj("odd_w_in", 8, 24, rhs, 256, ht)
        t = A(Nc, b[:, 0:256], ACT.Identity, t, free, bias=P("fxb"))
        ps.give(s, t)
        ct = []

        def forget(t):
            t = yield from log_sigmoid(Cc, Nc, La, Lb, t)
            t = SCAN(La, C("ones"), Cc, 0.0, ALU.mult, ALU.add, t)
            t1 = CP(Cc, La, t)
            ct.append(TS(Nc, La, -1.0, None, ALU.mult, None, t, t1))

        background.append(forget(t))
        vt = []
        for c in range(2):
            for n, (s, b, t) in enumerate(proj_tok("odd_w_in", 8, 16 + 4 * c, blocks(rhs), 2, 512, ht)):
                t = A(Vt[:, n, 512 * c:512 * c + 512], b[:, 0:512], ACT.Copy, t, free)
                ps.give(s, t)
                vt.append(t)
        finish()
        yt = [None] * 8
        state = {}

        def qk(j):
            qq, (qe, qo, kk), f = QK.take()
            s, b, t = proj("odd_w_in", 8, j, rhs, 256, ht)
            t1 = TS(qe, b[:, 0:256], c_even, None, ALU.mult, None, t, f, free)
            t2 = TS(qo, b[:, 0:256], c_odd, None, ALU.mult, None, t)
            ps.give(s, t2)
            s, b, t = proj("odd_w_in", 8, 8 + j, rhs, 256, ht)
            t3 = A(kk, b[:, 0:256], ACT.Copy, t, f, free)
            ps.give(s, t3)
            state[j] = (qq, qe, qo, kk, [t1, t2, t3])

        def head(h):
            j, par = h // 2, h % 2
            if par == 0:
                qk(j)
            yield
            qq, qe, qo, kk, tq = state[j]
            Q = qo if par else qe
            sel = ident[:, h:h + 1]
            soft = []
            for qb in range(2):
                end = 128 * (qb + 1)
                s, b, fr = ps.take()
                t = MM([(b[:, 0:end], Q[:, 128 * qb:end], kk[:, 0:end]),
                        (b[:, 0:end], Cc[:, 128 * qb:end], sel.to_broadcast([128, end])),
                        (b[:, 0:end], sel.to_broadcast([128, 128]), Nc[:, 0:end]),
                        (b[:, 128 * qb:end], ident, C("trib"))], fr, tq, ct, T_CS)
                soft.append((soft_first(s, b, t, end, 1.0, PP), end))
            if par:
                QK.give(qq, t)
            yield
            qp, pt, pf = PT.take()
            ptt = [soft_turn(*x, end, PP, [pf, free], pt[:, end - 128:2 * end - 128], (h + i) % 2)
                   for i, (x, end) in enumerate(soft)]
            yield
            s, b, fr = ps.take()
            vc = slice(128 * j, 128 * j + 128)
            t = MM([(b[:, 0:256], Vt[:, 0, vc], pt[:, 0:256]),
                    (b[:, 128:256], Vt[:, 1, vc], pt[:, 256:384])], fr, ptt, vt)
            PT.give(qp, t)
            r = slice(64 * par, 64 * par + 64)
            if par == 0:
                q, y, f = YS.take()
                t = CP(y[r], b[r, 0:256], t, f, free)
                state[j, "y"] = (q, y, t)
                ps.give(s, t)
            else:
                q, y, t0 = state[j, "y"]
                t = CP(y[r], b[r, 0:256], t)
                ps.give(s, t)
                yt[j] = split((Y[0][:, j, :], Y[1][:, j, :]), y, [t0, t], free)
                YS.give(q, yt[j])

        pipeline(head(h) for h in range(16))
        out_and_norm("odd_w_out", 8, 0, operand(Y), yt, MIX, 256, lambda j, s: P("ng", 40 + j), free, 1)

    def two(ap):
        return ap.rearrange("p (s t) -> p s t", s=2)

    def conv3(b, tok, s, dst, N, taps, bias, *w):
        t = A(dst, b[:, 0:N], ACT.Identity, tok, *w, bias=bias, scale=taps(1))
        if N == 512:
            d, x = two(dst), two(b[:, 0:N])
            t = STT(d[:, :, 1:256], x[:, :, 0:255], taps(0), d[:, :, 1:256], ALU.mult, ALU.add, t)
            t = STT(d[:, :, 0:255], x[:, :, 1:256], taps(2), d[:, :, 0:255], ALU.mult, ALU.add, t)
        else:
            t = STT(dst[:, 1:256], b[:, 0:255], taps(0), dst[:, 1:256], ALU.mult, ALU.add, t)
            t = STT(dst[:, 0:255], b[:, 1:256], taps(2), dst[:, 0:255], ALU.mult, ALU.add, t)
        ps.give(s, t)
        return t

    def sine(dst, x, k, tok):
        big = 12582912.0
        t = TS(k, x, 1.0 / (2 * math.pi), big, ALU.mult, ALU.add, tok)
        t = TS(k, k, big, None, ALU.subtract, None, t)
        c1 = 6.28125
        t = STT(x, k, -c1, x, ALU.mult, ALU.add, t)
        t = STT(x, k, -(2 * math.pi - c1), x, ALU.mult, ALU.add, t)
        t = TS(x, x, 3.1415925, -3.1415925, ALU.min, ALU.max, t)
        return A(dst, x, ACT.Sin, t)

    hd = []
    HE = view(4096, 256)

    def hyena_head(free):
        FW, ZT = view(4352, 128), view(4480, 256)
        HD, HK = view(4736, 256), view(4992, 256)
        R = slice(0, 64)
        load(FW[R, :], fw[:, 0:128], s_fw, free)
        load(ZT[R, :], fw[:, 2176:2432], s_fw, free)
        fww = fw[:, 128:2176].rearrange("p (a b) -> p a b", a=2)
        for c in range(2):
            load(view(5248 + 1024 * c, 2, 512)[R], fww[:, :, 512 * c:512 * c + 512], s_fw2, free)
            load(view(7296 + 1024 * c, 2, 512), dec[:, :, 512 * c:512 * c + 512], s_dec, free)
        for _ in range(8):
            yield
        s, b, fr = ps.take()
        t = MM([(b[R, 0:256], FW[R, 0:64], ZT[R])], fr, (s_fw, 32))
        t = TS(HD[R], b[R, 0:256], P("fb1")[R], P("ffr")[R], ALU.add, ALU.mult, t, free)
        ps.give(s, t)
        t = sine(HE[R], HD[R], HK[R], t)
        for _ in range(8):
            yield
        s, b, fr = ps.take()
        t = MM([(b[R, 0:256], FW[R, 64:128], HE[R])], fr, t)
        t = TS(HD[R], b[R, 0:256], P("fb2")[R], P("ffr")[R], ALU.add, ALU.mult, t)
        ps.give(s, t)
        hd.append(sine(HE[R], HD[R], HK[R], t))

    HF = view(0, 4, 1024)
    hft = []

    def filter_half(c, free):
        W3, DC = view(5248 + 1024 * c, 2, 512), view(7296 + 1024 * c, 2, 512)
        HP, HM = view(9344 + 2048 * c, 2, 512), view(10368 + 2048 * c, 2, 512)
        R = slice(0, 64)
        cc = slice(512 * c, 512 * c + 512)
        hpm, acc = [], None
        for n in range(2):
            q0, a0, f0 = tmp.take()
            q1, a1, f1 = tmp.take()
            s, b, fr = ps.take()
            t = MM([(b[:, :], HE[R, 128 * n:128 * n + 128], W3[R, 0, :])], fr, hd, (s_fw2, 32))
            t0 = TT(a0, b[:, :], DC[:, n, :], ALU.mult, t, f0, (s_dec, 32))
            ps.give(s, t0)
            s, b, fr = ps.take()
            t = MM([(b[:, :], HE[R, 128 * n:128 * n + 128], W3[R, 1, :])], fr)
            if n == 0:
                t1 = STT(a1, b[:, :], c_m0, DC[:, n, :], ALU.mult, ALU.mult, t, f1)
            else:
                t1 = TT(a1, b[:, :], DC[:, n, :], ALU.mult, t, f1)
            ps.give(s, t1)
            tp = TT(HP[:, n, :], a0, a1, ALU.add, t0, t1, free)
            tm_ = TT(HM[:, n, :], a0, a1, ALU.subtract, t0, t1)
            hpm += [tp, tm_]
            for q, a in ((q0, a0), (q1, a1)):
                t = A(a, a, ACT.Abs, tp, tm_)
                if acc is None:
                    acc = (q, a, t)
                else:
                    acc = (acc[0], acc[1], TT(acc[1], acc[1], a, ALU.add, t, acc[2], q=pool))
                    tmp.give(q, acc[2])
            yield
        s, b, fr = ps.take()
        t = MM([(b[:, :], ones, acc[1])], fr, acc[2])
        tmp.give(acc[0], t)
        q, NI, f = tmp.take()
        nt = REC(NI, b[:, :], t, f)
        ps.give(s, nt)
        yield
        yield
        for f in range(4):
            src = HP if f < 2 else HM
            s, b, fr = ps.take()
            t = MM([(b[:, :], C("dft")[:, 512 * n + 128 * f:512 * n + 128 * f + 128], src[:, n, :])
                    for n in range(2)], fr, hpm)
            hft.append(TT(HF[:, f, cc], b[:, :], NI, ALU.mult, t, nt, free))
            ps.give(s, hft[-1])
            yield
        tmp.give(q, hft[-1])

    def whole_filter(free):
        a, b = filter_half(0, free), filter_half(1, free)
        for i, x in enumerate((a, a, b, a, b, a, b, a, b, a, b, a, b, a, b, a, b, a, b)):
            next(x, None)
            if i in (2, 5):
                fill()
            yield

    def layer_even2():
        fill_all(0)
        free = everything_read()
        assert hd
        rhs, ht = pre_norm(lambda j, s: MC[:, 2 * j + s:2 * j + s + 1], 512, free, shift=lambda j, s: mod(0, j, s),
                           behind=whole_filter(free))
        G = view(4096, 8, 512)
        free = everything_read()
        gt = [None] * 8

        def gunit(j):
            q0, a0, f0 = tmp.take()
            s, b, t = proj("e_w_in", 8, 8 + j, rhs, 512, ht)
            t0 = conv3(b, t, s, a0, 512, lambda k: P("ecw", 24 * k + 8 + j), P("ecb", 8 + j), f0)
            s, b, t = proj("e_w_in", 8, 16 + j, rhs, 512, ht)
            t1 = conv3(b, t, s, G[:, j, :], 512, lambda k: P("ecw", 24 * k + 16 + j), P("ecb", 16 + j), free)
            gt[j] = TT(G[:, j, :], G[:, j, :], a0, ALU.mult, t0, t1)
            tmp.give(q0, gt[j])
            yield

        pipeline(gunit(j) for j in range(8))
        GT = Slots([view(8192 + 1024 * i, 2, 512) for i in range(2)])
        SPC = Slots([view(10240 + 512 * i, 512) for i in range(6)])

        def cunit(seq, c):
            qg, g_, gf = GT.take()
            trs = []
            for tb in range(2):
                s, b, fr = ps.take()
                c0 = 256 * seq + 128 * tb
                t = TR([(b[:, 128 * jj:128 * jj + 128], G[:, 4 * c + jj, c0:c0 + 128]) for jj in range(4)], 128, fr,
                       gt[4 * c:4 * c + 4])
                t = A(g_[:, tb, :], b[:, :], ACT.Copy, t, gf, free)
                ps.give(s, t)
                trs.append(t)
            yield
            spec = []
            for fb in range(2):
                U = []
                for part in range(2):
                    f = 2 * part + fb
                    s, b, fr = ps.take()
                    t = MM([(b[:, :], C("dft")[:, 512 * n + 128 * f:512 * n + 128 * f + 128], g_[:, n, :])
                            for n in range(2)], fr, trs)
                    U.append((s, b, t))
                cc = slice(512 * c, 512 * c + 512)
                (sr, ur, tr_), (si, ui, ti_) = U
                hr, hi = HF[:, fb, cc], HF[:, 2 + fb, cc]
                qa, a_, fa = SPC.take()
                ring = tmp if fb else SPC
                qc_, c_, fc_ = ring.take()
                qb_, b_, fb_ = tmp.take()
                t0 = TT(a_, ur, hr, ALU.mult, tr_, fa, hft, free)
                t1 = TT(b_, ui, hi, ALU.mult, ti_, fb_)
                t2 = TT(a_, a_, b_, ALU.subtract, t0, t1)
                t3 = TT(c_, ur, hi, ALU.mult, tr_, fc_, free)
                ps.give(sr, t3)
                t4 = TT(b_, ui, hr, ALU.mult, ti_, t2)
                ps.give(si, t4)
                t5 = TT(c_, c_, b_, ALU.add, t3, t4)
                tmp.give(qb_, t5)
                spec.append((qa, a_, t2, qc_, c_, t5, ring))
            GT.give(qg, U[1][2])
            yield
            for jj in range(4):
                j = 4 * c + jj
                s, b, fr = ps.take()
                rows = [(spec[0][1], 0), (spec[1][1], 1), (spec[0][4], 2), (spec[1][4], 3)]
                t = MM([(b[:, 0:256], a[:, 128 * jj:128 * jj + 128], C("idft")[:, 256 * f:256 * f + 256])
                        for a, f in rows], fr, [x[2] for x in spec], [x[5] for x in spec])
                sc_ = slice(256 * seq, 256 * seq + 256)
                t1 = STT(G[:, j, sc_], G[:, j, sc_], P("hyb", j), b[:, 0:256], ALU.mult, ALU.add, t)
                ps.give(s, t1)
                ct_.append(t1)
            for x in spec:
                SPC.give(x[0], t)
                x[6].give(x[3], t)

        ct_ = []
        pipeline(cunit(seq, c) for c in range(2) for seq in range(2))
        free = everything_read()
        Q = view(0, 8, 512)
        KR = view(8192, 2, 512)
        VT = view(9216, 4, 256)
        PTb = Slots([view(10240 + 512 * i, 512) for i in range(6)])
        kt, qt, vt = [None] * 2, [None] * 8, []

        def qk_norm(dst, m, gain, toks, i):
            s, b, t = proj("e_w_in", 8, m, rhs, 512, ht)
            t0 = A(dst, b[:, :], ACT.Copy, t, free)
            ps.give(s, t0)
            q, x, f = tmp.take()
            t = A(x, dst, ACT.Square, t0, f)
            yield
            s, b, fr = ps.take()
            t = MM([(b[:, :], ones, x)], fr, t, T_CS)
            tmp.give(q, t)
            rs, r, t = rstd(b, s, 512, 128, t)
            t = STT(dst, dst, gain, r, ALU.mult, ALU.mult, t)
            rbs.give(rs, t)
            yield
            s, b, fr = ps.take()
            t1 = MM([(b[:, 0:256], C("perm"), dst[:, 0:256])], fr, t)
            q, tb, tf = tmp.take()
            t2 = TT(tb[:, 0:256], b[:, 0:256], C("sin"), ALU.mult, t1, tf)
            ps.give(s, t2)
            t3 = TT(dst[:, 0:256], dst[:, 0:256], C("cos"), ALU.mult, t, t1)
            t4 = TT(dst[:, 0:256], dst[:, 0:256], tb[:, 0:256], ALU.add, t2, t3)
            tmp.give(q, t4)
            toks[i] = t4

        def vproj():
            for n, (s, b, t) in enumerate(proj_tok("e_w_in", 8, 42, blocks(rhs), 4, 256, ht)):
                t = A(VT[:, n, :], b[:, 0:256], ACT.Copy, t, free)
                ps.give(s, t)
                vt.append(t)
            yield

        scale = 128 ** -0.5

        def att(h, seq):
            Qh, Kh = Q[:, h, :], KR[:, h // 4, :]
            vc = slice(128 * (h // 4), 128 * (h // 4) + 128)
            nk, k0 = (4, 0) if seq == 0 else (2, 2)
            soft = []
            for qb in range(2):
                qc = slice(256 * seq + 128 * qb, 256 * seq + 128 * qb + 128)
                s, b, fr = ps.take()
                t = MM([(b[:, 0:128 * nk], Qh[:, qc], Kh[:, 128 * k0:512])], fr, kt, qt[h])
                soft.append((soft_first(s, b, t, 128 * nk, scale, tmp), t))
            next(slow, None)
            yield
            turned = []
            for i, (x, _) in enumerate(soft):
                qp, pt, pf = PTb.take()
                turned.append((qp, pt, soft_turn(*x, 128 * nk, tmp, [pf, free], pt[:, 0:128 * nk], i)))
            yield
            s, b, fr = ps.take()
            for qb, (qp, pt, tt) in enumerate(turned):
                t = MM([(b[:, 128 * qb:128 * qb + 128], VT[:, k0 + k, vc], pt[:, 128 * k:128 * k + 128])
                        for k in range(nk)], fr, tt, vt)
                PTb.give(qp, t)
            t1 = CP(Qh[:, 256 * seq:256 * seq + 256], b[:, 0:256], t)
            ps.give(s, t1)
            ot[h].append(t1)

        ot = [[] for _ in range(8)]
        Y = rview(8192, 8, 512)
        yt = [None] * 8

        def gated(src, m, j, toks):
            s, b, t = proj("e_w_in", 8, m, rhs, 512, ht)
            q, x, f = tmp.take()
            t1 = A(x, b[:, :], ACT.Tanh, t, f, scale=0.5)
            t = STT(x, x, 1.0, b[:, :], ALU.add, ALU.mult, t1, t)
            ps.give(s, t)
            t = STT(src, x, 0.5, src, ALU.mult, ALU.mult, t, toks)
            tmp.give(q, t)
            return split((Y[0][:, j, :], Y[1][:, j, :]), src, t, free)

        def agate(h):
            yt[h] = gated(Q[:, h, :], 44 + h, h, ot[h])
            yield

        units = [qk_norm(KR[:, 0, :], 40, P("kn"), kt, 0), qk_norm(KR[:, 1, :], 41, P("kn"), kt, 1), vproj()]
        units += [qk_norm(Q[:, h, :], 32 + h, P("qn"), qt, h) for h in range(2)]
        pipeline(units)
        slow = trickle()
        units = []
        for h in range(8):
            units.append(att(h, 0))
            if h < 6:
                units.append(qk_norm(Q[:, h + 2, :], 34 + h, P("qn"), qt, h + 2))
            units.append(att(h, 1))
            if h > 1:
                units.append(agate(h - 2))
        pipeline(units)
        for _ in slow:
            pass
        pipeline([agate(6), agate(7)])
        MIX = Q
        free2 = everything_read()
        y2t = [None] * 8

        def hy():
            for j in range(8):
                q, x, f = tmp.take()
                s, b, t = proj("e_w_in", 8, j, rhs, 512, ht)
                t = conv3(b, t, s, x, 512, lambda k: P("ecw", 24 * k + j), P("ecb", j), f)
                t = TT(G[:, j, :], G[:, j, :], x, ALU.mult, t, ct_)
                tmp.give(q, t)
                y2t[j] = gated(G[:, j, :], 24 + j, j, t)

        half = []
        for m in range(8):
            s, b, t = proj("e_w_out", 8, m, operand(Y), 512, yt, 8)
            half.append(A(MIX[:, m, :], b[:, :], ACT.Copy, t, free2))
            ps.give(s, half[-1])
        free = everything_read()
        hy()
        out_and_norm("e_w_out", 8, 0, operand(Y), y2t, MIX, 512, lambda j, s: MC[:, 16 + 2 * j + s:16 + 2 * j + s + 1],
                     None, 0, half)

    def layer_odd2():
        fill_all(1)
        free = everything_read()
        VT = [view(2048 * i, 4, 512) for i in range(2)]
        NM, EM = view(4096, 2, 256), view(4608, 2, 256)
        LI, LF, LB, LM = (view(5120 + 1024 * i, 2, 512) for i in range(4))
        AN = view(9216, 2, 512)
        GI, GF = view(10240, 512), view(10752, 512)
        a1, a2 = view(11264, 512), view(11776, 512)
        AC = SM[:, 256:320]
        rhs, ht = pre_norm(lambda j, s: MC[:, 32 + 2 * j + s:32 + 2 * j + s + 1], 512, free,
                           shift=lambda j, s: mod(1, j, s))
        rhs1 = lambda k: tuple(v[:, 0:256] for v in rhs(k))
        s, b, t = proj("o_w_in", 8, 64, rhs, 512, ht)
        tg = A(GI, b[:, :], ACT.Identity, t, free, bias=P("gtb"))
        ps.give(s, tg)
        vtt = {}

        def vproj(p, w):
            vtt[p] = []
            for n, (s, b, t) in enumerate(proj_tok("o_w_in", 8, 16 + 4 * p, blocks(rhs), 4, 512, ht)):
                t = A(VT[p % 2][:, n, :], b[:, :], ACT.Copy, t, free, w)
                ps.give(s, t)
                vtt[p].append(t)

        R8 = slice(0, 8)
        rows = []

        def gates():
            t = yield from log_sigmoid(GF, GI, a1, a2, [tg, free])
            one8 = C("ones", 8)
            lat, cx = slice(0, 256), slice(256, 512)
            for d in range(2):
                for dst, src, row in ((LI, GI, 64 * d), (LF, GF, 64 * d + 32)):
                    for o, c in ((0, cx), (256, lat)):
                        sv = src[row:row + 8, c]
                        if d:
                            sv = sv[:, ::-1]
                        t1 = CP(dst[R8, d, o:o + 256], sv, t, tg, free)
                yield
            for d in range(2):
                t = SCAN(LB[R8, d, 0:256], one8, LF[R8, d, 0:256], 0.0, ALU.mult, ALU.add, t1)
                t = SCAN(LB[R8, d, 256:512], one8, LF[R8, d, 256:512], LB[R8, d, 255:256], ALU.mult, ALU.add, t)
                yield
                t = TT(LI[R8, d, :], LI[R8, d, :], LB[R8, d, :], ALU.subtract, t)
                t = SCAN(LM[R8, d, :], LI[R8, d, :], LI[R8, d, :], 0.0, ALU.max, ALU.max, t)
                yield
                t = TT(LB[R8, d, :], LB[R8, d, :], LM[R8, d, :], ALU.add, t)
                v = (lambda x: x[:, ::-1]) if d else (lambda x: x)
                t2 = CP(AN[R8, d, 0:256], v(LI[R8, d, 256:512]), t, free)
                t3 = CP(AN[R8, d, 256:512], v(LI[R8, d, 0:256]), t)
                t4 = TS(NM[R8, d, :], v(LM[R8, d, 256:512]), -1.0, None, ALU.mult, None, t, free)
                t5 = TS(EM[R8, d, :], v(LB[R8, d, 256:512]), -1.0, None, ALU.mult, None, t, free)
                rows.extend([t4, A(EM[R8, d, :], EM[R8, d, :], ACT.Exp, t5)])
                yield
            s, b, fr = ps.take()
            t = TR([(b[:, 8 * (4 * d + k):8 * (4 * d + k) + 8], AN[R8, d, 128 * k:128 * k + 128])
                    for d in range(2) for k in range(4)], 8, fr, t3)
            rows.append(CP(AC, b[:, 0:64], t))
            ps.give(s, rows[-1])

        background.append(gates())
        vproj(0, None)
        vproj(1, None)
        finish()
        rows_t = rows + [(s_dve, dve.n)]
        QK = Slots([(view(5120 + 768 * i, 256), view(5376 + 768 * i, 512)) for i in range(2)])
        ST = Slots([view(6656 + 1024 * i, 4, 256) for i in range(2)])
        WW = Slots([view(8704 + 1024 * i, 4, 256) for i in range(2)])
        EMS = Slots([view(10752 + 512 * i, 512) for i in range(2)])
        HS = Slots([view(11776 + 512 * i, 2, 256) for i in range(3)])
        Y = rview(8192, 16, 256)
        yt = [None] * 16
        vread = {}

        def head(h):
            qq, (qh, kh), f = QK.take()
            s, b, t = proj("o_w_in", 8, h, rhs1, 256, ht)
            t = conv3(b, t, s, qh, 256, lambda k: P("ocw", 16 * k + h), P("ocb", h), rows_t, f)
            q1, x1, f1 = tmp.take()
            t1 = A(x1[:, 0:256], qh, ACT.Tanh, t, f1, scale=0.5)
            tq = STT(qh, x1[:, 0:256], 1.0, qh, ALU.add, ALU.mult, t1)
            tmp.give(q1, tq)
            s, b, t = proj("o_w_in", 8, 8 + h, rhs, 512, ht)
            t = conv3(b, t, s, kh, 512, lambda k: P("ocw", 16 * k + 8 + h), P("ocb", 8 + h), rows_t, f)
            q1, x1, f1 = tmp.take()
            t1 = A(x1, kh, ACT.Tanh, t, f1, scale=0.5)
            tk = STT(kh, x1, 1.0, kh, ALU.add, ALU.mult, t1)
            tmp.give(q1, tk)
            yield
            qs, st, sf = ST.take()
            stt = []
            for p in range(2):
                s, b, fr = ps.take()
                for i in range(2):
                    k = 2 * p + i
                    t = MM([(b[:, 256 * i:256 * i + 256], kh[:, 128 * k:128 * k + 128], qh)], fr, tq, tk)
                t1 = A(st[:, 2 * p:2 * p + 2, :], two(b[:, :]), ACT.Copy, t, sf, rows_t, scale=0.25 * 128 ** -0.5)
                ps.give(s, t1)
                stt.append(t1)
            QK.give(qq, t)
            sel = ident[R8, h:h + 1].to_broadcast([8, 128])
            hsq, hs, hf = HS.take()
            ha = None
            for d in range(2):
                s, b, fr = ps.take()
                t = MM([(b[:, 0:256], sel, NM[R8, d, :])], fr, rows_t)
                t = MM([(b[:, 256:512], sel, EM[R8, d, :])])
                qe, ems, ef = EMS.take()
                te = A(ems, b[:, :], ACT.Copy, t, ef, rows_t)
                ps.give(s, te)
                nm, em = ems[:, 0:256], ems[:, 256:512]
                qw, W, wf = WW.take()
                col = [AC[:, 8 * (4 * d + k) + h:8 * (4 * d + k) + h + 1] for k in range(4)]
                tri = C("trib" if d else "trif")
                rng = []
                wt = []
                for k in range(2):
                    dg = slice(128 * k, 128 * k + 128)
                    t1 = STT(W[:, k, dg], nm[:, dg], col[k], tri, ALU.add, ALU.add, te, wf, rows_t)
                    full = (d == 0 and k == 0) or (d == 1 and k == 1)
                    if full:
                        oc = slice(128, 256) if k == 0 else slice(0, 128)
                        wt.append(A(W[:, k, oc], nm[:, oc], ACT.Exp, te, wf, rows_t, bias=col[k]))
                    wt.append(A(W[:, k, dg], W[:, k, dg], ACT.Exp, t1))
                    rng.append(slice(0, 256) if full else dg)
                for k in (2, 3):
                    wt.append(A(W[:, k, :], nm, ACT.Exp, te, wf, rows_t, bias=col[k]))
                t1 = [TT(W[:, k, rng[k]], W[:, k, rng[k]], st[:, k, rng[k]], ALU.mult, wt, stt) for k in range(2)]
                t2 = TT(W[:, 2:4, :], W[:, 2:4, :], st[:, 2:4, :], ALU.mult, wt, stt, q=pool)
                if d == 1:
                    ST.give(qs, t1, t2)
                f_, o_ = (0, 1) if d == 0 else (1, 0)
                al = nm
                ta = TT(al, W[:, 2, :], W[:, 3, :], ALU.add, t2, wt, q=pool)
                ta = TT(al, al, W[:, f_, :], ALU.add, ta, t1, q=pool)
                ta = TT(al[:, rng[o_]], al[:, rng[o_]], W[:, o_, rng[o_]], ALU.add, ta, q=pool)
                yield
                seq = [(2, slice(0, 256)), (3, slice(0, 256)), (0, rng[0]), (1, rng[1])]
                sd, bd, frd = ps.take()
                td = MM([(bd[:, 0:256], ones, al)], frd, ta)
                sn, bn, frn = ps.take()
                V = VT[(h // 2) % 2]
                for vb in range(2):
                    vc = 256 * (h % 2) + 128 * vb
                    tn = MM([(bn[:, 256 * vb + c.start:256 * vb + c.stop], V[:, k, vc:vc + 128], W[:, k, c])
                             for k, c in seq], frn, t1, t2, vtt[h // 2])
                WW.give(qw, tn)
                qd_, den, df = tmp.take()
                den = den[:, 0:256]
                t = A(den, bd[:, 0:256], ACT.Abs, td, df, rows_t)
                ps.give(sd, t)
                t = TT(den, den, em, ALU.max, t, te)
                EMS.give(qe, t, td)
                t = REC(den, den, t)
                if d == 0:
                    for vb in range(2):
                        ha = TT(hs[:, vb, :], bn[:, 256 * vb:256 * vb + 256], den, ALU.mult, t, tn, hf, rows_t)
                else:
                    q, x_, f = tmp.take()
                    for vb in range(2):
                        t1 = TT(x_[:, 256 * vb:256 * vb + 256], bn[:, 256 * vb:256 * vb + 256], den, ALU.mult, t, tn, f)
                    ha = TT(hs[:, :, :], hs[:, :, :], two(x_), ALU.add, t1, ha)
                    tmp.give(q, ha)
                ps.give(sn, ha)
                tmp.give(qd_, ha)
                if d == 1:
                    vread[h] = tn
            yield
            if h % 2 and h // 2 < 2:
                vproj(h // 2 + 2, [vread[h - 1], vread[h]])
            for vb in range(2):
                s, b, t = proj("o_w_in", 8, 32 + 2 * h + vb, rhs1, 256, ht)
                q, x_, f = tmp.take()
                t = A(x_[:, 0:256], b[:, 0:256], ACT.Tanh, t, f, scale=0.5)
                ps.give(s, t)
                ho = STT(hs[:, vb, :], x_[:, 0:256], 1.0, hs[:, vb, :], ALU.add, ALU.mult, t, ha)
                tmp.give(q, ho)
            yield
            z = []
            for vb in range(2):
                s, b, t = proj("o_w_in", 8, 48 + 2 * h + vb, rhs1, 256, ht)
                q, x_, f = tmp.take()
                t = A(x_[:, 0:256], b[:, 0:256], ACT.Tanh, t, f, scale=0.5)
                t = STT(x_[:, 0:256], x_[:, 0:256], 1.0, b[:, 0:256], ALU.add, ALU.mult, t)
                ps.give(s, t)
                z.append((q, x_, t))
            s, b, t = square_sum(lambda j: hs[:, j, :], 2, 256, [ho, ho], scale=0.5)
            rs, r, t = rstd(b, s, 256, 256, t)
            for vb in range(2):
                j = 2 * h + vb
                q, x_, tz = z[vb]
                t1 = STT(hs[:, vb, :], hs[:, vb, :], P("ohn", j), r, ALU.mult, ALU.mult, t)
                t1 = STT(hs[:, vb, :], hs[:, vb, :], 0.25, x_[:, 0:256], ALU.mult, ALU.mult, t1, tz)
                tmp.give(q, t1)
                yt[j] = split((Y[0][:, j, :], Y[1][:, j, :]), hs[:, vb, :], t1, free)
            rbs.give(rs, t1)
            HS.give(hsq, yt[2 * h], yt[2 * h + 1])

        heads = [head(h) for h in range(8)]
        for r in range(11):
            for h in (r - 3, r - 3, r - 2, r - 3, r - 1, r):
                if 0 <= h < 8:
                    next(heads[h], None)
        MIX = view(0, 8, 256)
        out_and_norm("o_w_out", 16, 0, operand(Y), yt, MIX, 256, lambda j, s: MC[:, 48 + 2 * j:48 + 2 * j + 1],
                     everything_read())

    def whole():
        layer_even()
        ffn(0, 1)
        layer_fox()
        ffn(1, 1)
        layer_even2()
        layer_odd2()
        load(out, X[:, :, 0:256], s_out, xt)

    whole()
    assert len(plan) == NTILES
    ld = Queue(None)
    for c in range((len(plan) + TPC - 1) // TPC):
        while extra and extra[0][0] <= c:
            _, dst, src, sm, toks = extra.pop(0)
            ld.dma(lambda e, dst=dst, src=src: e.dma_start(dst, src), sm, *toks)
        ld.dma(lambda e, c=c: e.dma_start(RAWB[:, c % RAW, :], ws[c]), s_w[c % RAW], raw_free.get(c - RAW))
    for _, dst, src, sm, toks in extra:
        ld.dma(lambda e, dst=dst, src=src: e.dma_start(dst, src), sm, *toks)
    ld.wait((s_out, 16))
    return pe, act, dve, pool, ld, plan, mine


NTILES = 3152


def build_program(nc, xT, ctxT, ws, pr, cs, rgw, fw, dec, out):
    _, PN = param_layout()
    _, CN = const_layout()
    ctx = ExitStack()
    with ctx:
        def sb(name, *shape, dt=F32):
            return ctx.enter_context(nc.sbuf_tensor(name, [128, *shape], dt))

        def sem(name):
            return ctx.enter_context(nc.semaphore(name))

        bufs = (sb("X", 8, 512), sb("RH", 16384, dt=F32R), sb("RAWB", RAW, TPC * 128),
                sb("WH", SPL, TPC * 128, dt=F32R), sb("WL", SPL, TPC * 128, dt=F32R), sb("PR", PN), sb("CS", CN),
                [sb(f"TMP{i}", 512) for i in range(6)], [sb(f"RB{i}", 512) for i in range(2)], sb("SM", 320),
                sb("MODB", 272), sb("AR", NA), [ctx.enter_context(nc.psum_tensor(f"PS{i}", [128, 512], F32))
                                                for i in range(8)])
        sems = (sem("s_pe"), sem("s_act"), sem("s_dve"), sem("s_pool"), [sem(f"s_w{i}") for i in range(RAW)],
                *(sem(n) for n in ("s_cs", "s_cs2", "s_pr", "s_x", "s_xc", "s_rg", "s_fw", "s_fw2", "s_dec", "s_out")))
        dram = (xT, ctxT, ws, pr, cs, rgw, fw, dec, out)
        kinds = record(bufs, sems, dram, [])[6]
        pe, act, dve, pool, ld, plan, again = record(bufs, sems, dram, kinds)
        assert kinds == again
        block = ctx.enter_context(nc.Block())

        @block.sync
        def _(eng):
            ld.emit(eng)

        @block.tensor
        def _(eng):
            pe.emit(eng)

        @block.scalar
        def _(eng):
            act.emit(eng)

        @block.vector
        def _(eng):
            dve.emit(eng)

        @block.gpsimd
        def _(eng):
            pool.emit(eng)
    return plan


def constants():
    off, n = const_layout()
    c = np.zeros((128, n), np.float64)

    def put(name, a):
        o, w = off[name]
        c[:a.shape[0], o:o + a.shape[1]] = a

    p = np.arange(128)[:, None]
    put("ident", np.eye(128))
    put("ones", np.ones((128, 256)))
    perm = np.zeros((128, 128))
    for base in (0, 64):
        for i in range(32):
            perm[base + 32 + i, base + i] = -1
            perm[base + i, base + 32 + i] = 1
    put("perm", perm)
    inv = (np.float32(10000.0) ** (-np.arange(32, dtype=np.float32) / np.float32(32))).astype(np.float32)
    pos = [np.arange(256) // 64, np.arange(256) % 64]
    ang = np.stack([(pos[d // 64].astype(np.float32) * inv[d % 32]).astype(np.float32) for d in range(128)])
    put("cos", np.cos(ang.astype(np.float64)))
    put("sin", np.sin(ang.astype(np.float64)))
    put("trif", np.where(p <= np.arange(128)[None], 0, NEG))
    put("trib", np.where(p >= np.arange(128)[None], 0, NEG))
    cols = np.zeros((128, 8))
    cols[:, 0] = EPS
    cols[0:64, 1] = 0.125
    cols[64:, 2] = 0.125
    cols[1:, 3] = 1
    put("cols", cols)
    th = np.pi * (2 * np.arange(256) + 1) / 512
    t = np.arange(256)
    fwd = np.concatenate([np.cos(np.outer(t, th)), -np.sin(np.outer(t, th))], 1)
    put("dft", np.concatenate([fwd[:128], fwd[128:]], 1))
    bwd = np.concatenate([np.cos(np.outer(th, t)), -np.sin(np.outer(th, t))], 0) / 256
    put("idft", np.concatenate([bwd[128 * i:128 * i + 128] for i in range(4)], 1))
    n_ = 256
    tt = np.linspace(0.0, 1.0, n_, dtype=np.float32)[:, None]
    bands = np.linspace(1e-4, 15, 16, dtype=np.float32)
    a = (np.float32(2 * math.pi / n_) * np.arange(n_, dtype=np.float32)[:, None] * bands).astype(np.float32)
    z = np.concatenate([tt, np.cos(a), -np.sin(a)], 1)
    lo, hi = math.log(1e-2) / 1.5, math.log(1e-2) / 0.3
    deltas = np.linspace(lo, hi, 1024, dtype=np.float32)
    decay = np.exp((-tt * np.abs(deltas)).astype(np.float32).astype(np.float64))
    dec = decay.reshape(2, 128, 1024).transpose(1, 0, 2)
    zT = np.zeros((64, 256), np.float32)
    zT[0:33] = z.T
    return c.astype(np.float32), np.ascontiguousarray(dec.astype(np.float32)), zT


def columns(v):
    v = np.asarray(v)
    return v.reshape(-1, 128).T


def padded(v):
    o = np.zeros((128, 1), v.dtype)
    o[:v.size, 0] = v.reshape(-1)
    return o


def lay_out(i, plan):
    a = {k: np.asarray(v) for k, v in i.items()}
    fT = lambda x: np.ascontiguousarray(x.reshape(256, 8, 128).transpose(2, 1, 0))
    gb = a["o_gate_b_2"][0].reshape(4, 8)
    gtb = np.zeros((128, 1), gb.dtype)
    for g in range(4):
        gtb[32 * g:32 * g + 8, 0] = gb[g]
    parts = {
        "ng": columns(a["norm_gains"]), "lbl": columns(a["hgrn_lb_logits"]), "hgn": columns(a["hgrn_norm"]),
        "rcw": columns(a["rg_conv_w"]), "rcb": columns(a["rg_conv_b"]), "rba": columns(a["rg_ba"]),
        "rbx": columns(a["rg_bx"]), "lam": columns(a["rg_lambda"]), "fxb": padded(a["fox_f_bias"]),
        "fcw": columns(a["ffn_conv_w"]), "fcb": columns(a["ffn_conv_b"]),
        "cc": np.stack([columns(a["c_2"]), columns(a["c_ctx_2"])], 2).reshape(128, 16),
        "bmod": np.repeat(columns(a["b_mod_2"]), 2, axis=1),
        "gpre": np.repeat(columns(a["g_pre_2"]), 2, axis=1), "gpost": np.repeat(columns(a["g_post_2"]), 2, axis=1),
        "ecw": columns(a["e_conv_w_2"]), "ecb": columns(a["e_conv_b_2"]),
        "fb1": padded(a["e_filt_b1_2"]), "ffr": padded(a["e_filt_freq_2"]), "fb2": padded(a["e_filt_b2_2"]),
        "hyb": columns(a["e_hy_bias_2"]), "qn": columns(a["e_q_norm_2"]), "kn": columns(a["e_k_norm_2"]),
        "ocw": columns(a["o_conv_w_2"]), "ocb": columns(a["o_conv_b_2"]), "gtb": gtb,
        "ohn": columns(a["o_head_norm_2"]),
    }
    off, n = param_layout()
    pr = np.zeros((128, n), np.float32)
    for k, v in parts.items():
        pr[:, off[k]:off[k] + v.shape[1]] = v
    ow = a["o_w_in_2"][0]
    gates = np.zeros((1024, 128), ow.dtype)
    for g in range(4):
        gates[:, 32 * g:32 * g + 8] = ow[:, 8192 + 8 * g:8192 + 8 * g + 8]
    od = a["odd_w_in"][0]
    od = np.concatenate([od, np.zeros((1024, 3200 - od.shape[1]), od.dtype)], 1)
    mats = {
        "even_w_in": a["even_w_in"][0], "even_w_out": a["even_w_out"][0], "odd_w_in": od,
        "odd_w_out": a["odd_w_out"][0], "e_w_in": a["e_w_in_2"][0], "e_w_out": a["e_w_out_2"][0],
        "o_w_in": np.concatenate([ow[:, 0:8192], gates], 1), "o_w_out": a["o_w_out_2"][0],
    }
    for l in range(2):
        mats[f"ffn_up{l}"] = a["ffn_w_up"][l]
        mats[f"ffn_down{l}"] = a["ffn_w_down"][l]
        mats[f"w_mod{l}"] = a["w_mod_2"][l]
    nchunk = (len(plan) + TPC - 1) // TPC
    ws = np.zeros((nchunk, 128, TPC, 128), np.float32)
    for t, (name, k, m) in enumerate(plan):
        ws[t // TPC, :, t % TPC, :] = mats[name][128 * k:128 * k + 128, 128 * m:128 * m + 128]
    ws = ws.reshape(nchunk, 128, TPC * 128)
    rgw = np.zeros((128, 8, 128), np.float32)
    for g, name in enumerate(("rg_wa", "rg_wx")):
        for b in range(8):
            o = 64 * (b % 2)
            rgw[o:o + 64, 4 * g + b // 2, o:o + 64] = a[name][0, b]
    fw = np.zeros((64, 2432), np.float32)
    fw[0:33, 0:64] = a["e_filt_w1_2"][0]
    fw[:, 64:128] = a["e_filt_w2_2"][0]
    fw[:, 128:2176] = a["e_filt_w3_2"][0]
    cs, dec, fw[:, 2176:] = constants()
    return {"xT": fT(a["x"]), "ctxT": fT(a["ctx_2"]), "ws": ws, "pr": pr, "cs": cs, "rgw": rgw, "fw": fw, "dec": dec}


SHAPES = {"xT": (128, 8, 256), "ctxT": (128, 8, 256), "ws": (NTILES // TPC, 128, TPC * 128),
          "pr": (128, param_layout()[1]), "cs": (128, const_layout()[1]), "rgw": (128, 8, 128), "fw": (64, 2432),
          "dec": (128, 2, 1024)}


def kernel(**inputs):
    import concourse.bacc as _bacc
    from concourse.bass_utils import run_bass_kernel_spmd as _run

    nc = _bacc.Bacc("TRN2", target_bir_lowering=False, num_devices=1)
    args = [nc.dram_tensor(k, v, F32, kind="ExternalInput").ap() for k, v in SHAPES.items()]
    out = nc.dram_tensor("outT", (128, 8, 256), F32, kind="ExternalOutput").ap()
    plan = build_program(nc, *args, out)
    r = _run(nc, [lay_out(inputs, plan)], core_ids=[0])
    return np.ascontiguousarray(r.results[0]["outT"].transpose(2, 1, 0).reshape(1, 256, 1024))
```
